# Optimizing a Trainium2 kernel written in Bass

```python
import math
import jax, jax.numpy as jnp
from jax import lax
import numpy as np

D_MODEL = 1024
BATCH = 1
SEQ = 256
DEPTH = 2

HALF = D_MODEL // 2
HGRN_HEADS = 4
HGRN_DIM = HALF // HGRN_HEADS
HGRN_CHUNK = 64
FOX_HEADS = 8
FOX_DIM = HALF // FOX_HEADS
LRU_WIDTH = HALF
LRU_BLOCKS = 8
LRU_BLOCK_DIM = LRU_WIDTH // LRU_BLOCKS
LRU_C = 8.0
CONV_WIDTH = 4
SB_HEADS = 8
SB_DIM = HALF // SB_HEADS
Q_BLOCK = 128
D_FF = -(-8 * D_MODEL // (3 * 256)) * 256
N_EVEN = (DEPTH + 1) // 2
N_ODD = DEPTH // 2
ALPHA = (2 * DEPTH) ** 0.25
BETA = (8 * DEPTH) ** -0.25
EVEN_IN = 7 * HALF + FOX_HEADS
ODD_IN = 2 * LRU_WIDTH + 3 * HALF
EPS = 1e-5


def layer_norm(x, g, b):
    xf = x.astype(jnp.float32)
    mu = jnp.mean(xf, axis=-1, keepdims=True)
    xc = xf - mu
    var = jnp.mean(xc * xc, axis=-1, keepdims=True)
    y = xc * lax.rsqrt(var + EPS) * g.astype(jnp.float32) + b.astype(jnp.float32)
    return y.astype(x.dtype)

def rms_norm_f32(x, g):
    xf = x.astype(jnp.float32)
    return xf * lax.rsqrt(jnp.mean(xf * xf, axis=-1, keepdims=True) + EPS) * g.astype(jnp.float32)

def split_cols(t, sizes):
    return jnp.split(t, np.cumsum(sizes)[:-1].tolist(), axis=-1)

def hgrn2(q, f_logit, inp, g, lb, norm_g):
    B, S, _ = q.shape
    nc = S // HGRN_CHUNK
    z = f_logit.astype(jnp.float32)
    log_f = jnp.log(lb + (1.0 - lb) * jax.nn.sigmoid(z))
    k = (1.0 - lb) * jax.nn.sigmoid(-z)

    def to_chunks(t):
        return t.astype(jnp.float32).reshape(B, nc, HGRN_CHUNK, HGRN_HEADS, HGRN_DIM).transpose(1, 0, 3, 2, 4)

    qc, kc, vc, lc = to_chunks(q), to_chunks(k), to_chunks(inp), to_chunks(log_f)
    causal = jnp.tril(jnp.ones((HGRN_CHUNK, HGRN_CHUNK), dtype=bool))[:, :, None]

    def step(state, chunk):
        qt, kt, vt, lt = chunk
        b = jnp.cumsum(lt, axis=2)
        o_inter = jnp.einsum('bhtk,bhkv->bhtv', qt * jnp.exp(b), state)
        rel = b[:, :, :, None, :] - b[:, :, None, :, :]
        decay = jnp.exp(jnp.where(causal, rel, -jnp.inf))
        scores = jnp.einsum('bhtk,bhtsk,bhsk->bhts', qt, decay, kt)
        o = o_inter + jnp.einsum('bhts,bhsv->bhtv', scores, vt)
        b_last = b[:, :, -1:, :]
        state = jnp.exp(b_last[:, :, 0, :])[..., None] * state + jnp.einsum(
            'bhsk,bhsv->bhkv', kt * jnp.exp(b_last - b), vt)
        return state, o

    s0 = jnp.zeros((B, HGRN_HEADS, HGRN_DIM, HGRN_DIM), jnp.float32)
    _, o = lax.scan(step, s0, (qc, kc, vc, lc))
    o = o.transpose(1, 0, 3, 2, 4).reshape(B, S, HGRN_HEADS, HGRN_DIM)
    o = rms_norm_f32(o, norm_g)
    gate = jax.nn.silu(g.astype(jnp.float32)).reshape(B, S, HGRN_HEADS, HGRN_DIM)
    return (o * gate).reshape(B, S, HALF).astype(g.dtype)

def forgetting_attention(q, k, v, f_logit, b_f):
    B, S, _ = q.shape
    q = q.reshape(B, S, FOX_HEADS, FOX_DIM)
    k = k.reshape(B, S, FOX_HEADS, FOX_DIM)
    v = v.reshape(B, S, FOX_HEADS, FOX_DIM)
    log_f = jax.nn.log_sigmoid(f_logit.astype(jnp.float32) + b_f.astype(jnp.float32))
    c = jnp.cumsum(log_f, axis=1).transpose(0, 2, 1)
    scale = FOX_DIM ** -0.5
    outs = []
    for blk in range(S // Q_BLOCK):
        q0, q1 = blk * Q_BLOCK, (blk + 1) * Q_BLOCK
        logits = jnp.einsum('bqhd,bkhd->bhqk', q[:, q0:q1], k[:, :q1]).astype(jnp.float32) * scale
        logits = logits + c[:, :, q0:q1, None] - c[:, :, None, :q1]
        qpos = jnp.arange(q0, q1)[:, None]
        kpos = jnp.arange(q1)[None, :]
        logits = jnp.where(kpos <= qpos, logits, -jnp.inf)
        p = jax.nn.softmax(logits, axis=-1)
        outs.append(jnp.einsum('bhqk,bkhd->bqhd', p.astype(v.dtype), v[:, :q1]))
    return jnp.concatenate(outs, axis=1).reshape(B, S, HALF)

def stick_breaking_attention(q, k, v):
    B, S, _ = q.shape
    q = q.reshape(B, S, SB_HEADS, SB_DIM)
    k = k.reshape(B, S, SB_HEADS, SB_DIM)
    v = v.reshape(B, S, SB_HEADS, SB_DIM)
    scale = SB_DIM ** -0.5
    outs = []
    for blk in range(S // Q_BLOCK):
        q0, q1 = blk * Q_BLOCK, (blk + 1) * Q_BLOCK
        z = jnp.einsum('bqhd,bkhd->bhqk', q[:, q0:q1], k[:, :q1]).astype(jnp.float32) * scale
        qpos = jnp.arange(q0, q1)[:, None]
        kpos = jnp.arange(q1)[None, :]
        mask = kpos < qpos
        log_one_minus = jnp.where(mask, jax.nn.log_sigmoid(-z), 0.0)
        suffix = lax.cumsum(log_one_minus, axis=3, reverse=True) - log_one_minus
        log_w = jax.nn.log_sigmoid(z) + suffix
        w = jnp.where(mask, jnp.exp(log_w), 0.0)
        outs.append(jnp.einsum('bhqk,bkhd->bqhd', w.astype(v.dtype), v[:, :q1]))
    return jnp.concatenate(outs, axis=1).reshape(B, S, HALF)

def rg_lru_branch(xr, gate, conv_w, conv_b, wa, ba, wx, bx, lam):
    B, S, W = xr.shape
    xpad = jnp.pad(xr, ((0, 0), (CONV_WIDTH - 1, 0), (0, 0)))
    xc = conv_b + sum(conv_w[j] * xpad[:, j:j + S] for j in range(CONV_WIDTH))
    xb = xc.reshape(B, S, LRU_BLOCKS, LRU_BLOCK_DIM)
    r = jax.nn.sigmoid(jnp.einsum('bsni,nij->bsnj', xb, wa).reshape(B, S, W) + ba)
    i = jax.nn.sigmoid(jnp.einsum('bsni,nij->bsnj', xb, wx).reshape(B, S, W) + bx)
    log_a = -LRU_C * r.astype(jnp.float32) * jax.nn.softplus(-lam.astype(jnp.float32))
    a = jnp.exp(log_a)
    u = jnp.sqrt(-jnp.expm1(2.0 * log_a)) * (i * xc).astype(jnp.float32)

    def combine(left, right):
        a1, b1 = left
        a2, b2 = right
        return a1 * a2, a2 * b1 + b2

    _, h = lax.associative_scan(combine, (a, u), axis=1)
    return (h * jax.nn.gelu(gate.astype(jnp.float32), approximate=True)).astype(xr.dtype)

def swiglu(x, w13, w2):
    a, b = jnp.split(x @ w13, 2, axis=-1)
    return (jax.nn.silu(a) * b) @ w2

def first_inputs(seed: int = 0) -> dict:
    key = jax.random.key(seed)
    ks = jax.random.split(key, 24)
    f32 = jnp.float32
    nrm = lambda k, shp, s: jax.random.normal(k, shp, f32) * s
    x = jax.random.normal(ks[0], (BATCH, SEQ, D_MODEL), f32)
    ev_w_in = nrm(ks[1], (N_EVEN, D_MODEL, EVEN_IN), D_MODEL ** -0.5)
    ev_fox_bf = 1.0 + nrm(ks[2], (N_EVEN, FOX_HEADS), 0.1)
    hgrn_lb = nrm(ks[3], (DEPTH + 1, HALF), 0.1)
    ev_hgrn_norm_g = 1.0 + nrm(ks[4], (N_EVEN, HGRN_DIM), 0.02)
    ev_w_out = nrm(ks[5], (N_EVEN, D_MODEL, D_MODEL), BETA * D_MODEL ** -0.5)
    od_w_in = nrm(ks[6], (N_ODD, D_MODEL, ODD_IN), D_MODEL ** -0.5)
    od_conv_w = nrm(ks[7], (N_ODD, CONV_WIDTH, LRU_WIDTH), CONV_WIDTH ** -0.5)
    od_conv_b = nrm(ks[8], (N_ODD, LRU_WIDTH), 0.02)
    od_gate_a_w = nrm(ks[9], (N_ODD, LRU_BLOCKS, LRU_BLOCK_DIM, LRU_BLOCK_DIM), LRU_BLOCK_DIM ** -0.5)
    od_gate_a_b = nrm(ks[10], (N_ODD, LRU_WIDTH), 0.02)
    od_gate_x_w = nrm(ks[11], (N_ODD, LRU_BLOCKS, LRU_BLOCK_DIM, LRU_BLOCK_DIM), LRU_BLOCK_DIM ** -0.5)
    od_gate_x_b = nrm(ks[12], (N_ODD, LRU_WIDTH), 0.02)
    a_c = jax.random.uniform(ks[13], (N_ODD, LRU_WIDTH), f32, 0.9, 0.999) ** (1.0 / LRU_C)
    od_lru_lambda = jnp.log(a_c) - jnp.log1p(-a_c)
    od_w_out = nrm(ks[14], (N_ODD, D_MODEL, D_MODEL), BETA * D_MODEL ** -0.5)
    ffn_w13 = nrm(ks[15], (DEPTH, D_MODEL, 2 * D_FF), D_MODEL ** -0.5)
    ffn_w2 = nrm(ks[16], (DEPTH, D_FF, D_MODEL), BETA * D_FF ** -0.5)
    ln_g = 1.0 + nrm(ks[17], (DEPTH, 2, D_MODEL), 0.02)
    ln_b = nrm(ks[18], (DEPTH, 2, D_MODEL), 0.02)
    return {'x': x, 'ev_w_in': ev_w_in, 'ev_fox_bf': ev_fox_bf, 'hgrn_lb': hgrn_lb,
            'ev_hgrn_norm_g': ev_hgrn_norm_g, 'ev_w_out': ev_w_out, 'od_w_in': od_w_in,
            'od_conv_w': od_conv_w, 'od_conv_b': od_conv_b, 'od_gate_a_w': od_gate_a_w,
            'od_gate_a_b': od_gate_a_b, 'od_gate_x_w': od_gate_x_w, 'od_gate_x_b': od_gate_x_b,
            'od_lru_lambda': od_lru_lambda, 'od_w_out': od_w_out, 'ffn_w13': ffn_w13,
            'ffn_w2': ffn_w2, 'ln_g': ln_g, 'ln_b': ln_b}

def first_block(x, ev_w_in, ev_fox_bf, hgrn_lb, ev_hgrn_norm_g, ev_w_out, od_w_in, od_conv_w,
              od_conv_b, od_gate_a_w, od_gate_a_b, od_gate_x_w, od_gate_x_b, od_lru_lambda,
              od_w_out, ffn_w13, ffn_w2, ln_g, ln_b):
    lb_all = jnp.cumsum(jax.nn.softmax(hgrn_lb.astype(jnp.float32), axis=0), axis=0)
    for layer in range(DEPTH):
        if layer % 2 == 0:
            e = layer // 2
            proj = x @ ev_w_in[e]
            qa, fa, ia, ga, qb, kb, vb, fb = split_cols(proj, [HALF] * 7 + [FOX_HEADS])
            ya = hgrn2(qa, fa, ia, ga, lb_all[layer], ev_hgrn_norm_g[e])
            yb = forgetting_attention(qb, kb, vb, fb, ev_fox_bf[e])
            mix = jnp.concatenate([ya, yb], axis=-1) @ ev_w_out[e]
        else:
            o = layer // 2
            proj = x @ od_w_in[o]
            xr, gr, qd, kd, vd = split_cols(proj, [LRU_WIDTH, LRU_WIDTH, HALF, HALF, HALF])
            yc = rg_lru_branch(xr, gr, od_conv_w[o], od_conv_b[o], od_gate_a_w[o], od_gate_a_b[o],
                               od_gate_x_w[o], od_gate_x_b[o], od_lru_lambda[o])
            yd = stick_breaking_attention(qd, kd, vd)
            mix = jnp.concatenate([yc, yd], axis=-1) @ od_w_out[o]
        x = layer_norm(ALPHA * x + mix, ln_g[layer, 0], ln_b[layer, 0])
        x = layer_norm(ALPHA * x + swiglu(x, ffn_w13[layer], ffn_w2[layer]), ln_g[layer, 1], ln_b[layer, 1])
    return x


N_EVEN_2 = (DEPTH + 1) // 2
N_ODD_2 = DEPTH // 2
EPS_2 = 1e-6
NEG = -1e30
TINY = 1e-30

D_FF_2 = 2816

NUM_BUCKETS = 32
MAX_DISTANCE = 2048
N_BIAS_COLS = 16

MLA_HEADS = 8
MLA_Q_RANK = 256
MLA_KV_RANK = 128
MLA_NOPE = 64
MLA_ROPE = 32
MLA_V = 64
MLA_QK_DIM = MLA_NOPE + MLA_ROPE
ROPE_THETA = 10000.0

DIL_PATTERNS = ((128, 1), (512, 4), (2048, 16))
DIL_HEADS_PER_GROUP = 4
DIL_HEADS = DIL_HEADS_PER_GROUP * len(DIL_PATTERNS)
DIL_HEAD_DIM = 64
DIL_BIAS_COL0 = 0

SWA_HEADS = 8
SWA_KV_HEADS = 2
SWA_HEAD_DIM = 64
SWA_WINDOW = 128
SWA_BIAS_COL0 = 0

NSA_HEADS = 8
NSA_KV_HEADS = 2
NSA_HEAD_DIM = 64
NSA_CMP_LEN = 32
NSA_CMP_STRIDE = 16
NSA_CMP_HIDDEN = 128
NSA_SLC_BLOCK = 64
NSA_TOP_N = 16
NSA_WINDOW = 512
NSA_FORCE = 1e6
NSA_BIAS_COL0 = 8

AB_MLA_COLS = MLA_Q_RANK + MLA_KV_RANK + MLA_ROPE
AB_DIL_COLS = 3 * DIL_HEADS * DIL_HEAD_DIM
AB_IN = AB_MLA_COLS + AB_DIL_COLS
AB_MIX = MLA_HEADS * MLA_V + DIL_HEADS_PER_GROUP * DIL_HEAD_DIM
CD_SWA_COLS = (SWA_HEADS + 2 * SWA_KV_HEADS) * SWA_HEAD_DIM
CD_NSA_COLS = NSA_HEADS * NSA_HEAD_DIM + 6 * NSA_KV_HEADS * NSA_HEAD_DIM + 3 * NSA_HEADS
CD_IN = CD_SWA_COLS + CD_NSA_COLS
CD_MIX = SWA_HEADS * SWA_HEAD_DIM + NSA_HEADS * NSA_HEAD_DIM


def rms_norm(x, g):
    xf = x.astype(jnp.float32)
    y = xf * lax.rsqrt(jnp.mean(xf * xf, axis=-1, keepdims=True) + EPS_2)
    return (y * g.astype(jnp.float32)).astype(x.dtype)

def qk_norm(x, g):
    xf = x.astype(jnp.float32)
    return xf * lax.rsqrt(jnp.mean(xf * xf, axis=-1, keepdims=True) + EPS_2) * g.astype(jnp.float32)

def swiglu_half(x, g, w_gate, w_up, w_down):
    h = rms_norm(x, g)
    return (jax.nn.silu(h @ w_gate) * (h @ w_up)) @ w_down

def t5_bucket(dist):
    n = jnp.maximum(dist, 0)
    max_exact = NUM_BUCKETS // 2
    nf = jnp.maximum(n, 1).astype(jnp.float32)
    large = max_exact + (jnp.log(nf / max_exact) / math.log(MAX_DISTANCE / max_exact)
                         * (NUM_BUCKETS - max_exact)).astype(jnp.int32)
    large = jnp.minimum(large, NUM_BUCKETS - 1)
    return jnp.where(n < max_exact, n, large)

def rope(x, pos):
    half = x.shape[-1] // 2
    inv = jnp.power(ROPE_THETA, -jnp.arange(half, dtype=jnp.float32) / half)
    ang = pos[:, None] * inv[None, :]
    cos, sin = jnp.cos(ang)[:, None, :], jnp.sin(ang)[:, None, :]
    x1, x2 = x[..., :half], x[..., half:]
    return jnp.concatenate([x1 * cos - x2 * sin, x2 * cos + x1 * sin], axis=-1)

def causal_block_attention(q, k, v, scale):
    B_, S, H, dk = q.shape
    nb = S // Q_BLOCK
    qb = q.reshape(B_, nb, Q_BLOCK, H, dk).swapaxes(0, 1)
    kpos = jnp.arange(S)

    def one_block(args):
        qi, i = args
        qpos = i * Q_BLOCK + jnp.arange(Q_BLOCK)
        logits = jnp.einsum('bqhd,bkhd->bhqk', qi, k) * scale
        logits = jnp.where(kpos[None, :] <= qpos[:, None], logits, NEG)
        p = jax.nn.softmax(logits, axis=-1)
        return jnp.einsum('bhqk,bkhd->bqhd', p, v)

    out = lax.map(one_block, (qb, jnp.arange(nb)))
    return out.swapaxes(0, 1).reshape(B_, S, H, v.shape[-1])

def banded_attention(q, k, v, window, bias_cols, dist_scale=1, sinks=None):
    B_, S, G, R, dh = q.shape
    nb = -(-S // Q_BLOCK)
    Sp = nb * Q_BLOCK
    n_prev = -(-(window - 1) // Q_BLOCK)
    KW = (n_prev + 1) * Q_BLOCK
    q = jnp.pad(q, ((0, 0), (0, Sp - S), (0, 0), (0, 0), (0, 0)))
    kv_pad = ((0, 0), (n_prev * Q_BLOCK, Sp - S), (0, 0), (0, 0))
    k = jnp.pad(k, kv_pad)
    v = jnp.pad(v, kv_pad)
    qi_ = jnp.arange(Q_BLOCK)
    kc = jnp.arange(KW)
    delta = qi_[:, None] + n_prev * Q_BLOCK - kc[None, :]
    band = (delta >= 0) & (delta < window)
    bias = bias_cols.astype(jnp.float32)[t5_bucket(delta * dist_scale)]
    bias = jnp.transpose(bias.reshape(Q_BLOCK, KW, G, R), (2, 3, 0, 1))
    scale = dh ** -0.5
    qb = q.reshape(B_, nb, Q_BLOCK, G, R, dh).swapaxes(0, 1)

    def one_block(args):
        qblk, i = args
        start = i * Q_BLOCK
        kw = lax.dynamic_slice_in_dim(k, start, KW, axis=1)
        vw = lax.dynamic_slice_in_dim(v, start, KW, axis=1)
        logits = jnp.einsum('bqgrd,bkgd->bgrqk', qblk, kw) * scale + bias
        valid = band & (start - n_prev * Q_BLOCK + kc >= 0)[None, :]
        logits = jnp.where(valid, logits, NEG)
        if sinks is not None:
            sink_col = jnp.broadcast_to(sinks.astype(jnp.float32)[:, :, None, None],
                                        logits.shape[:-1] + (1,))
            logits = jnp.concatenate([logits, sink_col], axis=-1)
        lse = jax.nn.logsumexp(logits, axis=-1, keepdims=True)
        p = jnp.exp(logits - lse)[..., :KW]
        out = jnp.einsum('bgrqk,bkgd->bqgrd', p, vw)
        return out, lse[..., 0]

    out, lse = lax.map(one_block, (qb, jnp.arange(nb)))
    out = out.swapaxes(0, 1).reshape(B_, Sp, G, R, dh)[:, :S]
    lse = jnp.transpose(lse, (1, 0, 4, 2, 3)).reshape(B_, Sp, G, R)[:, :S]
    return out, lse

def mla_mixer(z, q_a_norm, w_q_b, kv_a_norm, w_kv_b, q_gain, k_gain, pos):
    B_, S, _ = z.shape
    c_q, c_kv, k_rope = jnp.split(z, [MLA_Q_RANK, MLA_Q_RANK + MLA_KV_RANK], axis=-1)
    q = (rms_norm(c_q, q_a_norm) @ w_q_b).reshape(B_, S, MLA_HEADS, MLA_QK_DIM)
    kv = (rms_norm(c_kv, kv_a_norm) @ w_kv_b).reshape(B_, S, MLA_HEADS, MLA_NOPE + MLA_V)
    k_nope, v = kv[..., :MLA_NOPE], kv[..., MLA_NOPE:]
    k = jnp.concatenate([k_nope, jnp.broadcast_to(k_rope[:, :, None, :], (B_, S, MLA_HEADS, MLA_ROPE))], axis=-1)
    q = qk_norm(q, q_gain)
    k = qk_norm(k, k_gain)
    q = jnp.concatenate([q[..., :MLA_NOPE], rope(q[..., MLA_NOPE:], pos)], axis=-1)
    k = jnp.concatenate([k[..., :MLA_NOPE], rope(k[..., MLA_NOPE:], pos)], axis=-1)
    return causal_block_attention(q, k, v.astype(jnp.float32), MLA_QK_DIM ** -0.5)

def dilated_mixer(z, q_gain, k_gain, rel_bias):
    B_, S, _ = z.shape
    Hg, dh = DIL_HEADS_PER_GROUP, DIL_HEAD_DIM
    zd = z.reshape(B_, S, 3, len(DIL_PATTERNS), Hg, dh)
    q = qk_norm(zd[:, :, 0], q_gain)
    k = qk_norm(zd[:, :, 1], k_gain)
    v = zd[:, :, 2].astype(jnp.float32)
    outs, lses = [], []
    for g, (w, d) in enumerate(DIL_PATTERNS):
        Sd = S // d

        def to_res(t):
            return t.reshape(B_, Sd, d, Hg, dh).transpose(0, 2, 1, 3, 4).reshape(B_ * d, Sd, Hg, dh)

        cols = rel_bias[:, DIL_BIAS_COL0 + g * Hg: DIL_BIAS_COL0 + (g + 1) * Hg]
        o, lse = banded_attention(to_res(q[:, :, g])[:, :, :, None], to_res(k[:, :, g]), to_res(v[:, :, g]),
                                  w // d + 1, cols, dist_scale=d)
        outs.append(o[:, :, :, 0].reshape(B_, d, Sd, Hg, dh).transpose(0, 2, 1, 3, 4).reshape(B_, S, Hg, dh))
        lses.append(lse[..., 0].reshape(B_, d, Sd, Hg).transpose(0, 2, 1, 3).reshape(B_, S, Hg))
    wts = jax.nn.softmax(jnp.stack(lses), axis=0)
    return jnp.sum(wts[..., None] * jnp.stack(outs), axis=0)

def swa_mixer(z, q_gain, k_gain, sinks, rel_bias):
    B_, S, _ = z.shape
    G, R, dh = SWA_KV_HEADS, SWA_HEADS // SWA_KV_HEADS, SWA_HEAD_DIM
    zq, zk, zv = jnp.split(z, [SWA_HEADS * dh, SWA_HEADS * dh + G * dh], axis=-1)
    q = qk_norm(zq.reshape(B_, S, G, R, dh), q_gain)
    k = qk_norm(zk.reshape(B_, S, G, dh), k_gain)
    v = zv.reshape(B_, S, G, dh).astype(jnp.float32)
    cols = rel_bias[:, SWA_BIAS_COL0:SWA_BIAS_COL0 + SWA_HEADS]
    o, _ = banded_attention(q, k, v, SWA_WINDOW, cols, sinks=sinks.reshape(G, R))
    return o.reshape(B_, S, SWA_HEADS * dh)

def nsa_mixer(z, q_gain, k_gains, cmp_pos, cmp_w1, cmp_w2, rel_bias):
    B_, S, _ = z.shape
    G, R, dh = NSA_KV_HEADS, NSA_HEADS // NSA_KV_HEADS, NSA_HEAD_DIM
    f32 = jnp.float32
    offs = np.cumsum([NSA_HEADS * dh] + [G * dh] * 6).tolist()
    zq, zkc, zvc, zks, zvs, zkw, zvw, zg = jnp.split(z, offs, axis=-1)
    q = qk_norm(zq.reshape(B_, S, G, R, dh), q_gain)

    def kvs(t):
        return t.reshape(B_, S, G, dh)

    scale = dh ** -0.5
    cols = rel_bias[:, NSA_BIAS_COL0:NSA_BIAS_COL0 + NSA_HEADS]
    tq = jnp.arange(S)

    n_cmp = (S - NSA_CMP_LEN) // NSA_CMP_STRIDE + 1
    blk_idx = np.arange(n_cmp)[:, None] * NSA_CMP_STRIDE + np.arange(NSA_CMP_LEN)[None, :]

    def compress(t, pos_emb, w1, w2):
        blocks = kvs(t)[:, blk_idx] + pos_emb[:, None, :]
        flat = blocks.transpose(0, 1, 3, 2, 4).reshape(B_, n_cmp, G, NSA_CMP_LEN * dh)
        return jax.nn.gelu(flat @ w1) @ w2

    k_c = qk_norm(compress(zkc, cmp_pos[0], cmp_w1[0], cmp_w2[0]), k_gains[0])
    v_c = compress(zvc, cmp_pos[1], cmp_w1[1], cmp_w2[1]).astype(f32)
    cmp_ok = jnp.asarray(blk_idx[:, -1])[None, :] <= tq[:, None]
    logits = jnp.einsum('bsgrd,bcgd->bgrsc', q, k_c) * scale
    logits = jnp.where(cmp_ok, logits, NEG)
    e = jnp.exp(logits - jnp.max(logits, axis=-1, keepdims=True)) * cmp_ok
    p_cmp = e / jnp.maximum(jnp.sum(e, axis=-1, keepdims=True), TINY)
    o_cmp = jnp.einsum('bgrsc,bcgd->bsgrd', p_cmp, v_c)

    n_slc = S // NSA_SLC_BLOCK
    ci = np.arange(n_cmp)[:, None] * NSA_CMP_STRIDE
    sj = np.arange(n_slc)[None, :] * NSA_SLC_BLOCK
    overlap = jnp.asarray(((ci < sj + NSA_SLC_BLOCK) & (ci + NSA_CMP_LEN > sj)).astype(np.float32))
    imp = jnp.einsum('bgrsc,cj->bgsj', p_cmp, overlap)
    tb = tq // NSA_SLC_BLOCK
    jj = jnp.arange(n_slc)
    causal_blk = jj[None, :] <= tb[:, None]
    forced = (jj[None, :] == 0) | (jj[None, :] == tb[:, None]) | (jj[None, :] == tb[:, None] - 1)
    score = jnp.where(causal_blk, imp + jnp.where(forced, NSA_FORCE, 0.0), -NSA_FORCE)
    top_n = min(NSA_TOP_N, n_slc)
    _, sel = lax.top_k(score, top_n)

    k_s = qk_norm(kvs(zks), k_gains[1]).transpose(0, 2, 1, 3).reshape(B_, G, n_slc, NSA_SLC_BLOCK, dh)
    v_s = kvs(zvs).astype(f32).transpose(0, 2, 1, 3).reshape(B_, G, n_slc, NSA_SLC_BLOCK, dh)
    nb = S // Q_BLOCK
    q_blk = q.transpose(0, 2, 3, 1, 4).reshape(B_, G, R, nb, Q_BLOCK, dh).transpose(3, 0, 1, 2, 4, 5)
    sel_blk = sel.reshape(B_, G, nb, Q_BLOCK, top_n).transpose(2, 0, 1, 3, 4)
    bias_gr = cols.astype(f32).T.reshape(G, R, NUM_BUCKETS)
    b_ix = jnp.arange(B_)[:, None, None, None]
    g_ix = jnp.arange(G)[None, :, None, None]
    g6 = jnp.arange(G)[None, :, None, None, None, None]
    r6 = jnp.arange(R)[None, None, :, None, None, None]
    tok = jnp.arange(NSA_SLC_BLOCK)

    def slc_block(args):
        qi, si, i = args
        kg = k_s[b_ix, g_ix, si]
        vg = v_s[b_ix, g_ix, si]
        dist = (i * Q_BLOCK + jnp.arange(Q_BLOCK))[None, None, :, None, None] - (si[..., None] * NSA_SLC_BLOCK + tok)
        bias = bias_gr[g6, r6, t5_bucket(dist)[:, :, None]]
        lg = jnp.einsum('bgrqd,bgqnkd->bgrqnk', qi, kg) * scale + bias
        lg = jnp.where((dist >= 0)[:, :, None], lg, NEG)
        p = jax.nn.softmax(lg, axis=(-2, -1))
        return jnp.einsum('bgrqnk,bgqnkd->bqgrd', p, vg)

    o_slc = lax.map(slc_block, (q_blk, sel_blk, jnp.arange(nb))).swapaxes(0, 1).reshape(B_, S, G, R, dh)

    o_win, _ = banded_attention(q, qk_norm(kvs(zkw), k_gains[2]), kvs(zvw).astype(f32), NSA_WINDOW, cols)

    gate = jax.nn.sigmoid(zg.astype(f32)).reshape(B_, S, G, R, 3)
    out = gate[..., 0:1] * o_cmp + gate[..., 1:2] * o_slc + gate[..., 2:3] * o_win
    return out.reshape(B_, S, NSA_HEADS * dh)

def second_inputs(seed: int = 0) -> dict:
    key = jax.random.key(seed)
    keys = iter(jax.random.split(key, 48))
    f32 = jnp.float32

    def w(shape, fan_in):
        return jax.random.normal(next(keys), shape, f32) * fan_in ** -0.5

    def gain(shape):
        return 1.0 + 0.05 * jax.random.normal(next(keys), shape, f32)

    NE, NO = N_EVEN_2, N_ODD_2
    return {
        "x": jax.random.normal(next(keys), (BATCH, SEQ, D_MODEL), f32),
        "rel_bias": 0.5 * jax.random.normal(next(keys), (NUM_BUCKETS, N_BIAS_COLS), f32),
        "ffn1_norm": gain((DEPTH, D_MODEL)),
        "ffn1_w_gate": w((DEPTH, D_MODEL, D_FF_2), D_MODEL),
        "ffn1_w_up": w((DEPTH, D_MODEL, D_FF_2), D_MODEL),
        "ffn1_w_down": w((DEPTH, D_FF_2, D_MODEL), D_FF_2),
        "mix_norm": gain((DEPTH, D_MODEL)),
        "ffn2_norm": gain((DEPTH, D_MODEL)),
        "ffn2_w_gate": w((DEPTH, D_MODEL, D_FF_2), D_MODEL),
        "ffn2_w_up": w((DEPTH, D_MODEL, D_FF_2), D_MODEL),
        "ffn2_w_down": w((DEPTH, D_FF_2, D_MODEL), D_FF_2),
        "ab_w_in": w((NE, D_MODEL, AB_IN), D_MODEL),
        "mla_q_a_norm": gain((NE, MLA_Q_RANK)),
        "mla_w_q_b": w((NE, MLA_Q_RANK, MLA_HEADS * MLA_QK_DIM), MLA_Q_RANK),
        "mla_kv_a_norm": gain((NE, MLA_KV_RANK)),
        "mla_w_kv_b": w((NE, MLA_KV_RANK, MLA_HEADS * (MLA_NOPE + MLA_V)), MLA_KV_RANK),
        "mla_q_norm": gain((NE, MLA_QK_DIM)),
        "mla_k_norm": gain((NE, MLA_QK_DIM)),
        "dil_q_norm": gain((NE, DIL_HEAD_DIM)),
        "dil_k_norm": gain((NE, DIL_HEAD_DIM)),
        "ab_w_out": w((NE, AB_MIX, D_MODEL), AB_MIX),
        "cd_w_in": w((NO, D_MODEL, CD_IN), D_MODEL),
        "swa_q_norm": gain((NO, SWA_HEAD_DIM)),
        "swa_k_norm": gain((NO, SWA_HEAD_DIM)),
        "swa_sinks": jax.random.normal(next(keys), (NO, SWA_HEADS), f32),
        "nsa_q_norm": gain((NO, NSA_HEAD_DIM)),
        "nsa_k_norm": gain((NO, 3, NSA_HEAD_DIM)),
        "nsa_cmp_pos": 0.1 * jax.random.normal(next(keys), (NO, 2, NSA_CMP_LEN, NSA_HEAD_DIM), f32),
        "nsa_cmp_w1": w((NO, 2, NSA_CMP_LEN * NSA_HEAD_DIM, NSA_CMP_HIDDEN), NSA_CMP_LEN * NSA_HEAD_DIM),
        "nsa_cmp_w2": w((NO, 2, NSA_CMP_HIDDEN, NSA_HEAD_DIM), NSA_CMP_HIDDEN),
        "cd_w_out": w((NO, CD_MIX, D_MODEL), CD_MIX),
    }

def second_block(x, rel_bias, ffn1_norm, ffn1_w_gate, ffn1_w_up, ffn1_w_down, mix_norm,
              ffn2_norm, ffn2_w_gate, ffn2_w_up, ffn2_w_down, ab_w_in, mla_q_a_norm, mla_w_q_b,
              mla_kv_a_norm, mla_w_kv_b, mla_q_norm, mla_k_norm, dil_q_norm, dil_k_norm, ab_w_out,
              cd_w_in, swa_q_norm, swa_k_norm, swa_sinks, nsa_q_norm, nsa_k_norm, nsa_cmp_pos,
              nsa_cmp_w1, nsa_cmp_w2, cd_w_out):
    B_, S, _ = x.shape
    pos = jnp.arange(S, dtype=jnp.float32)
    for layer in range(DEPTH):
        x = x + 0.5 * swiglu_half(x, ffn1_norm[layer], ffn1_w_gate[layer], ffn1_w_up[layer], ffn1_w_down[layer])
        h = rms_norm(x, mix_norm[layer])
        if layer % 2 == 0:
            e = layer // 2
            z = h @ ab_w_in[e]
            o_a = mla_mixer(z[..., :AB_MLA_COLS], mla_q_a_norm[e], mla_w_q_b[e], mla_kv_a_norm[e],
                            mla_w_kv_b[e], mla_q_norm[e], mla_k_norm[e], pos)
            o_b = dilated_mixer(z[..., AB_MLA_COLS:], dil_q_norm[e], dil_k_norm[e], rel_bias)
            mixed = jnp.concatenate([o_a.reshape(B_, S, -1), o_b.reshape(B_, S, -1)], axis=-1)
            mixed = mixed.astype(x.dtype) @ ab_w_out[e]
        else:
            o = layer // 2
            z = h @ cd_w_in[o]
            o_c = swa_mixer(z[..., :CD_SWA_COLS], swa_q_norm[o], swa_k_norm[o], swa_sinks[o], rel_bias)
            o_d = nsa_mixer(z[..., CD_SWA_COLS:], nsa_q_norm[o], nsa_k_norm[o], nsa_cmp_pos[o],
                            nsa_cmp_w1[o], nsa_cmp_w2[o], rel_bias)
            mixed = jnp.concatenate([o_c, o_d], axis=-1).astype(x.dtype) @ cd_w_out[o]
        x = x + mixed
        x = x + 0.5 * swiglu_half(x, ffn2_norm[layer], ffn2_w_gate[layer], ffn2_w_up[layer], ffn2_w_down[layer])
    return x


def setup_inputs(seed=0):
    out = dict(first_inputs(seed))
    for name, value in second_inputs(seed + 1).items():
        if name != "x":
            out[name + "_2"] = value
    return out


def reference(
    x, ev_w_in, ev_fox_bf, hgrn_lb, ev_hgrn_norm_g, ev_w_out, od_w_in, od_conv_w, od_conv_b,
    od_gate_a_w, od_gate_a_b, od_gate_x_w, od_gate_x_b, od_lru_lambda, od_w_out, ffn_w13,
    ffn_w2, ln_g, ln_b, rel_bias_2, ffn1_norm_2, ffn1_w_gate_2, ffn1_w_up_2, ffn1_w_down_2,
    mix_norm_2, ffn2_norm_2, ffn2_w_gate_2, ffn2_w_up_2, ffn2_w_down_2, ab_w_in_2,
    mla_q_a_norm_2, mla_w_q_b_2, mla_kv_a_norm_2, mla_w_kv_b_2, mla_q_norm_2, mla_k_norm_2,
    dil_q_norm_2, dil_k_norm_2, ab_w_out_2, cd_w_in_2, swa_q_norm_2, swa_k_norm_2, swa_sinks_2,
    nsa_q_norm_2, nsa_k_norm_2, nsa_cmp_pos_2, nsa_cmp_w1_2, nsa_cmp_w2_2, cd_w_out_2,
):
    x = first_block(
        x, ev_w_in, ev_fox_bf, hgrn_lb, ev_hgrn_norm_g, ev_w_out, od_w_in, od_conv_w, od_conv_b,
        od_gate_a_w, od_gate_a_b, od_gate_x_w, od_gate_x_b, od_lru_lambda, od_w_out, ffn_w13,
        ffn_w2, ln_g, ln_b,
    )
    return second_block(
        x, rel_bias_2, ffn1_norm_2, ffn1_w_gate_2, ffn1_w_up_2, ffn1_w_down_2, mix_norm_2,
        ffn2_norm_2, ffn2_w_gate_2, ffn2_w_up_2, ffn2_w_down_2, ab_w_in_2, mla_q_a_norm_2,
        mla_w_q_b_2, mla_kv_a_norm_2, mla_w_kv_b_2, mla_q_norm_2, mla_k_norm_2, dil_q_norm_2,
        dil_k_norm_2, ab_w_out_2, cd_w_in_2, swa_q_norm_2, swa_k_norm_2, swa_sinks_2,
        nsa_q_norm_2, nsa_k_norm_2, nsa_cmp_pos_2, nsa_cmp_w1_2, nsa_cmp_w2_2, cd_w_out_2,
    )


_drawn_inputs = setup_inputs


def setup_inputs(seed=0):
    import zlib

    import numpy as np

    out = dict(_drawn_inputs(seed))
    spreads = {}
    factors = {'ev_fox_bf': 64.0,
     'hgrn_lb': 5.408,
     'ev_hgrn_norm_g': 8.0,
     'od_conv_b': 3.952,
     'od_gate_a_b': 8.0,
     'od_gate_x_b': 8.0,
     'mla_q_a_norm_2': 7.171,
     'mla_kv_a_norm_2': 4.145,
     'mla_q_norm_2': 6.943,
     'mla_k_norm_2': 7.062,
     'dil_q_norm_2': 8.0,
     'dil_k_norm_2': 8.0,
     'swa_q_norm_2': 8.0,
     'swa_k_norm_2': 8.0,
     'swa_sinks_2': 200.0,
     'nsa_q_norm_2': 8.0,
     'nsa_k_norm_2': 8.0,
     'nsa_cmp_pos_2': 3.539,
     'ffn2_norm_2': 3.333}
    for name, (base, spread) in spreads.items():
        noise = np.random.default_rng([zlib.crc32(name.encode()), seed]).standard_normal(out[name].shape)
        drawn = base * np.exp(spread * noise) if base else spread * noise
        out[name] = __import__('jax').numpy.asarray(drawn.astype(out[name].dtype))
    for name, factor in factors.items():
        out[name] = (out[name] * factor).astype(out[name].dtype)
    return out
```

```python
from contextlib import ExitStack

import numpy as np

import concourse.bass as bass
from concourse import mybir

F32 = mybir.dt.float32
F32R = mybir.dt.float32r
ALU = mybir.AluOpType
ACT = mybir.ActivationFunctionType
AX = mybir.AxisListType

P = 128
S = 256
TT = S // P
D = 1024
KD = D // P
HALF = D // 2
NH = HALF // P
D_FF = 2816
FT = D_FF // P
ALPHA = 4 ** 0.25
EPS_LN = 1e-5
EPS_RMS = 1e-6
NEG = -1e30
FLT_MAX = 3.0e38
SLOTS = 4
SLOT = 4096
BANK = 512

HGRN_HEADS, HGRN_DIM = 4, 128
HD = 64
MLA_H, MLA_NOPE, MLA_ROPE = 8, 64, 32
MLA_QK = MLA_NOPE + MLA_ROPE
N_CMP, CMP_STRIDE, CMP_LEN = 15, 16, 32


class Mark:

    def __init__(self, nc, name):
        self.sem = nc.alloc_semaphore(name)
        self.at = 0

    def after(self, n):
        return self.sem, self.at + n

    def passed(self, n):
        self.at += n


class Steps:

    def __init__(self, nc, name):
        self.sem = nc.alloc_semaphore(name)
        self.n = 0

    def done(self, eng, ins):
        self.n += 1
        ins.then_inc(self.sem, 1)
        eng.wait_ge(self.sem, self.n)


def bc(ap, axis, n):
    a = ap.unsqueeze(axis)
    shape = list(a.shape)
    shape[axis] = n
    return a.to_broadcast(shape)


class Core:

    def __init__(self, nc, w, out):
        self.nc, self.w, self.out = nc, w, out
        sb = nc.alloc_sbuf_tensor
        self.ident = sb("ident", [P, P], F32)
        self.ones = sb("ones", [P, S], F32)
        self.causal = sb("causal", [P, S], F32)
        self.slot = sb("weight_slots", [P, SLOTS, SLOT], F32)
        self.x = sb("residual", [P, TT, D], F32)
        self.xn = sb("normed", [P, TT, D], F32)
        self.act_hi = sb("act_hi", [P, KD, S], F32R)
        self.act_lo = sb("act_lo", [P, KD, S], F32R)
        self.gb = sb("ln_gain_bias", [P, 2, D], F32)
        self.cols = sb("param_cols", [P, P], F32)
        self.cols2 = sb("param_cols2", [P, P], F32)
        self.st = sb("stats", [P, 64], F32)
        self.small = sb("small_tables", [P, w["const_small"].shape[1]], F32)
        self.bias_dram = nc.dram_tensor("bias_rows_dram", (28, 3 * P), F32).ap()
        self.ps = nc.alloc_psum_tensor("banks", [P, 8, BANK], F32)
        self.loaded = Mark(nc, "loaded")
        self.consts_ready = Mark(nc, "consts_ready")
        self.set_up = Mark(nc, "set_up")
        self.gate_up_hi = Mark(nc, "gate_up_hi")
        self.gate_up_split = Mark(nc, "gate_up_split")
        self.down_hi = Mark(nc, "down_hi")
        self.down_split = Mark(nc, "down_split")
        self.hidden_hi = Mark(nc, "hidden_hi")
        self.hidden_split = Mark(nc, "hidden_split")
        self.part_hi = Mark(nc, "part_hi")
        self.part_split = Mark(nc, "part_split")
        self.part_used = Mark(nc, "part_used")
        self.gate_up_ready = Mark(nc, "gate_up_ready")
        self.silu_ready = Mark(nc, "silu_ready")
        self.hidden_ready = Mark(nc, "hidden_ready")
        self.down_used = Mark(nc, "down_used")
        self.product_ready = Mark(nc, "product_ready")
        self.product_copied = Mark(nc, "product_copied")
        self.acc_ready = Mark(nc, "acc_ready")
        self.scores_ready = Mark(nc, "scores_ready")
        self.logits_ready = Mark(nc, "logits_ready")
        self.probs_ready = Mark(nc, "probs_ready")
        self.probs_flipped = Mark(nc, "probs_flipped")
        self.probs_T_ready = Mark(nc, "probs_T_ready")
        self.heads_ready = Mark(nc, "heads_ready")
        self.heads_done = Mark(nc, "heads_done")
        self.stats_ready = Mark(nc, "stats_ready")
        self.root_ready = Mark(nc, "root_ready")
        self.normed_ready = Mark(nc, "normed_ready")
        self.flipped = Mark(nc, "flipped")
        self.flip_copied = Mark(nc, "flip_copied")
        self.stored = Mark(nc, "stored")
        self.pe_a = Mark(nc, "pe_a")
        self.pe_b = Mark(nc, "pe_b")
        self.pe_c = Mark(nc, "pe_c")
        self.act_a = Mark(nc, "act_a")
        self.act_b = Mark(nc, "act_b")
        self.act_c = Mark(nc, "act_c")
        self.dve_a = Mark(nc, "dve_a")
        self.dve_b = Mark(nc, "dve_b")
        self.dve_c = Mark(nc, "dve_c")
        self.pool_a = Mark(nc, "pool_a")
        self.pool_b = Mark(nc, "pool_b")
        self.weights_in = [nc.alloc_semaphore(f"weights_in{i}") for i in range(SLOTS)]
        self.weights_used = nc.alloc_semaphore("weights_used")
        self.dve = Steps(nc, "dve_steps")
        self.act = Steps(nc, "act_steps")
        self.pool = Steps(nc, "pool_steps")
        self.n_names = 0
        self.items, self.arrived, self.first, self.issued = [], [], {}, 0
        self.plan_weights()


    def slot_view(self, j, k, n, at=0):
        return self.slot[:, j % SLOTS, at:at + k * n].rearrange("p (k n) -> p k n", k=k)

    def plan_weights(self):
        w = self.w

        def add(*pieces):
            j = len(self.items)
            self.items.append([(self.slot_view(j, k, n, at), src) for src, k, n, at in pieces])
            before = self.arrived[j - SLOTS] if j >= SLOTS else 0
            self.arrived.append(before + 16 * len(pieces))

        def columns(name, mat, k, width):
            self.first[name] = len(self.items)
            for c in range(0, width, BANK):
                n = min(BANK, width - c)
                add((mat[:, c:c + n].rearrange("(k p) n -> p k n", p=P), k, n, 0))

        def ffn(name, gate, up, down):
            self.first[name] = len(self.items)
            for c in range(FT // 2):
                h = slice(256 * c, 256 * c + 256)
                add((gate[:, h].rearrange("(k p) n -> p k n", p=P), KD, 256, 0),
                    (up[:, h].rearrange("(k p) n -> p k n", p=P), KD, 256, 2048))
                add((down[h, 0:HALF].rearrange("(k p) n -> p k n", p=P), 2, HALF, 0),
                    (down[h, HALF:D].rearrange("(k p) n -> p k n", p=P), 2, HALF, 1024))

        w13, w2 = w["ffn_w13"], w["ffn_w2"]
        columns("ev_in", w["ev_w_in"][0], KD, 3592)
        columns("ev_out", w["ev_w_out"][0], KD, D)
        ffn("ffn0", w13[0, :, 0:D_FF], w13[0, :, D_FF:2 * D_FF], w2[0])
        columns("od_in", w["od_w_in"][0], KD, 2560)
        columns("od_out", w["od_w_out"][0], KD, D)
        ffn("ffn1", w13[1, :, 0:D_FF], w13[1, :, D_FF:2 * D_FF], w2[1])
        for layer in range(2):
            ffn(f"ffn{2 + 2 * layer}", w["ffn1_w_gate_2"][layer], w["ffn1_w_up_2"][layer],
                w["ffn1_w_down_2"][layer])
            if layer == 0:
                columns("ab_in", w["ab_w_in_2"][0], KD, 2720)
                self.first["mla_b"] = len(self.items)
                add((w["mla_w_q_b_2"][0].rearrange("(k p) n -> p k n", p=P), 2, 768, 0),
                    (w["mla_w_kv_b_2"][0].rearrange("(k p) n -> p k n", p=P), 1, D, 1536))
                columns("ab_out", w["ab_w_out_2"][0], 6, D)
            else:
                columns("cd_in", w["cd_w_in_2"][0], KD, 2072)
                self.first["cmp_w1"] = len(self.items)
                add((w["nsa_cmp_w1_2"][0, 0].rearrange("(l p) n -> p l n", p=P), 16, P, 0),
                    (w["nsa_cmp_w1_2"][0, 1].rearrange("(l p) n -> p l n", p=P), 16, P, 2048))
                columns("cd_out", w["cd_w_out_2"][0], KD, D)
            ffn(f"ffn{3 + 2 * layer}", w["ffn2_w_gate_2"][layer], w["ffn2_w_up_2"][layer],
                w["ffn2_w_down_2"][layer])

    def uid(self):
        self.n_names += 1
        return self.n_names

    def load_weights(self, sp, until):
        while self.issued < min(until, len(self.items)):
            j = self.issued
            if j >= SLOTS:
                sp.wait_ge(self.weights_used, j - SLOTS + 1)
            for dst, src in self.items[j]:
                sp.dma_start(dst, src).then_inc(self.weights_in[j % SLOTS], 16)
            self.issued += 1



PARAM_ROWS = [("hgrn_lb", 12), ("od_conv_w", 16), ("od_conv_b", 4), ("od_gate_a_b", 4), ("od_gate_x_b", 4),
              ("od_lru_lambda", 4), ("ffn1_norm_2", 16), ("mix_norm_2", 16), ("ffn2_norm_2", 16),
              ("mla_q_a_norm_2", 2), ("mla_kv_a_norm_2", 1), ("nsa_cmp_pos_2", 32)]
PARAM_AT = {}
_n = 0
for _name, _rows in PARAM_ROWS:
    PARAM_AT[_name] = _n
    _n += _rows
N_ROWS = _n
HEAD_GAINS = ["dil_q_norm_2", "dil_k_norm_2", "swa_q_norm_2", "swa_k_norm_2", "nsa_q_norm_2",
              "nsa_k0", "nsa_k1", "nsa_k2"]
GAIN_AT = {name: i for i, name in enumerate(HEAD_GAINS)}
FOX_ROW = len(HEAD_GAINS)
N_ROWS2 = FOX_ROW + 1


def flat_rows(ap):
    s = ap.shape
    if len(s) == 1:
        return ap.rearrange("(r c) -> r c", c=P)
    if len(s) == 2:
        return ap.rearrange("a (r c) -> (a r) c", c=P)
    if len(s) == 3:
        return ap.rearrange("a b (r c) -> (a b r) c", c=P)
    return ap.rearrange("a b (r l) c -> (a b r) (l c)", l=2)


def constants(k):
    nc, w = k.nc, k.w
    with ExitStack() as ctx:
        rows = ctx.enter_context(nc.sbuf_tensor("param_rows", [P, P], F32))
        rows2 = ctx.enter_context(nc.sbuf_tensor("param_rows2", [P, P], F32))
        block = ctx.enter_context(nc.Block())
        loads = len(PARAM_ROWS) + 2 * len(HEAD_GAINS) + 3

        @block.sync
        def _(sp):
            sp.dma_start(k.x[:], w["x"][0].rearrange("(t p) d -> p t d", p=P)).then_inc(k.loaded.sem, 16)
            for name, n in PARAM_ROWS:
                r = PARAM_AT[name]
                sp.dma_start(rows[r:r + n, :], flat_rows(w[name])).then_inc(k.loaded.sem, 16)
            k.load_weights(sp, SLOTS)

        @block.scalar
        def _(act):
            act.dma_start(k.small[:], w["const_small"]).then_inc(k.loaded.sem, 16)
            act.wait_ge(*k.set_up.after(1))
            for i, name in enumerate(HEAD_GAINS):
                src = w["nsa_k_norm_2"][0, int(name[-1]):int(name[-1]) + 1, :] if name.startswith("nsa_k") else w[name]
                for half in range(2):
                    act.dma_start(rows2[i:i + 1, half * HD:half * HD + HD], src).then_inc(k.loaded.sem, 16)
            act.dma_start(rows2[FOX_ROW:FOX_ROW + 1, 0:8], w["ev_fox_bf"]).then_inc(k.loaded.sem, 16)

        @block.gpsimd
        def _(pool):
            k.pool.done(pool, pool.memset(rows2[:], 0.0))
            pool.sem_inc(k.set_up.sem, 1)
            pool.memset(k.ones[:], 1.0).then_inc(k.consts_ready.sem, 1)
            k.pool.done(pool, pool.memset(k.ident[:], 0.0))
            k.pool.done(pool, pool.memset(k.causal[:], 0.0))
            pool.affine_select(out=k.ident[:], in_=k.ident[:], compare_op=ALU.not_equal, fill=1.0, base=0,
                               pattern=[[-1, P]], channel_multiplier=1).then_inc(k.consts_ready.sem, 1)
            pool.affine_select(out=k.causal[:], in_=k.causal[:], compare_op=ALU.is_ge, fill=NEG, base=P,
                               pattern=[[-1, S]], channel_multiplier=1).then_inc(k.consts_ready.sem, 1)

        @block.vector
        def _(dve):
            dve.wait_ge(*k.pe_a.after(1))
            dve.tensor_copy(k.cols[:, 0:N_ROWS], k.ps[:, 0, 0:N_ROWS]).then_inc(k.product_copied.sem, 1)
            dve.tensor_copy(k.cols2[:, 0:P], k.ps[:, 1, 0:P]).then_inc(k.product_copied.sem, 1)

        @block.tensor
        def _(pe):
            pe.wait_ge(*k.consts_ready.after(3))
            pe.wait_ge(*k.loaded.after(16 * loads))
            pe.transpose(k.ps[:, 0, 0:N_ROWS], rows[0:N_ROWS, :], k.ident[0:N_ROWS, 0:N_ROWS])
            pe.transpose(k.ps[:, 1, 0:P], rows2[:], k.ident[:]).then_inc(k.pe_a.sem, 1)
    k.loaded.passed(16 * loads)
    k.set_up.passed(1)
    k.consts_ready.passed(3)
    k.pe_a.passed(1)
    k.product_copied.passed(2)



def norm(k, residual=None, layer_norm=None, rms=None):
    ps, x = k.ps, k.x
    st = k.st
    src = k.xn if rms is not None else k.x
    with k.nc.Block() as block:
        @block.vector
        def _(dve):
            if residual is not None:
                a, b = residual
                for t in range(TT):
                    acc = ps[:, 2 * t:2 * t + 2, :].rearrange("p b n -> p (b n)")
                    if a == 1.0:
                        ins = dve.scalar_tensor_tensor(out=x[:, t], in0=acc, scalar=b, in1=x[:, t],
                                                       op0=ALU.mult, op1=ALU.add)
                    else:
                        ins = dve.scalar_tensor_tensor(out=x[:, t], in0=x[:, t], scalar=a, in1=acc,
                                                       op0=ALU.mult, op1=ALU.add)
                    k.dve.done(dve, ins)
            if layer_norm is not None:
                for t in range(TT):
                    for h in range(2):
                        c = 6 * (2 * t + h)
                        ins = dve.bn_stats(st[:, c:c + 6], x[:, t, BANK * h:BANK * h + BANK])
                k.dve.done(dve, ins)
                for t in range(TT):
                    ins = dve.bn_aggr(st[:, 24 + 2 * t:26 + 2 * t], st[:, 12 * t:12 * t + 12])
                k.dve.done(dve, ins)
                var = st[:, 24:28].rearrange("p (t c) -> p t c", c=2)[:, :, 1]
                dve.tensor_scalar(st[:, 32:34], var, EPS_LN, None, ALU.add).then_inc(k.stats_ready.sem, 1)
                dve.wait_ge(*k.root_ready.after(1))
                k.dve.done(dve, dve.reciprocal(st[:, 36:38], st[:, 34:36]))
                for t in range(TT):
                    ins = dve.tensor_scalar(x[:, t], x[:, t], st[:, 24 + 2 * t:25 + 2 * t], st[:, 36 + t:37 + t],
                                            ALU.subtract, ALU.mult)
                k.dve.done(dve, ins)
                dve.wait_ge(*k.loaded.after(32))
                for t in range(TT):
                    ins = dve.tensor_tensor(x[:, t], x[:, t], k.gb[:, 0], ALU.mult)
                k.dve.done(dve, ins)
                for t in range(TT):
                    ins = dve.tensor_tensor(x[:, t], x[:, t], k.gb[:, 1], ALU.add)
                k.dve.done(dve, ins)
            if rms is not None:
                for t in range(TT):
                    ins = dve.scalar_tensor_tensor(out=k.xn[:, t], in0=x[:, t], scalar=1.0 / D, in1=x[:, t],
                                                   op0=ALU.mult, op1=ALU.mult, accum_out=st[:, 40 + t:41 + t])
                k.dve.done(dve, ins)
                dve.tensor_scalar(st[:, 42:44], st[:, 40:42], EPS_RMS, None, ALU.add).then_inc(k.stats_ready.sem, 1)
                dve.wait_ge(*k.root_ready.after(1 + (layer_norm is not None)))
                k.dve.done(dve, dve.reciprocal(st[:, 46:48], st[:, 44:46]))
                for t in range(TT):
                    ins = dve.tensor_scalar(k.xn[:, t], x[:, t], st[:, 46 + t:47 + t], None, ALU.mult)
                k.dve.done(dve, ins)
            dve.sem_inc(k.normed_ready.sem, 1)
            for q in range(KD):
                dve.wait_ge(*k.flip_copied.after(q // 2 + 1))
                psum = ps[:, 4 + q // 2, S * (q % 2):S * (q % 2) + S]
                hi = k.act_hi[:, q].bitcast(F32)
                if rms is not None:
                    dve.scalar_tensor_tensor(out=k.act_lo[:, q], in0=psum, scalar=k.cols[:, rms + q:rms + q + 1],
                                             in1=hi, op0=ALU.mult, op1=ALU.subtract)
                else:
                    dve.tensor_tensor(k.act_lo[:, q], psum, hi, ALU.subtract)

        @block.scalar
        def _(act):
            n = 0
            if layer_norm is not None:
                n += 1
                act.wait_ge(*k.stats_ready.after(n))
                act.activation(st[:, 34:36], st[:, 32:34], ACT.Sqrt).then_inc(k.root_ready.sem, 1)
            if rms is not None:
                n += 1
                act.wait_ge(*k.stats_ready.after(n))
                act.activation(st[:, 44:46], st[:, 42:44], ACT.Sqrt).then_inc(k.root_ready.sem, 1)
            for q in range(KD):
                act.wait_ge(*k.flipped.after(q // 2 + 1))
                psum = ps[:, 4 + q // 2, S * (q % 2):S * (q % 2) + S]
                scale = k.cols[:, rms + q:rms + q + 1] if rms is not None else 1.0
                ins = act.activation(k.act_hi[:, q], psum, ACT.Copy, scale=scale)
                if q % 2:
                    ins.then_inc(k.flip_copied.sem, 1)

        @block.tensor
        def _(pe):
            pe.wait_ge(*k.normed_ready.after(1))
            for q in range(KD):
                for t in range(TT):
                    c = S * (q % 2) + P * t
                    ins = pe.transpose(ps[:, 4 + q // 2, c:c + P], src[:, t, P * q:P * q + P], k.ident[:])
                if q % 2:
                    ins.then_inc(k.flipped.sem, 1)

        @block.sync
        def _(sp):
            if layer_norm is not None:
                i, j = layer_norm
                for n, name in enumerate(("ln_g", "ln_b")):
                    row = k.w[name][i, j:j + 1, :]
                    sp.dma_start(k.gb[:, n], row.to_broadcast([P, D])).then_inc(k.loaded.sem, 16)
    n = (layer_norm is not None) + (rms is not None)
    k.stats_ready.passed(n)
    k.root_ready.passed(n)
    k.loaded.passed(32 if layer_norm is not None else 0)
    k.normed_ready.passed(1)
    k.flipped.passed(KD // 2)
    k.flip_copied.passed(KD // 2)


def store_result(k):
    with k.nc.Block() as block:
        @block.vector
        def _(dve):
            for t in range(TT):
                acc = k.ps[:, 2 * t:2 * t + 2, :].rearrange("p b n -> p (b n)")
                dve.scalar_tensor_tensor(out=k.x[:, t], in0=acc, scalar=0.5, in1=k.x[:, t],
                                         op0=ALU.mult, op1=ALU.add).then_inc(k.normed_ready.sem, 1)

        @block.sync
        def _(sp):
            for t in range(TT):
                sp.wait_ge(*k.normed_ready.after(t + 1))
                sp.dma_start(k.out[0, P * t:P * t + P, :], k.x[:, t]).then_inc(k.stored.sem, 16)
            sp.wait_ge(*k.stored.after(16 * TT))
    k.normed_ready.passed(TT)
    k.stored.passed(16 * TT)



def split_products(pe, out, left, right, start, stop, **more):
    pe.matmul(out, left[0], right[0], start=start, stop=False, **more)
    pe.matmul(out, left[0], right[1], start=False, stop=False, **more)
    return pe.matmul(out, left[1], right[0], start=False, stop=stop, **more)


def product(k, name, kt, pieces):
    ps, nc = k.ps, k.nc
    first = k.first[name]
    per = kt // 2
    RING = 4
    done = [0]
    for kind, dst, width in pieces:
        done.append(done[-1] + {"token": TT, "feature": -(-width // P), "acc": 0}[kind])

    def results(i):
        kind, dst, width = pieces[i]
        if kind == "token":
            return [(4 * (i % 2) + t, ps[:, 4 * (i % 2) + t, 0:width], dst(t)) for t in range(TT)]
        if kind == "feature":
            return [(4 * (i % 2) + m, ps[0:min(P, width - P * m), 4 * (i % 2) + m, 0:S], dst(m))
                    for m in range(-(-width // P))]
        return []

    with ExitStack() as ctx:
        w_hi, w_lo = (ctx.enter_context(nc.sbuf_tensor(f"{name}_{n}", [P, RING, 2 * BANK], F32R)) for n in ("hi", "lo"))
        block = ctx.enter_context(nc.Block())

        def part(buf, n, width):
            return buf[:, n % RING, 0:2 * width].rearrange("p (k n) -> p k n", k=2)

        def raw(i, g):
            return k.slot_view(first + i, kt, pieces[i][2])[:, 2 * g:2 * g + 2, :]

        @block.scalar
        def _(act):
            for i in range(len(pieces)):
                j = first + i
                act.wait_ge(k.weights_in[j % SLOTS], k.arrived[j])
                for g in range(per):
                    n = per * i + g
                    if n >= RING:
                        act.wait_ge(*k.part_used.after(n - RING + 1))
                    act.activation(part(w_hi, n, pieces[i][2]), raw(i, g), ACT.Copy).then_inc(k.part_hi.sem, 1)

        @block.vector
        def _(dve):
            def copy_results(i):
                for r, (bank, psum, dst) in enumerate(results(i)):
                    if r == 0:
                        dve.wait_ge(*k.part_used.after(per * (i + 1)))
                    dve.tensor_copy(dst, psum).then_inc(k.product_copied.sem, 1)

            for i, (kind, dst, width) in enumerate(pieces):
                for g in range(per):
                    n = per * i + g
                    dve.wait_ge(*k.part_hi.after(n + 1))
                    dve.tensor_tensor(part(w_lo, n, width), raw(i, g), part(w_hi, n, width).bitcast(F32),
                                      ALU.subtract).then_inc(k.part_split.sem, 1)
                dve.wait_ge(*k.part_split.after(per * (i + 1)))
                dve.sem_inc(k.weights_used, 1)
                if i:
                    copy_results(i - 1)
            copy_results(len(pieces) - 1)

        @block.tensor
        def _(pe):
            for i, (kind, dst, width) in enumerate(pieces):
                if i >= 2 and done[i - 1]:
                    pe.wait_ge(*k.product_copied.after(done[i - 1]))
                for g in range(per):
                    n = per * i + g
                    pe.wait_ge(*k.part_split.after(n + 1))
                    wh, wl = part(w_hi, n, width), part(w_lo, n, width)
                    for e in range(2):
                        q = 2 * g + e
                        start, stop = q == 0, q == kt - 1
                        if kind == "feature":
                            for m, (bank, psum, _) in enumerate(results(i)):
                                c = slice(P * m, min(P * m + P, width))
                                ins = split_products(pe, psum, (wh[:, e, c], wl[:, e, c]),
                                                     (k.act_hi[:, q, :], k.act_lo[:, q, :]), start, stop)
                        else:
                            for t in range(TT):
                                bank = 2 * t + i if kind == "acc" else 4 * (i % 2) + t
                                c = slice(P * t, P * t + P)
                                ins = split_products(pe, ps[:, bank, 0:width], (k.act_hi[:, q, c], k.act_lo[:, q, c]),
                                                     (wh[:, e, :], wl[:, e, :]), start, stop)
                    ins.then_inc(k.part_used.sem, 1)

        @block.sync
        def _(sp):
            k.load_weights(sp, first + len(pieces) + SLOTS)
    n = per * len(pieces)
    k.part_hi.passed(n)
    k.part_split.passed(n)
    k.part_used.passed(n)
    k.product_copied.passed(done[-1])


def out_product(k, name, kt):
    product(k, name, kt, [("acc", None, BANK)] * 2)


def feed_forward(k, name):
    ps, nc = k.ps, k.nc
    first = k.first[name]
    BODY = 4
    pairs = FT // 2

    def item(f, down):
        return first + 2 * (f // 2) + down

    with ExitStack() as ctx:
        def sb(part, shape, dt):
            return ctx.enter_context(nc.sbuf_tensor(f"{name}_{part}", shape, dt))

        silu, hid = sb("silu", [P, 2, S], F32), sb("hidden", [P, 2, S], F32)
        hid_hi, hid_lo = (sb(n, [P, 2, S], F32R) for n in ("hidden_hi", "hidden_lo"))
        gu_hi, gu_lo = (sb(n, [P, 2, 2, KD, P], F32R) for n in ("gate_up_hi", "gate_up_lo"))
        dn_hi, dn_lo = (sb(n, [P, 2, 2, BANK], F32R) for n in ("down_hi", "down_lo"))
        block = ctx.enter_context(nc.Block())

        def raw_gate_up(f, u):
            w = k.slot[:, item(f, 0) % SLOTS, 2048 * u:2048 * u + 2048].rearrange("p (k n) -> p k n", k=KD)
            return w[:, :, P * (f % 2):P * (f % 2) + P]

        def raw_down(f):
            w = k.slot[:, item(f, 1) % SLOTS, 0:2048].rearrange("p (h k n) -> p h k n", h=2, k=2)
            return w[:, :, f % 2, :]

        def at(eng, mark, f, turn):
            eng.wait_ge(mark.sem, turn * BODY + (mark.at + f + 1))

        def arrived(eng, f, down, turn):
            j = item(f, down)
            eng.wait_ge(k.weights_in[j % SLOTS], turn * 32 + k.arrived[j])

        @block.tensor
        def _(pe):
            def gate_up(f, turn):
                for u in range(2):
                    pe.wait_ge(k.gate_up_split.sem, turn * 2 * BODY + (k.gate_up_split.at + 2 * f + u + 1))
                    for q in range(KD):
                        ins = split_products(pe, ps[:, 4 + f % 2, S * u:S * u + S],
                                             (gu_hi[:, f % 2, u, q, :], gu_lo[:, f % 2, u, q, :]),
                                             (k.act_hi[:, q, :], k.act_lo[:, q, :]), q == 0, q == KD - 1)
                ins.then_inc(k.gate_up_ready.sem, 1)

            def down(f, turn, start, stop):
                at(pe, k.down_split, f, turn)
                at(pe, k.hidden_split, f, turn)
                for t in range(TT):
                    c = slice(P * t, P * t + P)
                    for h in range(2):
                        ins = split_products(pe, ps[:, 2 * t + h, :], (hid_hi[:, f % 2, c], hid_lo[:, f % 2, c]),
                                             (dn_hi[:, f % 2, h, :], dn_lo[:, f % 2, h, :]), start, stop,
                                             skip_group_check=True)
                ins.then_inc(k.down_used.sem, 1)

            gate_up(0, 0)
            gate_up(1, 0)
            down(0, 0, True, False)
            turns = (FT - 2) // BODY
            assert 2 + BODY * turns == FT
            with pe.Fori(0, turns) as turn:
                for f in range(1, 1 + BODY):
                    gate_up(f + 1, turn)
                    down(f, turn, False, False)
            down(FT - 1, 0, False, True)

        FIRST = 2
        turns = (FT - FIRST - BODY) // BODY
        LAST = FIRST + BODY * turns

        def steps(eng, step):
            for f in range(FIRST):
                step(f, 0)
            with eng.Fori(0, turns) as turn:
                for f in range(FIRST, FIRST + BODY):
                    step(f, turn)
            for f in range(LAST, FT):
                step(f, 0)

        @block.scalar
        def _(act):
            def gate_up_hi(f, turn):
                if f % 2 == 0:
                    arrived(act, f, 0, turn)
                for u in range(2):
                    act.activation(gu_hi[:, f % 2, u], raw_gate_up(f, u), ACT.Copy).then_inc(k.gate_up_hi.sem, 1)

            def down_hi(f, turn):
                if f % 2 == 0:
                    arrived(act, f, 1, turn)
                if f >= 2:
                    at(act, k.down_used, f - 2, turn)
                act.activation(dn_hi[:, f % 2], raw_down(f), ACT.Copy).then_inc(k.down_hi.sem, 1)

            def step(f, turn):
                at(act, k.gate_up_ready, f, turn)
                if f >= 2:
                    at(act, k.hidden_ready, f - 2, turn)
                act.activation(silu[:, f % 2, :], ps[:, 4 + f % 2, 0:S], ACT.Silu).then_inc(k.silu_ready.sem, 1)
                at(act, k.hidden_ready, f, turn)
                if f >= 2:
                    at(act, k.down_used, f - 2, turn)
                act.activation(hid_hi[:, f % 2, :], hid[:, f % 2, :], ACT.Copy).then_inc(k.hidden_hi.sem, 1)
                if f + 2 < FT:
                    gate_up_hi(f + 2, turn)
                if f + 1 < FT:
                    down_hi(f + 1, turn)

            gate_up_hi(0, 0)
            gate_up_hi(1, 0)
            down_hi(0, 0)
            steps(act, step)

        @block.vector
        def _(dve):
            def gate_up_lo(f, turn):
                for u in range(2):
                    dve.wait_ge(k.gate_up_hi.sem, turn * 2 * BODY + (k.gate_up_hi.at + 2 * f + u + 1))
                    dve.tensor_tensor(gu_lo[:, f % 2, u], raw_gate_up(f, u), gu_hi[:, f % 2, u].bitcast(F32),
                                      ALU.subtract).then_inc(k.gate_up_split.sem, 1)

            def down_lo(f, turn):
                at(dve, k.down_hi, f, turn)
                dve.tensor_tensor(dn_lo[:, f % 2], raw_down(f), dn_hi[:, f % 2].bitcast(F32),
                                  ALU.subtract).then_inc(k.down_split.sem, 1)
                if f % 2:
                    at(dve, k.down_split, f, turn)
                    dve.sem_inc(k.weights_used, 2)

            def step(f, turn):
                at(dve, k.silu_ready, f, turn)
                if f >= 2:
                    at(dve, k.hidden_split, f - 2, turn)
                dve.tensor_tensor(hid[:, f % 2, :], ps[:, 4 + f % 2, S:2 * S], silu[:, f % 2, :],
                                  ALU.mult).then_inc(k.hidden_ready.sem, 1)
                at(dve, k.hidden_hi, f, turn)
                dve.tensor_tensor(hid_lo[:, f % 2, :], hid[:, f % 2, :], hid_hi[:, f % 2, :].bitcast(F32),
                                  ALU.subtract).then_inc(k.hidden_split.sem, 1)
                if f + 2 < FT:
                    gate_up_lo(f + 2, turn)
                if f + 1 < FT:
                    down_lo(f + 1, turn)

            gate_up_lo(0, 0)
            gate_up_lo(1, 0)
            down_lo(0, 0)
            steps(dve, step)

        @block.sync
        def _(sp):
            assert k.issued == first + SLOTS

            def pair(c, turn):
                for down in range(2):
                    j = first + 2 * c + down
                    sp.wait_ge(k.weights_used, turn * 4 + (j - SLOTS + 1))
                    for dst, src in k.items[j]:
                        step = turn * (512 * D if down else 512)
                        sp.dma_start(dst, bass.AP(src.tensor, src.offset + step, src.ap))\
                          .then_inc(k.weights_in[j % SLOTS], 16)

            turns = (pairs - 3) // 2
            with sp.Fori(0, turns) as turn:
                for c in (2, 3):
                    pair(c, turn)
            k.issued = first + 2 * (2 + 2 * turns)
            k.load_weights(sp, first + FT + SLOTS)
    k.gate_up_hi.passed(2 * FT)
    k.gate_up_split.passed(2 * FT)
    for mark in (k.down_hi, k.down_split, k.hidden_hi, k.hidden_split, k.gate_up_ready, k.silu_ready,
                 k.hidden_ready, k.down_used):
        mark.passed(FT)



def softmax_attention(k, heads, out, sink=None, gate=None, add=False):
    nc, ps = k.nc, k.ps
    H, G = len(heads), len(heads[0])
    RING = 6
    blocks = ((0, P), (P, P + S))
    with ExitStack() as ctx:
        def sb(name, shape):
            return ctx.enter_context(nc.sbuf_tensor(f"att{k.uid()}_{name}", shape, F32))

        logits, probs, probs_T = (sb(n, [P, RING, 3 * P]) for n in ("logits", "probs", "probs_T"))
        nmax_u, rows = sb("nmax_u", [P, H, TT, G]), sb("rows", [P, H, TT, G])
        nmax, den, fac, esink = (sb(n, [P, H, TT]) for n in ("nmax", "den", "fac", "esink"))
        tmp = sb("tmp", [P, 2, TT, HD])
        block = ctx.enter_context(nc.Block())

        @block.tensor
        def _(pe):
            def scores(h):
                for u, x in enumerate(heads[h]):
                    n = h * G + u
                    bank = ps[:, n % 4, :]
                    if n >= 4:
                        pe.wait_ge(*k.logits_ready.after((n - 4) // G + 1))
                    for t in range(TT):
                        a, b = blocks[t]
                        keys = P * (t + 1)
                        ins = pe.matmul(bank[:, a:b], x["q"](t), x["kT"][:, 0:keys], start=True, stop="extra" not in x)
                        if "extra" in x:
                            lhsT, rhs = x["extra"]
                            ins = pe.matmul(bank[:, a:b], lhsT, rhs[:, 0:keys], start=False, stop=True)
                    ins.then_inc(k.scores_ready.sem, 1)

            def flips(h):
                for u in range(G):
                    n = h * G + u
                    pe.wait_ge(*k.probs_ready.after(n + 1))
                    if n >= 2:
                        pe.wait_ge(*k.probs_T_ready.after(n - 1))
                    for j in range(3):
                        ins = pe.transpose(ps[:, 4 + n % 2, P * j:P * j + P], probs[:, n % RING, P * j:P * j + P],
                                           k.ident[:])
                    ins.then_inc(k.probs_flipped.sem, 1)

            def values(h):
                pe.wait_ge(*k.probs_T_ready.after(h * G + G))
                if h >= 2:
                    pe.wait_ge(*k.heads_done.after(h - 1))
                for t in range(TT):
                    o = ps[:, 6 + h % 2, HD * t:HD * t + HD]
                    for u, x in enumerate(heads[h]):
                        n = h * G + u
                        for s in range(t + 1):
                            j = t + s
                            ins = pe.matmul(o, probs_T[:, n % RING, P * j:P * j + P], x["v"](s),
                                            start=u == 0 and s == 0, stop=u == G - 1 and s == t)
                ins.then_inc(k.heads_ready.sem, 1)

            for i in range(H + 2):
                if i < H:
                    scores(i)
                if 1 <= i <= H:
                    flips(i - 1)
                if i >= 2:
                    values(i - 2)

        @block.vector
        def _(dve):
            def add_bias(h):
                for u, x in enumerate(heads[h]):
                    n = h * G + u
                    dve.wait_ge(*k.scores_ready.after(n + 1))
                    if n >= RING:
                        dve.wait_ge(*k.probs_ready.after(n - RING + 1))
                    for t in range(TT):
                        a, b = blocks[t]
                        ins = dve.tensor_tensor_reduce(out=logits[:, n % RING, a:b], in0=ps[:, n % 4, a:b],
                                                       in1=x["bias"][:, P * (1 - t):S], scale=-1.0, scalar=FLT_MAX,
                                                       op0=ALU.add, op1=ALU.min, accum_out=nmax_u[:, h, t, u:u + 1])
                if G > 1:
                    k.dve.done(dve, ins)
                    ins = dve.tensor_reduce(nmax[:, h, :], nmax_u[:, h], AX.X, ALU.min)
                elif sink:
                    k.dve.done(dve, ins)
                    ins = dve.tensor_scalar(nmax[:, h, :], nmax_u[:, h, :, 0], sink(h)[1], None, ALU.min)
                ins.then_inc(k.logits_ready.sem, 1)

            def copy_flips(h):
                for u in range(G):
                    n = h * G + u
                    dve.wait_ge(*k.probs_flipped.after(n + 1))
                    if n >= RING:
                        dve.wait_ge(*k.heads_ready.after((n - RING) // G + 1))
                    dve.tensor_copy(probs_T[:, n % RING, :], ps[:, 4 + n % 2, 0:3 * P]).then_inc(k.probs_T_ready.sem, 1)

            def finish(h):
                dve.wait_ge(*k.heads_ready.after(h + 1))
                total = rows[:, h, :, 0]
                if G > 1:
                    k.dve.done(dve, dve.tensor_reduce(den[:, h, :], rows[:, h], AX.X, ALU.add))
                    total = den[:, h, :]
                elif sink:
                    k.dve.done(dve, dve.tensor_tensor(den[:, h, :], rows[:, h, :, 0], esink[:, h, :], ALU.add))
                    total = den[:, h, :]
                k.dve.done(dve, dve.reciprocal(fac[:, h, :], total))
                if gate:
                    k.dve.done(dve, dve.tensor_tensor(fac[:, h, :], fac[:, h, :], gate(h), ALU.mult))
                o = ps[:, 6 + h % 2, 0:TT * HD].rearrange("p (t d) -> p t d", t=TT)
                if add:
                    k.dve.done(dve, dve.tensor_tensor(tmp[:, h % 2], o, bc(fac[:, h, :], 2, HD), ALU.mult))
                    ins = dve.tensor_tensor(out(h), out(h), tmp[:, h % 2], ALU.add)
                else:
                    ins = dve.tensor_tensor(out(h), o, bc(fac[:, h, :], 2, HD), ALU.mult)
                ins.then_inc(k.heads_done.sem, 1)

            for i in range(H + 2):
                if i < H:
                    add_bias(i)
                if 1 <= i <= H:
                    copy_flips(i - 1)
                if i >= 2:
                    finish(i - 2)

        @block.scalar
        def _(act):
            for h in range(H):
                act.wait_ge(*k.logits_ready.after(h + 1))
                top = nmax_u[:, h, :, 0] if G == 1 and not sink else nmax[:, h, :]
                if sink:
                    act.activation(esink[:, h, :], top, ACT.Exp, bias=sink(h)[0])
                for u in range(G):
                    n = h * G + u
                    if n >= RING:
                        act.wait_ge(*k.probs_flipped.after(n - RING + 1))
                    for t in range(TT):
                        a, b = blocks[t]
                        ins = act.activation(probs[:, n % RING, a:b], logits[:, n % RING, a:b], ACT.Exp,
                                             bias=top[:, t:t + 1], scale=-1.0, accum_out=rows[:, h, t, u:u + 1])
                    ins.then_inc(k.probs_ready.sem, 1)
    for mark in (k.scores_ready, k.probs_ready, k.probs_flipped, k.probs_T_ready):
        mark.passed(H * G)
    for mark in (k.logits_ready, k.heads_ready, k.heads_done):
        mark.passed(H)


def transpose_mix(k, tiles):
    ps = k.ps
    with k.nc.Block() as block:
        @block.tensor
        def _(pe):
            for n, q in enumerate(tiles):
                for t in range(TT):
                    ins = pe.transpose(ps[:, n % 8, P * t:P * t + P], k.xn[:, t, P * q:P * q + P], k.ident[:])
                ins.then_inc(k.flipped.sem, 1)

        @block.scalar
        def _(act):
            for n, q in enumerate(tiles):
                act.wait_ge(*k.flipped.after(n + 1))
                act.activation(k.act_hi[:, q], ps[:, n % 8, 0:S], ACT.Copy).then_inc(k.act_a.sem, 1)

        @block.vector
        def _(dve):
            for n, q in enumerate(tiles):
                dve.wait_ge(*k.act_a.after(n + 1))
                dve.tensor_tensor(k.act_lo[:, q], ps[:, n % 8, 0:S], k.act_hi[:, q].bitcast(F32), ALU.subtract)
    k.flipped.passed(len(tiles))
    k.act_a.passed(len(tiles))



LEVELS = [S >> (i + 1) for i in range(8)]


def hgrn_masks():
    s, t = np.arange(P)[:, None], np.arange(P)[None, :]
    out = [((s // (2 * m) == t // (2 * m)) & (s % (2 * m) < m) & (t % (2 * m) >= m)) for m in LEVELS[1:]]
    return np.stack(out + [s == t], axis=1).astype(np.float32)


def hgrn(k, q, z, v, g):
    nc, ps, w = k.nc, k.ps, k.w
    H = HGRN_HEADS
    with ExitStack() as ctx:
        def sb(name, shape):
            return ctx.enter_context(nc.sbuf_tensor(f"hgrn_{name}", shape, F32))

        masks = sb("masks", [P, len(LEVELS), P])
        key, fgt, B = sb("key", [P, H, S]), sb("forget", [P, H, S]), sb("B", [P, H, S])
        dif, E, qe, ke = (sb(n, [P, 2, H * S]) for n in ("dif", "E", "qe", "ke"))
        sT = sb("scores_T", [P, H, 3, P])
        lbs, lb, oml, top, tot = (sb(n, [P, 12 if n == "lbs" else 4]) for n in ("lbs", "lb", "oml", "top", "tot"))
        ng = sb("norm_gain", [P, P])
        o2, sil = sb("o2", [P, TT, HALF]), sb("silu", [P, TT, HALF])
        ssq, rms = sb("ssq", [P, TT * H]), sb("rms", [P, TT * H])
        row = k.cols[:, PARAM_AT["hgrn_lb"]:PARAM_AT["hgrn_lb"] + 12]

        with nc.Block() as block:
            @block.sync
            def _(sp):
                sp.dma_start(masks[:], w["const_hgrn_masks"]).then_inc(k.loaded.sem, 16)
                sp.dma_start(ng[:], w["ev_hgrn_norm_g"].to_broadcast([P, P])).then_inc(k.loaded.sem, 16)

            @block.gpsimd
            def _(pool):
                pool.memset(sT[:], 0.0)
                pool.memset(qe[:], 0.0)
                pool.memset(ke[:], 0.0)

            @block.scalar
            def _(act):
                act.activation(key[:], z[:], ACT.Sigmoid, scale=-1.0).then_inc(k.act_a.sem, 1)
                act.activation(fgt[:], z[:], ACT.Sigmoid).then_inc(k.act_a.sem, 1)
                act.wait_ge(*k.dve_a.after(1))
                act.activation(lbs[:], lbs[:], ACT.Exp).then_inc(k.act_a.sem, 1)
                act.wait_ge(*k.dve_a.after(2))
                act.activation(fgt[:], fgt[:], ACT.Ln).then_inc(k.act_a.sem, 1)

            @block.vector
            def _(dve):
                k.dve.done(dve, dve.tensor_tensor(top[:], row[:, 0:4], row[:, 4:8], ALU.max))
                k.dve.done(dve, dve.tensor_tensor(top[:], top[:], row[:, 8:12], ALU.max))
                dve.tensor_tensor(lbs[:].rearrange("p (r c) -> p r c", r=3), row.rearrange("p (r c) -> p r c", r=3),
                                  bc(top[:], 1, 3), ALU.subtract).then_inc(k.dve_a.sem, 1)
                dve.wait_ge(*k.act_a.after(3))
                k.dve.done(dve, dve.tensor_reduce(tot[:], lbs[:].rearrange("p (r c) -> p c r", r=3), AX.X, ALU.add))
                k.dve.done(dve, dve.reciprocal(tot[:], tot[:]))
                k.dve.done(dve, dve.tensor_tensor(lb[:], lbs[:, 0:4], tot[:], ALU.mult))
                k.dve.done(dve, dve.tensor_scalar(oml[:], lb[:], -1.0, 1.0, ALU.mult, ALU.add))
                for h in range(H):
                    ins = dve.tensor_scalar(fgt[:, h], fgt[:, h], oml[:, h:h + 1], lb[:, h:h + 1], ALU.mult, ALU.add)
                ins.then_inc(k.dve_a.sem, 1)
                for h in range(H):
                    ins = dve.tensor_scalar(key[:, h], key[:, h], oml[:, h:h + 1], None, ALU.mult)
                dve.wait_ge(*k.act_a.after(4))
                for h in range(H):
                    ins = dve.tensor_tensor_scan(B[:, h], k.ones[:], fgt[:, h], 0.0, ALU.mult, ALU.add)
                dve.wait_ge(*k.loaded.after(32))
        k.loaded.passed(32)
        k.act_a.passed(4)
        k.dve_a.passed(2)

        N = len(LEVELS)

        def half(buf, i, m, second):
            return buf[:, i % 2, :].rearrange("p (r c) -> p r c", c=2 * m)[:, :, m * second:m * second + m]

        with nc.Block() as block:
            @block.vector
            def _(dve):
                flat = B[:].rearrange("p h s -> p (h s)")

                def difference(i):
                    m = LEVELS[i]
                    pairs = flat.rearrange("p (r c) -> p r c", c=2 * m)
                    if i >= 2:
                        dve.wait_ge(*k.act_a.after(i - 1))
                    dve.tensor_tensor(dif[:, i % 2, :].rearrange("p (r c) -> p r c", c=2 * m), pairs,
                                      pairs[:, :, m - 1:m].to_broadcast([P, H * S // (2 * m), 2 * m]),
                                      ALU.subtract).then_inc(k.dve_a.sem, 1)

                def keep(i):
                    dve.wait_ge(*k.pe_a.after(i + 1))
                    b = 2 * (i % 2)
                    if i == 0:
                        dve.tensor_copy(sT[:, :, 1, :], ps[:, b, :].rearrange("p (h n) -> p h n", h=H))\
                           .then_inc(k.dve_b.sem, 1)
                        return
                    for t in range(TT):
                        mask = bc(masks[:, i - 1, :].bitcast(mybir.dt.int32), 1, H)
                        ins = dve.copy_predicated(sT[:, :, 2 * t, :], mask,
                                                  ps[:, b + t, :].rearrange("p (h n) -> p h n", h=H))
                    k.dve.done(dve, ins)
                    dve.sem_inc(k.dve_b.sem, 1)

                difference(0)
                difference(1)
                for i in range(N + 1):
                    if i + 2 < N:
                        difference(i + 2)
                    keep(i)

            @block.scalar
            def _(act):
                for i, m in enumerate(LEVELS):
                    act.wait_ge(*k.dve_a.after(i + 1))
                    if i >= 2:
                        act.wait_ge(*k.pool_a.after(i - 1))
                    act.activation(half(E, i, m, 0), half(dif, i, m, 0), ACT.Exp, scale=-1.0)
                    act.activation(half(E, i, m, 1), half(dif, i, m, 1), ACT.Exp).then_inc(k.act_a.sem, 1)

            @block.gpsimd
            def _(pool):
                for i, m in enumerate(LEVELS):
                    pool.wait_ge(*k.act_a.after(i + 1))
                    if i >= 2:
                        pool.wait_ge(*k.pe_a.after(i - 1))
                    pairs = dict(c=2 * m)
                    pool.tensor_tensor(half(qe, i, m, 1), q.rearrange("p h s -> p (h s)").rearrange(
                        "p (r c) -> p r c", **pairs)[:, :, m:2 * m], half(E, i, m, 1), ALU.mult)
                    pool.tensor_tensor(half(ke, i, m, 0), key[:].rearrange("p h s -> p (h s)").rearrange(
                        "p (r c) -> p r c", **pairs)[:, :, 0:m], half(E, i, m, 0), ALU.mult).then_inc(k.pool_a.sem, 1)

            @block.tensor
            def _(pe):
                for i in range(N + 1):
                    b = 2 * (i % 2)
                    if i < N:
                        pe.wait_ge(*k.pool_a.after(i + 1))
                    if i >= 2:
                        pe.wait_ge(*k.dve_b.after(i - 1))
                    for h in range(H):
                        for t in range(TT):
                            if i == 0:
                                if t:
                                    continue
                                left, right = ke[:, 0, S * h:S * h + P], qe[:, 0, S * h + P:S * h + S]
                            elif i < N:
                                c = S * h + P * t
                                left, right = ke[:, i % 2, c:c + P], qe[:, i % 2, c:c + P]
                            else:
                                left, right = key[:, h, P * t:P * t + P], q[:, h, P * t:P * t + P]
                            ins = pe.matmul(ps[:, b + t, P * h:P * h + P], left, right, start=True, stop=True)
                    ins.then_inc(k.pe_a.sem, 1)
                pe.wait_ge(*k.dve_b.after(N + 1))
                for t in range(TT):
                    for h in range(H):
                        for s in range(t + 1):
                            ins = pe.matmul(ps[:, 4 + t, P * h:P * h + P], sT[:, h, t + s, :],
                                            v[:, s, P * h:P * h + P], start=s == 0, stop=s == t)
                ins.then_inc(k.pe_b.sem, 1)
        k.dve_a.passed(N)
        k.act_a.passed(N)
        k.pool_a.passed(N)
        k.pe_a.passed(N + 1)
        k.dve_b.passed(N + 1)
        k.pe_b.passed(1)

        with nc.Block() as block:
            o = ps[:, 4:6, :]

            @block.scalar
            def _(act):
                act.activation(o2[:], o, ACT.Square).then_inc(k.act_a.sem, 1)
                act.activation(sil[:], g, ACT.Silu).then_inc(k.act_a.sem, 1)
                act.wait_ge(*k.dve_a.after(1))
                act.activation(rms[:], ssq[:], ACT.Sqrt).then_inc(k.act_a.sem, 1)

            @block.gpsimd
            def _(pool):
                pool.wait_ge(*k.act_a.after(2))
                pool.tensor_tensor(sil[:].rearrange("p t (h n) -> p (t h) n", h=H),
                                   sil[:].rearrange("p t (h n) -> p (t h) n", h=H), bc(ng[:], 1, TT * H),
                                   ALU.mult).then_inc(k.pool_a.sem, 1)

            @block.vector
            def _(dve):
                dve.wait_ge(*k.act_a.after(1))
                k.dve.done(dve, dve.tensor_reduce(ssq[:], o2[:].rearrange("p t (h n) -> p (t h) n", h=H),
                                                  AX.X, ALU.add))
                dve.tensor_scalar(ssq[:], ssq[:], 1.0 / HGRN_DIM, EPS_LN, ALU.mult, ALU.add).then_inc(k.dve_a.sem, 1)
                dve.wait_ge(*k.act_a.after(3))
                k.dve.done(dve, dve.reciprocal(rms[:], rms[:]))
                k.dve.done(dve, dve.tensor_tensor(o2[:].rearrange("p t (h n) -> p (t h) n", h=H),
                                                  o.rearrange("p t (h n) -> p (t h) n", h=H),
                                                  bc(rms[:], 2, P), ALU.mult))
                dve.wait_ge(*k.pool_a.after(1))
                dve.tensor_tensor(k.xn[:, :, 0:HALF], o2[:], sil[:], ALU.mult)
        k.act_a.passed(3)
        k.dve_a.passed(1)
        k.pool_a.passed(1)


def log_sigmoid_parts(k, act, dve_mark, act_mark, x, a, n):
    k.act.done(act, act.activation(a, x, ACT.Abs))
    k.act.done(act, act.activation(a, a, ACT.Exp, scale=-1.0))
    return act.activation(a, a, ACT.Ln, bias=1.0)


def fox(k, q, key, v, f):
    nc = k.nc
    H = 8
    with ExitStack() as ctx:
        def sb(name, shape):
            return ctx.enter_context(nc.sbuf_tensor(f"fox_{name}", shape, F32))

        one, lf, c = sb("one_hot", [H, H, P]), sb("log_f", [H, S]), sb("minus_c", [H, S])
        with nc.Block() as block:
            @block.scalar
            def _(act):
                act.preload_act_table_set("natural_log_exp_and_others")
                act.activation(f, f, ACT.Identity, bias=k.cols2[0:H, FOX_ROW:FOX_ROW + 1]).then_inc(k.act_a.sem, 1)
                act.wait_ge(*k.act_a.after(1))
                log_sigmoid_parts(k, act, None, None, f, lf[:], 1).then_inc(k.act_a.sem, 1)

            @block.gpsimd
            def _(pool):
                pool.tensor_copy(one[:], k.ident[0:H, 0:H].unsqueeze(2).to_broadcast([H, H, P]))

            @block.vector
            def _(dve):
                dve.tensor_scalar(q, q, HD ** -0.5, None, ALU.mult)
                dve.wait_ge(*k.act_a.after(2))
                k.dve.done(dve, dve.scalar_tensor_tensor(out=f, in0=f, scalar=0.0, in1=lf[:], op0=ALU.min,
                                                         op1=ALU.subtract))
                k.dve.done(dve, dve.tensor_scalar(f, f, -1.0, None, ALU.mult))
                dve.tensor_tensor_scan(c[:], k.ones[0:H, :], f, 0.0, ALU.mult, ALU.add)
        k.act_a.passed(2)

        def unit(h):
            r = slice(HD * (h % 2), HD * (h % 2) + HD)
            return dict(q=lambda t: q[r, h // 2, P * t:P * t + P], kT=key[r, h // 2, :],
                        v=lambda s: v[:, s, HD * h:HD * h + HD], bias=k.causal, extra=(one[:, h, :], c))

        softmax_attention(k, [[unit(h)] for h in range(H)],
                          lambda h: k.xn[:, :, HALF + HD * h:HALF + HD * h + HD])


def even_layer(k):
    with ExitStack() as ctx:
        def sb(name, shape):
            return ctx.enter_context(k.nc.sbuf_tensor(f"ev_{name}", shape, F32))

        qa, fa, qb, kb = (sb(n, [P, NH, S]) for n in ("qa", "fa", "qb", "kb"))
        ia, ga, vb = (sb(n, [P, TT, HALF]) for n in ("ia", "ga", "vb"))
        fb = sb("fb", [8, S])

        def feature(dst):
            return "feature", lambda m: dst[:, m, :], HALF

        def token(dst):
            return "token", lambda t: dst[:, t, :], HALF

        product(k, "ev_in", KD, [feature(qa), feature(fa), token(ia), token(ga), feature(qb), feature(kb),
                                       token(vb), ("feature", lambda m: fb[:], 8)])
        hgrn(k, qa[:], fa[:], ia, ga[:])
        fox(k, qb[:], kb, vb, fb[:])
        transpose_mix(k, range(KD))



def rg_lru(k, xr, gr):
    nc, ps, w = k.nc, k.ps, k.w
    with ExitStack() as ctx:
        def sb(name, shape):
            return ctx.enter_context(nc.sbuf_tensor(f"lru_{name}", shape, F32))

        pad = sb("padded", [P, NH, S + 3])
        xc, a, u, r = (sb(n, [P, NH, S]) for n in ("xc", "a", "u", "r"))
        ig, th, g3 = (sb(n, [P, NH, S]) for n in ("ig", "th", "g3"))
        wa, wx = sb("wa", [P, NH, HD]), sb("wx", [P, NH, HD])
        sp8, sl = sb("sp8", [P, NH]), sb("sl", [P, NH])
        col = {n: k.cols[:, PARAM_AT[n]:PARAM_AT[n] + 4] for n in
               ("od_conv_b", "od_gate_a_b", "od_gate_x_b", "od_lru_lambda")}
        cw = k.cols[:, PARAM_AT["od_conv_w"]:PARAM_AT["od_conv_w"] + 16]
        lam = col["od_lru_lambda"]
        with nc.Block() as block:
            @block.sync
            def _(sp):
                sp.dma_start(wa[:], w["od_gate_a_w"][0].rearrange("(t n) i j -> (n i) t j", n=2)).then_inc(k.loaded.sem, 16)
                sp.dma_start(wx[:], w["od_gate_x_w"][0].rearrange("(t n) i j -> (n i) t j", n=2)).then_inc(k.loaded.sem, 16)

            @block.gpsimd
            def _(pool):
                pool.memset(pad[:, :, 0:3], 0.0)
                pool.tensor_copy(pad[:, :, 3:S + 3], xr).then_inc(k.pool_a.sem, 1)

            @block.scalar
            def _(act):
                act.preload_act_table_set("natural_log_exp_and_others")
                log_sigmoid_parts(k, act, None, None, lam, sl[:], 0).then_inc(k.act_a.sem, 1)
                for n in range(2 * NH):
                    t, which = n // 2, n % 2
                    act.wait_ge(*k.pe_a.after(n + 1))
                    act.activation((ig if which else r)[:, t, :], ps[:, n, 0:S], ACT.Sigmoid,
                                   bias=(col["od_gate_x_b"] if which else col["od_gate_a_b"])[:, t:t + 1])\
                       .then_inc(k.act_b.sem, 1)
                act.wait_ge(*k.dve_b.after(1))
                act.wait_ge(*k.act_b.after(2 * NH))
                for t in range(NH):
                    act.activation(a[:, t, :], r[:, t, :], ACT.Exp, scale=sp8[:, t:t + 1]).then_inc(k.act_b.sem, 1)
                act.wait_ge(*k.dve_b.after(2))
                for t in range(NH):
                    act.activation(th[:, t, :], u[:, t, :], ACT.Tanh).then_inc(k.act_b.sem, 1)
                act.wait_ge(*k.pool_b.after(1))
                act.activation(g3[:], g3[:], ACT.Tanh, scale=0.7978845608028654).then_inc(k.act_b.sem, 1)
                act.wait_ge(*k.dve_b.after(3))
                act.activation(u[:], u[:], ACT.Sqrt).then_inc(k.act_b.sem, 1)
                act.wait_ge(*k.dve_b.after(4))
                act.activation(k.act_hi[:, 0:NH, :], g3[:], ACT.Copy).then_inc(k.act_b.sem, 1)

            @block.tensor
            def _(pe):
                pe.wait_ge(*k.loaded.after(32))
                pe.wait_ge(*k.dve_a.after(1))
                for n in range(2 * NH):
                    t, mat = n // 2, (wx if n % 2 else wa)
                    for b in range(2):
                        rows = slice(HD * b, HD * b + HD)
                        ins = pe.matmul(ps[rows, n, 0:S], mat[rows, t, :], xc[rows, t, :], start=True, stop=True)
                    ins.then_inc(k.pe_a.sem, 1)

            @block.vector
            def _(dve):
                dve.wait_ge(*k.pool_a.after(1))
                for t in range(NH):
                    ins = dve.tensor_scalar(xc[:, t, :], pad[:, t, 0:S], cw[:, t:t + 1], col["od_conv_b"][:, t:t + 1],
                                            ALU.mult, ALU.add)
                k.dve.done(dve, ins)
                for j in range(1, 4):
                    for t in range(NH):
                        ins = dve.scalar_tensor_tensor(out=xc[:, t, :], in0=pad[:, t, j:j + S],
                                                       scalar=cw[:, 4 * j + t:4 * j + t + 1], in1=xc[:, t, :],
                                                       op0=ALU.mult, op1=ALU.add)
                    k.dve.done(dve, ins)
                dve.sem_inc(k.dve_a.sem, 1)
                dve.wait_ge(*k.act_a.after(1))
                k.dve.done(dve, dve.scalar_tensor_tensor(out=sp8[:], in0=lam, scalar=0.0, in1=sl[:], op0=ALU.min,
                                                         op1=ALU.subtract))
                k.dve.done(dve, dve.tensor_scalar(sp8[:], sp8[:], 8.0, None, ALU.mult))
                dve.sem_inc(k.dve_b.sem, 1)
                k.dve.done(dve, dve.tensor_scalar(sl[:], sp8[:], -1.0, None, ALU.mult))
                dve.wait_ge(*k.act_b.after(2 * NH))
                for t in range(NH):
                    ins = dve.tensor_scalar(u[:, t, :], r[:, t, :], sl[:, t:t + 1], None, ALU.mult)
                ins.then_inc(k.dve_b.sem, 1)
                dve.wait_ge(*k.act_b.after(4 * NH))
                k.dve.done(dve, dve.tensor_tensor(u[:], a[:], a[:], ALU.mult))
                k.dve.done(dve, dve.scalar_tensor_tensor(out=u[:], in0=u[:], scalar=1.0, in1=th[:], op0=ALU.add,
                                                         op1=ALU.mult))
                dve.sem_inc(k.dve_b.sem, 1)
                k.dve.done(dve, dve.tensor_tensor(ig[:], ig[:], xc[:], ALU.mult))
                dve.wait_ge(*k.act_b.after(4 * NH + 2))
                k.dve.done(dve, dve.tensor_tensor(u[:], u[:], ig[:], ALU.mult))
                for t in range(NH):
                    ins = dve.tensor_tensor_scan(xc[:, t, :], a[:, t, :], u[:, t, :], 0.0, ALU.mult, ALU.add)
                k.dve.done(dve, ins)
                k.dve.done(dve, dve.scalar_tensor_tensor(out=g3[:], in0=g3[:], scalar=1.0, in1=gr, op0=ALU.add,
                                                         op1=ALU.mult))
                dve.scalar_tensor_tensor(out=g3[:], in0=g3[:], scalar=0.5, in1=xc[:], op0=ALU.mult,
                                         op1=ALU.mult).then_inc(k.dve_b.sem, 1)
                dve.wait_ge(*k.act_b.after(4 * NH + 3))
                dve.tensor_tensor(k.act_lo[:, 0:NH, :], g3[:], k.act_hi[:, 0:NH, :].bitcast(F32), ALU.subtract)

            @block.gpsimd
            def _(pool):
                k.pool.done(pool, pool.tensor_tensor(g3[:], gr, gr, ALU.mult))
                k.pool.done(pool, pool.tensor_scalar(g3[:], g3[:], 0.044715, 1.0, ALU.mult, ALU.add))
                pool.tensor_tensor(g3[:], g3[:], gr, ALU.mult).then_inc(k.pool_b.sem, 1)
        k.loaded.passed(32)
        k.pool_a.passed(1)
        k.pool_b.passed(1)
        k.pe_a.passed(2 * NH)
        k.act_a.passed(1)
        k.act_b.passed(4 * NH + 3)
        k.dve_a.passed(1)
        k.dve_b.passed(4)


def stick_breaking(k, q, key, v):
    nc, ps = k.nc, k.ps
    H = 8
    W = 3 * P
    with ExitStack() as ctx:
        def sb(name, shape):
            return ctx.enter_context(nc.sbuf_tensor(f"stick_{name}", shape, F32))

        minus, shut, tri = sb("minus", [P, W]), sb("shut", [P, W]), sb("tri", [P, P])
        la, lom, lw, wt = (sb(n, [P, 2, W]) for n in ("la", "lom", "lw", "wt"))
        with nc.Block() as block:
            @block.vector
            def _(dve):
                dve.tensor_scalar(q, q, HD ** -0.5, None, ALU.mult)

            @block.gpsimd
            def _(pool):
                pool.memset(minus[:], -1.0)
                pool.memset(shut[:], 0.0)
                k.pool.done(pool, pool.memset(tri[:], 1.0))
                for c in (0, 2 * P):
                    for buf, fill in ((minus, 0.0), (shut, NEG)):
                        pool.affine_select(out=buf[:, c:c + P], in_=buf[:, c:c + P], compare_op=ALU.is_gt, fill=fill,
                                           base=0, pattern=[[1, P]], channel_multiplier=-1)
                pool.affine_select(out=tri[:], in_=tri[:], compare_op=ALU.is_ge, fill=0.0, base=0,
                                   pattern=[[-1, P]], channel_multiplier=1)

        with nc.Block() as block:
            @block.tensor
            def _(pe):
                def rows(h):
                    return slice(HD * (h % 2), HD * (h % 2) + HD)

                def scores(h):
                    if h >= 4:
                        pe.wait_ge(*k.logits_ready.after(h - 3))
                    r, b = rows(h), ps[:, h % 4, :]
                    pe.matmul(b[:, 0:S], key[r, h // 2, 0:P], q[r, h // 2, :], start=True, stop=True)
                    pe.matmul(b[:, S:W], key[r, h // 2, P:S], q[r, h // 2, P:S], start=False, stop=True,
                              skip_group_check=True)\
                      .then_inc(k.scores_ready.sem, 1)

                def suffix(h):
                    pe.wait_ge(*k.dve_a.after(h + 1))
                    b, x = ps[:, h % 4, :], lom[:, h % 2, :]
                    pe.matmul(b[:, 0:S], tri[:], x[:, 0:S], start=False, stop=False, skip_group_check=True)
                    pe.matmul(b[:, P:S], k.ones[:, 0:P], x[:, S:W], start=False, stop=False, skip_group_check=True)
                    pe.matmul(b[:, S:W], tri[:], x[:, S:W], start=False, stop=True, skip_group_check=True)\
                      .then_inc(k.pe_a.sem, 1)

                def values(h):
                    pe.wait_ge(*k.probs_ready.after(h + 1))
                    if h >= 2:
                        pe.wait_ge(*k.heads_done.after(h - 1))
                    for t in range(TT):
                        for s in range(t + 1):
                            c = P * t if s == 0 else S
                            ins = pe.matmul(ps[:, 6 + h % 2, HD * t:HD * t + HD], wt[:, h % 2, c:c + P],
                                            v[:, s, HD * h:HD * h + HD], start=s == 0, stop=s == t)
                    ins.then_inc(k.heads_ready.sem, 1)

                for i in range(H + 2):
                    if i < H:
                        scores(i)
                    if 1 <= i <= H:
                        suffix(i - 1)
                    if i >= 2:
                        values(i - 2)

            @block.scalar
            def _(act):
                act.preload_act_table_set("natural_log_exp_and_others")

                def softplus_part(h):
                    act.wait_ge(*k.scores_ready.after(h + 1))
                    if h >= 2:
                        act.wait_ge(*k.dve_a.after(h - 1))
                    log_sigmoid_parts(k, act, None, None, ps[:, h % 4, 0:W], la[:, h % 2, :], 0)\
                        .then_inc(k.act_a.sem, 1)

                def weights(h):
                    act.wait_ge(*k.logits_ready.after(h + 1))
                    if h >= 2:
                        act.wait_ge(*k.heads_ready.after(h - 1))
                    act.activation(wt[:, h % 2, :], lw[:, h % 2, :], ACT.Exp).then_inc(k.probs_ready.sem, 1)

                for i in range(H + 1):
                    if i < H:
                        softplus_part(i)
                    if i >= 1:
                        weights(i - 1)

            @block.vector
            def _(dve):
                def break_part(h):
                    dve.wait_ge(*k.act_a.after(h + 1))
                    if h >= 2:
                        dve.wait_ge(*k.pe_a.after(h - 1))
                    x = lom[:, h % 2, :]
                    k.dve.done(dve, dve.scalar_tensor_tensor(out=x, in0=ps[:, h % 4, 0:W], scalar=0.0,
                                                             in1=la[:, h % 2, :], op0=ALU.max, op1=ALU.add))
                    dve.tensor_tensor(x, x, minus[:], ALU.mult).then_inc(k.dve_a.sem, 1)

                def close(h):
                    dve.wait_ge(*k.pe_a.after(h + 1))
                    if h >= 2:
                        dve.wait_ge(*k.probs_ready.after(h - 1))
                    dve.tensor_tensor(lw[:, h % 2, :], ps[:, h % 4, 0:W], shut[:], ALU.add)\
                       .then_inc(k.logits_ready.sem, 1)

                def finish(h):
                    dve.wait_ge(*k.heads_ready.after(h + 1))
                    dve.tensor_copy(k.xn[:, :, HALF + HD * h:HALF + HD * h + HD],
                                    ps[:, 6 + h % 2, 0:TT * HD].rearrange("p (t d) -> p t d", t=TT))\
                       .then_inc(k.heads_done.sem, 1)

                for i in range(H + 2):
                    if i < H:
                        break_part(i)
                    if 1 <= i <= H:
                        close(i - 1)
                    if i >= 2:
                        finish(i - 2)
        for mark in (k.scores_ready, k.dve_a, k.pe_a, k.act_a, k.probs_ready, k.heads_ready, k.heads_done,
                     k.logits_ready):
            mark.passed(H)


def odd_layer(k):
    with ExitStack() as ctx:
        def sb(name, shape):
            return ctx.enter_context(k.nc.sbuf_tensor(f"od_{name}", shape, F32))

        xr, gr, qd, kd = (sb(n, [P, NH, S]) for n in ("xr", "gr", "qd", "kd"))
        vd = sb("vd", [P, TT, HALF])

        def feature(dst):
            return "feature", lambda m: dst[:, m, :], HALF

        product(k, "od_in", KD, [feature(xr), feature(gr), feature(qd), feature(kd),
                                       ("token", lambda t: vd[:, t, :], HALF)])
        rg_lru(k, xr[:], gr[:])
        stick_breaking(k, qd[:], kd, vd)
        transpose_mix(k, range(NH, KD))


def first_block(k):
    norm(k)
    even_layer(k)
    out_product(k, "ev_out", KD)
    norm(k, residual=(ALPHA, 1.0), layer_norm=(0, 0))
    feed_forward(k, "ffn0")
    norm(k, residual=(ALPHA, 1.0), layer_norm=(0, 1))
    odd_layer(k)
    out_product(k, "od_out", KD)
    norm(k, residual=(ALPHA, 1.0), layer_norm=(1, 0))
    feed_forward(k, "ffn1")
    norm(k, residual=(ALPHA, 1.0), layer_norm=(1, 1), rms=PARAM_AT["ffn1_norm_2"])



DELTA = np.arange(3 * P) - (P - 1)
MASK_SETS = 5
BIAS_HEADS = 12 + 8 + 8


def bias_tables():
    n = np.maximum(DELTA, 0)
    nf = np.maximum(n, 1).astype(np.float32)
    large = 16 + (np.log(nf / np.float32(16)) / np.float32(np.log(2048 / 16)) * np.float32(16)).astype(np.int32)
    bucket = np.where(n < 16, n, np.minimum(large, 31))
    one = ((np.arange(32)[:, None] == bucket) & (DELTA >= 0)).astype(np.float32)
    causal = DELTA >= 0
    valid = np.stack([causal & (DELTA <= 128), causal & (DELTA % 4 == 0), causal & (DELTA % 16 == 0),
                      causal & (DELTA < 128), causal])
    return np.concatenate([one, np.where(valid, 0.0, NEG).astype(np.float32)])


def bias_sets():
    of = [0] * 4 + [1] * 4 + [2] * 4 + [3] * 8 + [4] * 8
    return (np.arange(MASK_SETS)[:, None] == np.array(of)).astype(np.float32)


SEL, BLK, CNEG, COK, COS, SIN, SMALL = 0, 128, 136, 168, 200, 232, 264


def small_tables():
    out = np.zeros((P, SMALL), np.float32)
    p = np.arange(P)
    out[0:16, SEL:SEL + P] = np.arange(16)[:, None] == p % 16
    out[:, BLK:BLK + 8] = p[:, None] // 16 == np.arange(8)
    end = np.arange(16) * CMP_STRIDE + CMP_LEN - 1
    inv = np.power(np.float32(10000.0), -np.arange(16, dtype=np.float32) / np.float32(16))
    for t in range(TT):
        ok = end[None, :] <= (P * t + p)[:, None]
        out[:, CNEG + 16 * t:CNEG + 16 * t + 16] = np.where(ok, 0.0, NEG)
        out[:, COK + 16 * t:COK + 16 * t + 16] = ok
        angle = (P * t + p).astype(np.float32)[:, None] * inv[None, :]
        out[:, COS + 16 * t:COS + 16 * t + 16] = np.cos(angle)
        out[:, SIN + 16 * t:SIN + 16 * t + 16] = np.sin(angle)
    return out


def bias_rows(k):
    nc, w = k.nc, k.w
    with ExitStack() as ctx:
        table = ctx.enter_context(nc.sbuf_tensor("bias_table", [32 + MASK_SETS, 3 * P], F32))
        rel = ctx.enter_context(nc.sbuf_tensor("bias_rel", [32 + MASK_SETS, BIAS_HEADS], F32))
        rows = ctx.enter_context(nc.sbuf_tensor("bias_rows", [BIAS_HEADS, 3 * P], F32))
        block = ctx.enter_context(nc.Block())

        @block.sync
        def _(sp):
            rb = w["rel_bias_2"]
            for dst, src in ((table[:], w["const_bias_tables"]), (rel[0:32, 0:12], rb[:, 0:12]),
                             (rel[0:32, 12:20], rb[:, 0:8]), (rel[0:32, 20:28], rb[:, 8:16]),
                             (rel[32:32 + MASK_SETS, :], w["const_bias_sets"])):
                sp.dma_start(dst, src).then_inc(k.loaded.sem, 16)
            sp.wait_ge(*k.dve_a.after(1))
            sp.dma_start(k.bias_dram, rows[:]).then_inc(k.stored.sem, 16)
            sp.wait_ge(*k.stored.after(16))

        @block.tensor
        def _(pe):
            pe.wait_ge(*k.loaded.after(80))
            pe.matmul(k.ps[0:BIAS_HEADS, 4, 0:3 * P], rel[:], table[:], start=True, stop=True).then_inc(k.pe_a.sem, 1)

        @block.vector
        def _(dve):
            dve.wait_ge(*k.pe_a.after(1))
            dve.tensor_copy(rows[:], k.ps[0:BIAS_HEADS, 4, 0:3 * P]).then_inc(k.dve_a.sem, 1)
    k.loaded.passed(80)
    k.stored.passed(16)
    k.dve_a.passed(1)
    k.pe_a.passed(1)


def load_bias(k, eng, dst, first, n):
    src = bass.AP(k.bias_dram.tensor, first * 3 * P, [[1, P], [3 * P, n], [1, S]])
    eng.dma_start(dst, src).then_inc(k.loaded.sem, 16)


def forwards(bias, head):
    x = bias[:, head, :]
    return bass.AP(x.tensor, x.offset + S - 1, [x.ap[0], [-1, S]])


def mla(k, z):
    nc, ps, w = k.nc, k.ps, k.w
    H, QK = MLA_H, MLA_QK
    with ExitStack() as ctx:
        def sb(name, shape):
            return ctx.enter_context(nc.sbuf_tensor(f"mla_{name}", shape, F32))

        qT, kT = sb("qT", [QK, H, S]), sb("kT", [QK, H, S])
        kv = sb("kv", [P, TT, H, P])
        with ExitStack() as inner:
            def sbi(name, shape):
                return inner.enter_context(nc.sbuf_tensor(f"mla_{name}", shape, F32))

            cn, cT = sbi("latent", [P, TT, 3 * P]), sbi("latent_T", [P, 3, S])
            qk, sq = sbi("qk", [P, 2, TT, H, QK]), sbi("sq", [P, 2, TT, H, QK])
            ss = sbi("ss", [P, 4])
            s2 = sbi("s2", [P, 2 * TT * H])
            gains = sbi("gains", [P, 2, QK])
            rot = sq[:].rearrange("p w t h d -> p (w t h d)")[:, 0:2 * 4 * TT * H * 16]\
                .rearrange("p (w i t h d) -> p w i t h d", w=2, i=4, t=TT, h=H)
            lat = ((0, 256), (256, 384))
            with nc.Block() as block:
                @block.sync
                def _(sp):
                    sp.dma_start(gains[:, 0], w["mla_q_norm_2"].to_broadcast([P, QK])).then_inc(k.loaded.sem, 16)
                    sp.dma_start(gains[:, 1], w["mla_k_norm_2"].to_broadcast([P, QK])).then_inc(k.loaded.sem, 16)

                @block.scalar
                def _(act):
                    for t in range(TT):
                        for i, (a, b) in enumerate(lat):
                            act.activation(cn[:, t, a:b], z[:, t, a:b], ACT.Square,
                                           scale=(b - a) ** -0.5, accum_out=ss[:, 2 * t + i:2 * t + i + 1])\
                               .then_inc(k.act_a.sem, 1)
                    act.wait_ge(*k.dve_a.after(1))
                    act.activation(ss[:], ss[:], ACT.Sqrt).then_inc(k.act_a.sem, 1)

                @block.vector
                def _(dve):
                    dve.wait_ge(*k.act_a.after(4))
                    dve.tensor_scalar(ss[:], ss[:], EPS_RMS, None, ALU.add).then_inc(k.dve_a.sem, 1)
                    dve.wait_ge(*k.act_a.after(5))
                    k.dve.done(dve, dve.reciprocal(ss[:], ss[:]))
                    for t in range(TT):
                        for i, (a, b) in enumerate(lat):
                            ins = dve.tensor_scalar(cn[:, t, a:b], z[:, t, a:b], ss[:, 2 * t + i:2 * t + i + 1], None,
                                                    ALU.mult)
                    ins.then_inc(k.dve_a.sem, 1)
                    for m in range(3):
                        dve.wait_ge(*k.pe_a.after(m + 1))
                        col = PARAM_AT["mla_q_a_norm_2"] + m
                        dve.tensor_scalar(cT[:, m, :], ps[:, m, 0:S], k.cols[:, col:col + 1], None, ALU.mult)\
                           .then_inc(k.dve_b.sem, 1)

                @block.tensor
                def _(pe):
                    pe.wait_ge(*k.dve_a.after(2))
                    for m in range(3):
                        for t in range(TT):
                            ins = pe.transpose(ps[:, m, P * t:P * t + P], cn[:, t, P * m:P * m + P], k.ident[:])
                        ins.then_inc(k.pe_a.sem, 1)
            k.act_a.passed(5)
            k.dve_a.passed(2)
            k.dve_b.passed(3)
            k.pe_a.passed(3)

            j = k.first["mla_b"]
            wq, wkv = k.slot_view(j, 2, 768), k.slot_view(j, 1, D, 1536)
            with nc.Block() as block:
                @block.tensor
                def _(pe):
                    pe.wait_ge(k.weights_in[j % SLOTS], k.arrived[j])
                    for t in range(TT):
                        for i, (a, b) in enumerate(((0, BANK), (BANK, 768))):
                            for m in range(2):
                                ins = pe.matmul(ps[:, 4 * t + i, 0:b - a], cT[:, m, P * t:P * t + P], wq[:, m, a:b],
                                                start=m == 0, stop=m == 1)
                        for i in range(2):
                            ins = pe.matmul(ps[:, 4 * t + 2 + i, :], cT[:, 2, P * t:P * t + P],
                                            wkv[:, 0, BANK * i:BANK * i + BANK], start=True, stop=True)
                        if t == 0:
                            ins.then_inc(k.pe_a.sem, 1)
                    ins.then_inc(k.weights_used, 1)

                @block.vector
                def _(dve):
                    for t in range(TT):
                        if t == 0:
                            dve.wait_ge(*k.pe_a.after(1))
                        else:
                            dve.wait_ge(k.weights_used, j + 1)
                        q = qk[:, 0, t].rearrange("p h d -> p (h d)")
                        dve.tensor_copy(q[:, 0:BANK], ps[:, 4 * t, :])
                        dve.tensor_copy(q[:, BANK:768], ps[:, 4 * t + 1, 0:256])

                @block.scalar
                def _(act):
                    for t in range(TT):
                        if t == 0:
                            act.wait_ge(*k.pe_a.after(1))
                        else:
                            act.wait_ge(k.weights_used, j + 1)
                        act.activation(kv[:, t], ps[:, 4 * t + 2:4 * t + 4, :].rearrange("p b (h d) -> p (b h) d", d=P),
                                       ACT.Copy)

                @block.gpsimd
                def _(pool):
                    for t in range(TT):
                        pool.tensor_copy(qk[:, 1, t, :, MLA_NOPE:QK], bc(z[:, t, 384:416], 1, H))

                @block.sync
                def _(sp):
                    k.load_weights(sp, j + 1 + SLOTS)
            k.pe_a.passed(1)

            def rotary(k, eng, steps, which):
                small = k.small
                x = qk[:, which, :, :, MLA_NOPE:QK]
                a, b = x[:, :, :, 0:16], x[:, :, :, 16:32]
                cos, sin = (bc(small[:, c:c + 32].rearrange("p (t d) -> p t d", t=TT), 2, H) for c in (COS, SIN))
                r = rot[:, which]
                for i, (u, v) in enumerate(((a, cos), (b, sin), (b, cos), (a, sin))):
                    ins = eng.tensor_tensor(r[:, i], u, v, ALU.mult)
                steps.done(eng, ins)
                eng.tensor_tensor(a, r[:, 0], r[:, 1], ALU.subtract)
                steps.done(eng, eng.tensor_tensor(b, r[:, 2], r[:, 3], ALU.add))

            with nc.Block() as block:
                @block.gpsimd
                def _(pool):
                    k.pool.done(pool, pool.tensor_copy(qk[:, 1, :, :, 0:MLA_NOPE], kv[:, :, :, 0:MLA_NOPE]))
                    pool.sem_inc(k.pool_a.sem, 1)
                    pool.wait_ge(*k.dve_a.after(2))
                    rotary(k, pool, k.pool, 1)
                    pool.sem_inc(k.pool_a.sem, 1)

                @block.scalar
                def _(act):
                    act.activation(sq[:, 0], qk[:, 0], ACT.Square, scale=QK ** -0.5).then_inc(k.act_a.sem, 1)
                    act.wait_ge(*k.pool_a.after(1))
                    act.activation(sq[:, 1], qk[:, 1], ACT.Square, scale=QK ** -0.5).then_inc(k.act_a.sem, 1)
                    act.wait_ge(*k.dve_a.after(1))
                    act.activation(s2[:], s2[:], ACT.Sqrt).then_inc(k.act_a.sem, 1)
                    for n in range(2 * H // 2):
                        which, m = n // (H // 2), n % (H // 2)
                        act.wait_ge(*k.pe_a.after(n + 1))
                        dst = (kT if which else qT)[:, 2 * m:2 * m + 2, :]
                        act.activation(dst, ps[0:QK, n, :].rearrange("p (h s) -> p h s", h=2), ACT.Copy,
                                       scale=1.0 if which else QK ** -0.5).then_inc(k.act_b.sem, 1)

                @block.vector
                def _(dve):
                    dve.wait_ge(*k.act_a.after(2))
                    k.dve.done(dve, dve.tensor_reduce(s2[:], sq[:].rearrange("p w t h d -> p (w t h) d"), AX.X, ALU.add))
                    dve.tensor_scalar(s2[:], s2[:], EPS_RMS, None, ALU.add).then_inc(k.dve_a.sem, 1)
                    dve.wait_ge(*k.act_a.after(3))
                    k.dve.done(dve, dve.reciprocal(s2[:], s2[:]))
                    dve.wait_ge(*k.loaded.after(32))
                    for which in (1, 0):
                        x = qk[:, which].rearrange("p t h d -> p (t h) d")
                        n = TT * H
                        k.dve.done(dve, dve.tensor_tensor(x, x, bc(s2[:, n * which:n * which + n], 2, QK), ALU.mult))
                        k.dve.done(dve, dve.tensor_tensor(x, x, bc(gains[:, which], 1, n), ALU.mult))
                        if which:
                            dve.sem_inc(k.dve_a.sem, 1)
                    rotary(k, dve, k.dve, 0)
                    dve.sem_inc(k.dve_b.sem, 1)

                @block.tensor
                def _(pe):
                    pe.wait_ge(*k.dve_b.after(1))
                    for n in range(2 * H // 2):
                        which, m = n // (H // 2), n % (H // 2)
                        if n == H // 2:
                            pe.wait_ge(*k.pool_a.after(2))
                        for h in (2 * m, 2 * m + 1):
                            for t in range(TT):
                                c = S * (h % 2) + P * t
                                ins = pe.transpose(ps[0:QK, n, c:c + P], qk[:, which, t, h, :], k.ident[:])
                        ins.then_inc(k.pe_a.sem, 1)
            k.loaded.passed(32)
            k.pool_a.passed(2)
            k.act_a.passed(3)
            k.act_b.passed(H)
            k.dve_a.passed(2)
            k.dve_b.passed(1)
            k.pe_a.passed(H)

        def unit(h):
            return dict(q=lambda t: qT[:, h, P * t:P * t + P], kT=kT[:, h, :],
                        v=lambda s: kv[:, s, h, MLA_NOPE:P], bias=k.causal)

        softmax_attention(k, [[unit(h)] for h in range(H)], lambda h: k.xn[:, :, HD * h:HD * h + HD])


def norm_and_flip(k, name, src, n_blocks, q_blocks, dst, tiles, loads=None, n_loads=0, gates=None):
    nc, ps = k.nc, k.ps
    B = n_blocks
    with ExitStack() as ctx:
        def sb(part, shape):
            return ctx.enter_context(nc.sbuf_tensor(f"{name}_{part}", shape, F32))

        sq = sb("sq", [P, TT, B, HD])
        nrm = sb("nrm", [P, TT, 2 * len(tiles), HD])
        rs = sb("rs", [P, TT, B])
        x = src.rearrange("p t (b d) -> p t b d", d=HD)
        runs = []
        for i, (a, b, gain) in enumerate(tiles):
            kind = (b - a, gain is None)
            if runs and runs[-1][2] == kind and a == runs[-1][1] + (2 if b > a else 1) * (i - runs[-1][0]):
                runs[-1][3] += 1
            else:
                runs.append([i, a, kind, 1])
        with nc.Block() as block:
            if loads:
                block.sync(loads)

            @block.scalar
            def _(act):
                for t in range(TT):
                    act.activation(sq[:, t], x[:, t], ACT.Square, scale=HD ** -0.5).then_inc(k.act_a.sem, 1)
                act.wait_ge(*k.dve_a.after(1))
                act.activation(rs[:], rs[:], ACT.Sqrt).then_inc(k.act_a.sem, 1)
                for i, (a, b, gain) in enumerate(tiles):
                    if gain is None:
                        continue
                    act.wait_ge(*k.pe_a.after(i + 1))
                    act.activation(dst[:, i, :], ps[:, i % 8, 0:S], ACT.Copy, scale=k.cols2[:, gain:gain + 1])\
                       .then_inc(k.act_b.sem, 1)
                if gates:
                    g = gates.rearrange("p t c -> p t c")
                    act.activation(g, g, ACT.Sigmoid)

            def spread(eng, t, run):
                i, a, (step, raw), n = run
                out = nrm[:, t, 2 * i:2 * i + 2 * n, :]
                wide = (2 if step else 1) * n
                src_x, r = x[:, t, a:a + wide, :], bc(rs[:, t, a:a + wide], 2, HD)
                if not step:
                    out = out.rearrange("p (b u) d -> p b u d", u=2)
                    src_x = bc(src_x, 2, 2)
                    r = bc(r, 2, 2)
                if raw:
                    return eng.tensor_copy(out, src_x)
                return eng.tensor_tensor(out, src_x, r, ALU.mult)

            @block.gpsimd
            def _(pool):
                ins = None
                for run in runs:
                    if run[2][1]:
                        for t in range(TT):
                            ins = spread(pool, t, run)
                if ins is not None:
                    ins.then_inc(k.pool_a.sem, 1)
                pool.wait_ge(*k.dve_a.after(2))
                for run in runs:
                    if not run[2][1]:
                        ins = spread(pool, 1, run)
                ins.then_inc(k.pool_b.sem, 1)

            @block.vector
            def _(dve):
                for t in range(TT):
                    dve.wait_ge(*k.act_a.after(t + 1))
                    ins = dve.tensor_reduce(rs[:, t], sq[:, t], AX.X, ALU.add)
                k.dve.done(dve, ins)
                dve.tensor_scalar(rs[:], rs[:], EPS_RMS, None, ALU.add).then_inc(k.dve_a.sem, 1)
                dve.wait_ge(*k.act_a.after(TT + 1))
                k.dve.done(dve, dve.reciprocal(rs[:], rs[:]))
                for a, b in q_blocks:
                    ins = dve.tensor_scalar(rs[:, :, a:b], rs[:, :, a:b], HD ** -0.5, None, ALU.mult)
                k.dve.done(dve, ins)
                dve.sem_inc(k.dve_a.sem, 1)
                for run in runs:
                    if not run[2][1]:
                        ins = spread(dve, 0, run)
                ins.then_inc(k.dve_a.sem, 1)
                for i, (a, b, gain) in enumerate(tiles):
                    if gain is None:
                        dve.wait_ge(*k.pe_a.after(i + 1))
                        dve.tensor_copy(dst[0:HD, i, :], ps[0:HD, i % 8, 0:S])
                        dve.tensor_copy(dst[HD:P, i, 0:S - 1], ps[HD:P, i % 8, 1:S]).then_inc(k.dve_b.sem, 1)

            @block.tensor
            def _(pe):
                pe.wait_ge(*k.dve_a.after(3))
                pe.wait_ge(*k.pool_b.after(1))
                raw = [i for i, x in enumerate(tiles) if x[2] is None]
                for i in range(len(tiles)):
                    if raw and i == raw[0]:
                        pe.wait_ge(*k.pool_a.after(1))
                    if i >= 8:
                        if i - 8 in raw:
                            pe.wait_ge(*k.dve_b.after(raw.index(i - 8) + 1))
                        else:
                            pe.wait_ge(*k.act_b.after(i - 8 + 1 - sum(j < i - 8 for j in raw)))
                    for t in range(TT):
                        ins = pe.transpose(ps[:, i % 8, P * t:P * t + P],
                                           nrm[:, t, 2 * i:2 * i + 2, :].rearrange("p b d -> p (b d)"), k.ident[:])
                    ins.then_inc(k.pe_a.sem, 1)
        raw = sum(x[2] is None for x in tiles)
        k.loaded.passed(n_loads)
        k.act_a.passed(TT + 1)
        k.act_b.passed(len(tiles) - raw)
        k.dve_a.passed(3)
        k.dve_b.passed(raw)
        k.pe_a.passed(len(tiles))
        k.pool_a.passed(bool(raw))
        k.pool_b.passed(1)


def dilated(k, z, bias):
    with ExitStack() as ctx:
        qkT = ctx.enter_context(k.nc.sbuf_tensor("dil_qkT", [P, 12, S], F32))
        at = 416
        gq, gk = GAIN_AT["dil_q_norm_2"], GAIN_AT["dil_k_norm_2"]
        tiles = [(2 * i, 2 * i + 1, gq if i < 6 else gk) for i in range(12)]
        norm_and_flip(k, "dil", z[:, :, at:at + 24 * HD], 24, [(0, 12)], qkT, tiles)

        def unit(i):
            r = slice(HD * (i % 2), HD * (i % 2) + HD)
            v0 = at + HD * (24 + i)
            return dict(q=lambda t: qkT[r, i // 2, P * t:P * t + P], kT=qkT[r, 6 + i // 2, :],
                        v=lambda s: z[:, s, v0:v0 + HD], bias=forwards(bias, i))

        softmax_attention(k, [[unit(4 * g + h) for g in range(3)] for h in range(4)],
                          lambda h: k.xn[:, :, HALF + HD * h:HALF + HD * h + HD])


def latent_layer(k):
    with ExitStack() as ctx:
        z = ctx.enter_context(k.nc.sbuf_tensor("ab_z", [P, TT, 2720], F32))
        bias = ctx.enter_context(k.nc.sbuf_tensor("ab_bias", [P, 12, S], F32))
        with k.nc.Block() as block:
            @block.scalar
            def _(act):
                load_bias(k, act, bias[:], 0, 12)
                act.wait_ge(*k.loaded.after(16))
        k.loaded.passed(16)
        pieces = []
        for c in range(0, 2720, BANK):
            n = min(BANK, 2720 - c)
            pieces.append(("token", lambda t, c=c, n=n: z[:, t, c:c + n], n))
        product(k, "ab_in", KD, pieces)
        mla(k, z)
        dilated(k, z, bias)
        transpose_mix(k, range(6))



def compressed(k, z, zT, q_tile, gate):
    nc, ps, w = k.nc, k.ps, k.w
    G, H, C, GC = 2, 8, N_CMP, 2 * N_CMP
    small = k.small
    j = k.first["cmp_w1"]
    with ExitStack() as ctx:
        def sb(name, shape):
            return ctx.enter_context(nc.sbuf_tensor(f"cmp_{name}", shape, F32))

        w2 = sb("w2", [P, 2, HD])
        hb, hid = sb("hidden_bias", [P, 2]), sb("hidden", [P, 2, GC])
        kc, ksq, kss = sb("kc", [GC, 2, HD]), sb("ksq", [GC, HD]), sb("kss", [GC, 1])
        kcT, vc, vblk = sb("kcT", [P, GC]), sb("vc", [C, G, HD]), sb("vblk", [P, H, HD])
        lg, pr = sb("lg", [P, TT, H, C]), sb("pr", [P, TT, H, 16])
        mx, sm = sb("mx", [P, TT, H]), sb("sm", [P, TT, H])
        prT = sb("prT", [P, TT, P])
        w1 = [k.slot_view(j, 16, P, 2048 * i) for i in range(2)]
        with nc.Block() as block:
            @block.sync
            def _(sp):
                sp.dma_start(w2[:], w["nsa_cmp_w2_2"][0].rearrange("a p d -> p a d")).then_inc(k.loaded.sem, 16)
                k.load_weights(sp, j + 1 + SLOTS)

            @block.gpsimd
            def _(pool):
                pool.memset(pr[:], 0.0).then_inc(k.pool_a.sem, 1)

            @block.tensor
            def _(pe):
                pe.wait_ge(k.weights_in[j % SLOTS], k.arrived[j])
                for i in range(2):
                    rhs = [zT[:, 14 + 2 * i:16 + 2 * i, 2 * l:2 * l + CMP_STRIDE * (C - 1) + 1:CMP_STRIDE] for l in range(16)]
                    for l in range(16):
                        pe.matmul(ps[:, i, 0:GC].rearrange("p (g c) -> p g c", g=G), w1[i][:, l, :], rhs[l],
                                  start=l == 0, stop=l == 15)
                    for l in range(16):
                        c = PARAM_AT["nsa_cmp_pos_2"] + 16 * i + l
                        ins = pe.matmul(ps[:, 2 + i, 0:1], w1[i][:, l, :], k.cols[:, c:c + 1], start=l == 0, stop=l == 15)
                    if i == 0:
                        ins.then_inc(k.pe_a.sem, 1)
                ins.then_inc(k.weights_used, 1)
                pe.wait_ge(*k.act_a.after(2))
                pe.wait_ge(*k.loaded.after(16))
                pe.matmul(ps[0:GC, 4, 0:HD], hid[:, 0, :], w2[:, 0, :], start=True, stop=True).then_inc(k.pe_a.sem, 1)
                for g in range(G):
                    ins = pe.matmul(ps[0:C, 5, HD * g:HD * g + HD], hid[:, 1, C * g:C * g + C], w2[:, 1, :],
                                    start=True, stop=True)
                ins.then_inc(k.pe_a.sem, 1)
                pe.wait_ge(*k.dve_b.after(1))
                pe.matmul(ps[:, 6, 0:P], small[0:C, SEL:SEL + P], vc[:].rearrange("c g d -> c (g d)"),
                          start=True, stop=True).then_inc(k.pe_a.sem, 1)
                pe.wait_ge(*k.dve_b.after(2))
                pe.transpose(ps[:, 7, 0:GC], kc[:].rearrange("c u d -> c (u d)"), k.ident[0:GC, 0:GC])\
                  .then_inc(k.pe_a.sem, 1)
                pe.wait_ge(*k.act_b.after(1))
                for t in range(TT):
                    for h in range(H):
                        r = slice(HD * (h % 2), HD * (h % 2) + HD)
                        c = (t * H + h) // 2 * 16
                        g = h // (H // G)
                        ins = pe.matmul(ps[:, h % 2, c:c + C], zT[r, q_tile + h // 2, P * t:P * t + P],
                                        kcT[r, C * g:C * g + C], start=True, stop=True)
                ins.then_inc(k.pe_a.sem, 1)
                pe.wait_ge(*k.dve_b.after(3))
                for t in range(TT):
                    ins = pe.transpose(ps[:, 4, P * t:P * t + P], pr[:, t].rearrange("p h c -> p (h c)"), k.ident[:])
                ins.then_inc(k.pe_a.sem, 1)
                pe.wait_ge(*k.dve_b.after(4))
                for t in range(TT):
                    ins = pe.matmul(ps[:, 2 + t, :], prT[:, t, :], vblk[:].rearrange("p h d -> p (h d)"),
                                    start=True, stop=True)
                ins.then_inc(k.pe_a.sem, 1)

            @block.scalar
            def _(act):
                for i in range(2):
                    act.wait_ge(*k.dve_a.after(i + 1))
                    act.activation(hid[:, i, :], ps[:, i, 0:GC], ACT.Gelu_apprx_tanh, bias=hb[:, i:i + 1])\
                       .then_inc(k.act_a.sem, 1)
                act.wait_ge(*k.dve_a.after(3))
                act.activation(kss[:], kss[:], ACT.Sqrt).then_inc(k.act_a.sem, 1)
                act.wait_ge(*k.pe_a.after(5))
                gain = GAIN_AT["nsa_k0"]
                act.activation(kcT[:], ps[:, 7, 0:GC], ACT.Copy, scale=k.cols2[:, gain:gain + 1]).then_inc(k.act_b.sem, 1)
                act.wait_ge(*k.dve_a.after(4))
                act.activation(lg[:], lg[:], ACT.Exp).then_inc(k.act_a.sem, 1)

            @block.vector
            def _(dve):
                for i in range(2):
                    if i == 0:
                        dve.wait_ge(*k.pe_a.after(1))
                    else:
                        dve.wait_ge(k.weights_used, j + 1)
                    dve.tensor_copy(hb[:, i:i + 1], ps[:, 2 + i, 0:1]).then_inc(k.dve_a.sem, 1)
                dve.wait_ge(*k.pe_a.after(2))
                key = ps[0:GC, 4, 0:HD]
                k.dve.done(dve, dve.tensor_copy(kc[:, 0, :], key))
                k.dve.done(dve, dve.scalar_tensor_tensor(out=ksq[:], in0=kc[:, 0, :], scalar=1.0 / HD, in1=kc[:, 0, :],
                                                         op0=ALU.mult, op1=ALU.mult, accum_out=kss[:]))
                dve.tensor_scalar(kss[:], kss[:], EPS_RMS, None, ALU.add).then_inc(k.dve_a.sem, 1)
                dve.wait_ge(*k.pe_a.after(3))
                dve.tensor_copy(vc[:], ps[0:C, 5, 0:G * HD].rearrange("c (g d) -> c g d", g=G)).then_inc(k.dve_b.sem, 1)
                dve.wait_ge(*k.act_a.after(3))
                k.dve.done(dve, dve.reciprocal(kss[:], kss[:]))
                for u in range(2):
                    ins = dve.tensor_scalar(kc[:, u, :], key, kss[:, 0:1], None, ALU.mult)
                ins.then_inc(k.dve_b.sem, 1)
                dve.wait_ge(*k.pe_a.after(4))
                for g in range(G):
                    n = H // G
                    rep = bc(ps[:, 6, HD * g:HD * g + HD], 1, n)
                    dve.tensor_tensor(vblk[:, n * g:n * g + n, :], rep,
                                      bc(small[:, BLK + n * g:BLK + n * g + n], 2, HD), ALU.mult)
                dve.wait_ge(*k.pe_a.after(6))
                dve.wait_ge(*k.pool_a.after(1))
                neg, ok = (small[:, c:c + 32].rearrange("p (t c) -> p t c", t=TT)[:, :, 0:C] for c in (CNEG, COK))
                flat = lg[:].rearrange("p t h c -> p (t h) c")
                mxf, smf = mx[:].rearrange("p t h -> p (t h)"), sm[:].rearrange("p t h -> p (t h)")
                for b in range(2):
                    logits = ps[:, b, 0:P].rearrange("p (t h c) -> p t h c", t=TT, h=H // 2)[:, :, :, 0:C]
                    ins = dve.tensor_tensor(lg[:, :, b:H:2, :], logits, bc(neg, 2, H // 2), ALU.add)
                k.dve.done(dve, ins)
                k.dve.done(dve, dve.tensor_reduce(mxf, flat, AX.X, ALU.max))
                dve.tensor_tensor(flat, flat, bc(mxf, 2, C), ALU.subtract).then_inc(k.dve_a.sem, 1)
                dve.wait_ge(*k.act_a.after(4))
                k.dve.done(dve, dve.tensor_tensor(lg[:], lg[:], bc(ok, 2, H), ALU.mult))
                k.dve.done(dve, dve.tensor_reduce(smf, flat, AX.X, ALU.add))
                k.dve.done(dve, dve.tensor_scalar(smf, smf, 1e-30, None, ALU.max))
                k.dve.done(dve, dve.reciprocal(smf, smf))
                k.dve.done(dve, dve.tensor_tensor(sm[:], sm[:], gate, ALU.mult))
                dve.tensor_tensor(pr[:, :, :, 0:C].rearrange("p t h c -> p (t h) c"), flat, bc(smf, 2, C), ALU.mult)\
                   .then_inc(k.dve_b.sem, 1)
                dve.wait_ge(*k.pe_a.after(7))
                dve.tensor_copy(prT[:], ps[:, 4, 0:S].rearrange("p (t n) -> p t n", t=TT)).then_inc(k.dve_b.sem, 1)
                dve.wait_ge(*k.pe_a.after(8))
                dve.tensor_copy(k.xn[:, :, HALF:D], ps[:, 2:4, :])
    k.loaded.passed(16)
    k.pool_a.passed(1)
    k.pe_a.passed(8)
    k.act_a.passed(4)
    k.act_b.passed(1)
    k.dve_a.passed(4)
    k.dve_b.passed(4)


def sparse_layer(k):
    nc, w = k.nc, k.w
    assert S // 64 <= 16
    with ExitStack() as ctx:
        def sb(name, shape):
            return ctx.enter_context(nc.sbuf_tensor(f"cd_{name}", shape, F32))

        z = sb("z", [P, TT, 2072])
        bias = sb("bias", [P, 16, S])
        sink = sb("sink", [P, 2, 8])
        pieces = []
        for c in range(0, 2072, BANK):
            n = min(BANK, 2072 - c)
            pieces.append(("token", lambda t, c=c, n=n: z[:, t, c:c + n], n))
        with nc.Block() as block:
            @block.scalar
            def _(act):
                load_bias(k, act, bias[:], 12, 16)
                act.dma_start(sink[:, 0, :], w["swa_sinks_2"].to_broadcast([P, 8])).then_inc(k.loaded.sem, 16)
                act.wait_ge(*k.loaded.after(32))

            @block.vector
            def _(dve):
                dve.wait_ge(*k.loaded.after(32))
                dve.tensor_scalar(sink[:, 1, :], sink[:, 0, :], -1.0, None, ALU.mult)
        k.loaded.passed(32)
        product(k, "cd_in", KD, pieces)
        zT = sb("zT", [P, 18, S])
        g = GAIN_AT
        tiles = ([(2 * i, 2 * i + 1, g["swa_q_norm_2"]) for i in range(4)]
                 + [(8 + i, 8 + i, g["swa_k_norm_2"]) for i in range(2)]
                 + [(12 + 2 * i, 13 + 2 * i, g["nsa_q_norm_2"]) for i in range(4)]
                 + [(24 + i, 24 + i, g["nsa_k1"]) for i in range(2)]
                 + [(28 + i, 28 + i, g["nsa_k2"]) for i in range(2)]
                 + [(20 + i, 20 + i, None) for i in range(4)])
        gates = z[:, :, 2048:2072]
        norm_and_flip(k, "cd", z[:, :, 0:2048], 32, [(0, 8), (12, 20)], zT, tiles, gates=gates)
        G4 = 4

        def unit(h, q_tile, k_tile, v_block, bias_at):
            r = slice(HD * (h % 2), HD * (h % 2) + HD)
            v0 = HD * (v_block + h // G4)
            return dict(q=lambda t: zT[r, q_tile + h // 2, P * t:P * t + P], kT=zT[r, k_tile + h // G4, :],
                        v=lambda s: z[:, s, v0:v0 + HD], bias=forwards(bias, bias_at + h))

        softmax_attention(k, [[unit(h, 0, 4, 10, 0)] for h in range(8)], lambda h: k.xn[:, :, HD * h:HD * h + HD],
                          sink=lambda h: (sink[:, 0, h:h + 1], sink[:, 1, h:h + 1]))

        def gate(branch):
            return gates.rearrange("p t (h b) -> p t h b", b=3)[:, :, :, branch]

        compressed(k, z, zT, 6, gate(0))
        for branch, k_tile, v_block in ((1, 10, 26), (2, 12, 30)):
            softmax_attention(k, [[unit(h, 6, k_tile, v_block, 8)] for h in range(8)],
                              lambda h: k.xn[:, :, HALF + HD * h:HALF + HD * h + HD],
                              gate=lambda h, b=branch: gate(b)[:, :, h], add=True)
        transpose_mix(k, range(KD))


def second_block(k):
    for layer in range(2):
        feed_forward(k, f"ffn{2 + 2 * layer}")
        norm(k, residual=(1.0, 0.5), rms=PARAM_AT["mix_norm_2"] + KD * layer)
        if layer == 0:
            latent_layer(k)
            out_product(k, "ab_out", 6)
        else:
            sparse_layer(k)
            out_product(k, "cd_out", KD)
        norm(k, residual=(1.0, 1.0), rms=PARAM_AT["ffn2_norm_2"] + KD * layer)
        feed_forward(k, f"ffn{3 + 2 * layer}")
        if layer == 0:
            norm(k, residual=(1.0, 0.5), rms=PARAM_AT["ffn1_norm_2"] + KD)
    store_result(k)


def program(nc, w, out):
    k = Core(nc, w, out)
    constants(k)
    bias_rows(k)
    first_block(k)
    second_block(k)



def kernel(**inputs):
    from concourse import bacc
    from concourse.bass_utils import run_bass_kernel_spmd

    nc = bacc.Bacc("TRN2", target_bir_lowering=False, num_devices=1)
    tables = {"const_hgrn_masks": hgrn_masks(), "const_bias_tables": bias_tables(),
              "const_bias_sets": bias_sets(), "const_small": small_tables()}
    arrays, w = {}, {}
    for name, a in {**inputs, **tables}.items():
        a = np.ascontiguousarray(a)
        arrays[f"in_{name}"] = a
        w[name] = nc.dram_tensor(f"in_{name}", a.shape, mybir.dt.from_np(a.dtype), kind="ExternalInput").ap()
    out = nc.dram_tensor("out_0", (1, S, D), F32, kind="ExternalOutput").ap()
    program(nc, w, out)
    result = run_bass_kernel_spmd(nc, [arrays], core_ids=[0])
    return result.results[0]["out_0"]
```

```python
from contextlib import ExitStack

import numpy as np

import concourse.bass as bass
from concourse import mybir

F32 = mybir.dt.float32
F32R = mybir.dt.float32r
ALU = mybir.AluOpType
ACT = mybir.ActivationFunctionType
AX = mybir.AxisListType

P = 128
S = 256
TT = S // P
D = 1024
KD = D // P
HALF = D // 2
NH = HALF // P
D_FF = 2816
FT = D_FF // P
ALPHA = 4 ** 0.25
EPS_LN = 1e-5
EPS_RMS = 1e-6
NEG = -1e30
FLT_MAX = 3.0e38
SLOTS = 4
WARM = (12, 8, 26, 0)
SLOT = 4096
BANK = 512

HGRN_HEADS, HGRN_DIM = 4, 128
HD = 64
MLA_H, MLA_NOPE, MLA_ROPE = 8, 64, 32
MLA_QK = MLA_NOPE + MLA_ROPE
N_CMP, CMP_STRIDE, CMP_LEN = 15, 16, 32


class Mark:

    def __init__(self, nc, name):
        self.sem = nc.alloc_semaphore(name)
        self.at = 0

    def after(self, n):
        return self.sem, self.at + n

    def passed(self, n):
        self.at += n


class Steps:

    def __init__(self, nc, name):
        self.sem = nc.alloc_semaphore(name)
        self.n = 0

    def done(self, eng, ins):
        self.n += 1
        ins.then_inc(self.sem, 1)
        eng.wait_ge(self.sem, self.n)


def bc(ap, axis, n):
    a = ap.unsqueeze(axis)
    shape = list(a.shape)
    shape[axis] = n
    return a.to_broadcast(shape)


class Core:

    def __init__(self, nc, w, out):
        self.nc, self.w, self.out = nc, w, out
        sb = nc.alloc_sbuf_tensor
        self.ident = sb("ident", [P, P], F32)
        self.ones = sb("ones", [P, S], F32)
        self.causal = sb("causal", [P, S], F32)
        self.slot = sb("weight_slots", [P, SLOTS, SLOT], F32)
        self.x = sb("residual", [P, TT, D], F32)
        self.xn = sb("normed", [P, TT, D], F32)
        self.act_hi = sb("act_hi", [P, KD, S], F32R)
        self.act_lo = sb("act_lo", [P, KD, S], F32R)
        self.gb = sb("ln_gain_bias", [P, 2, D], F32)
        self.cols = sb("param_cols", [P, P], F32)
        self.cols2 = sb("param_cols2", [P, P], F32)
        self.st = sb("stats", [P, 64], F32)
        self.small = sb("small_tables", [P, w["const_small"].shape[1]], F32)
        self.bias_dram = nc.dram_tensor("bias_rows_dram", (28, 3 * P), F32).ap()
        self.ps = nc.alloc_psum_tensor("banks", [P, 8, BANK], F32)
        self.diag = sb("diag_rrms", [P, TT, P], F32)
        self.whole = self.xn[:].rearrange("p t (q s) -> p (t q) s", s=S)
        self.eps = sb("eps", [P, 2], F32)
        self.fox_bias = sb("fox_bias", [8, 1], F32)
        self.unfinished = None
        self.loaded = Mark(nc, "loaded")
        self.x_loaded = Mark(nc, "x_loaded")
        self.params_loaded = Mark(nc, "params_loaded")
        self.bias_stored = Mark(nc, "bias_stored")
        self.bias_loaded = Mark(nc, "bias_loaded")
        self.summed = Mark(nc, "summed")
        self.whole_ready = Mark(nc, "whole_ready")
        self.split_ready = Mark(nc, "split_ready")
        self.early_split = Mark(nc, "early_split")
        self.split_by_pool = Mark(nc, "split_by_pool")
        self.consts_ready = Mark(nc, "consts_ready")
        self.gate_up_hi = Mark(nc, "gate_up_hi")
        self.gate_up_split = Mark(nc, "gate_up_split")
        self.down_hi = Mark(nc, "down_hi")
        self.down_split = Mark(nc, "down_split")
        self.hidden_hi = Mark(nc, "hidden_hi")
        self.hidden_split = Mark(nc, "hidden_split")
        self.part_hi = Mark(nc, "part_hi")
        self.part_split = Mark(nc, "part_split")
        self.part_used = Mark(nc, "part_used")
        self.gate_up_ready = Mark(nc, "gate_up_ready")
        self.silu_ready = Mark(nc, "silu_ready")
        self.hidden_ready = Mark(nc, "hidden_ready")
        self.down_used = Mark(nc, "down_used")
        self.product_ready = Mark(nc, "product_ready")
        self.product_copied = Mark(nc, "product_copied")
        self.acc_ready = Mark(nc, "acc_ready")
        self.scores_ready = Mark(nc, "scores_ready")
        self.logits_ready = Mark(nc, "logits_ready")
        self.probs_ready = Mark(nc, "probs_ready")
        self.probs_flipped = Mark(nc, "probs_flipped")
        self.probs_T_ready = Mark(nc, "probs_T_ready")
        self.heads_ready = Mark(nc, "heads_ready")
        self.heads_done = Mark(nc, "heads_done")
        self.stats_ready = Mark(nc, "stats_ready")
        self.root_ready = Mark(nc, "root_ready")
        self.normed_ready = Mark(nc, "normed_ready")
        self.flipped = Mark(nc, "flipped")
        self.flip_copied = Mark(nc, "flip_copied")
        self.stored = Mark(nc, "stored")
        self.pe_a = Mark(nc, "pe_a")
        self.pe_b = Mark(nc, "pe_b")
        self.pe_c = Mark(nc, "pe_c")
        self.act_a = Mark(nc, "act_a")
        self.act_b = Mark(nc, "act_b")
        self.act_c = Mark(nc, "act_c")
        self.dve_a = Mark(nc, "dve_a")
        self.dve_b = Mark(nc, "dve_b")
        self.dve_c = Mark(nc, "dve_c")
        self.pool_a = Mark(nc, "pool_a")
        self.pool_b = Mark(nc, "pool_b")
        self.weights_in = [nc.alloc_semaphore(f"weights_in{i}") for i in range(SLOTS)]
        self.weights_used = nc.alloc_semaphore("weights_used")
        self.dve = Steps(nc, "dve_steps")
        self.act = Steps(nc, "act_steps")
        self.pool = Steps(nc, "pool_steps")
        self.n_names = 0
        self.items, self.arrived, self.first, self.issued = [], [], {}, 0
        self.plan_weights()


    def slot_view(self, j, k, n, at=0):
        return self.slot[:, j % SLOTS, at:at + k * n].rearrange("p (k n) -> p k n", k=k)

    def plan_weights(self):
        w = self.w

        def add(*pieces):
            j = len(self.items)
            self.items.append([(self.slot_view(j, k, n, at), src) for src, k, n, at in pieces])
            before = self.arrived[j - SLOTS] if j >= SLOTS else 0
            self.arrived.append(before + 16 * len(pieces))

        def columns(name, mat, k, width):
            self.first[name] = len(self.items)
            for c in range(0, width, BANK):
                n = min(BANK, width - c)
                add((mat[:, c:c + n].rearrange("(k p) n -> p k n", p=P), k, n, 0))

        def ffn(name, gate, up, down):
            self.first[name] = len(self.items)
            for c in range(FT // 2):
                h = slice(256 * c, 256 * c + 256)
                add((gate[:, h].rearrange("(k p) n -> p k n", p=P), KD, 256, 0),
                    (up[:, h].rearrange("(k p) n -> p k n", p=P), KD, 256, 2048))
                add((down[h, 0:HALF].rearrange("(k p) n -> p k n", p=P), 2, HALF, 0),
                    (down[h, HALF:D].rearrange("(k p) n -> p k n", p=P), 2, HALF, 1024))

        w13, w2 = w["ffn_w13"], w["ffn_w2"]
        columns("ev_in", w["ev_w_in"][0], KD, 3592)
        columns("ev_out", w["ev_w_out"][0], KD, D)
        ffn("ffn0", w13[0, :, 0:D_FF], w13[0, :, D_FF:2 * D_FF], w2[0])
        columns("od_in", w["od_w_in"][0], KD, 2560)
        columns("od_out", w["od_w_out"][0], KD, D)
        ffn("ffn1", w13[1, :, 0:D_FF], w13[1, :, D_FF:2 * D_FF], w2[1])
        for layer in range(2):
            ffn(f"ffn{2 + 2 * layer}", w["ffn1_w_gate_2"][layer], w["ffn1_w_up_2"][layer],
                w["ffn1_w_down_2"][layer])
            if layer == 0:
                columns("ab_in", w["ab_w_in_2"][0], KD, 2720)
                self.first["mla_b"] = len(self.items)
                add((w["mla_w_q_b_2"][0].rearrange("(k p) n -> p k n", p=P), 2, 768, 0),
                    (w["mla_w_kv_b_2"][0].rearrange("(k p) n -> p k n", p=P), 1, D, 1536))
                columns("ab_out", w["ab_w_out_2"][0], 6, D)
            else:
                columns("cd_in", w["cd_w_in_2"][0], KD, 2072)
                self.first["cmp_w1"] = len(self.items)
                add((w["nsa_cmp_w1_2"][0, 0].rearrange("(l p) n -> p l n", p=P), 16, P, 0),
                    (w["nsa_cmp_w1_2"][0, 1].rearrange("(l p) n -> p l n", p=P), 16, P, 2048))
                columns("cd_out", w["cd_w_out_2"][0], KD, D)
            ffn(f"ffn{3 + 2 * layer}", w["ffn2_w_gate_2"][layer], w["ffn2_w_up_2"][layer],
                w["ffn2_w_down_2"][layer])

    def uid(self):
        self.n_names += 1
        return self.n_names

    def load_weights(self, sp, until):
        while self.issued < min(until, len(self.items)):
            j = self.issued
            if j >= SLOTS:
                sp.wait_ge(self.weights_used, j - SLOTS + 1)
            for dst, src in self.items[j]:
                sp.dma_start(dst, src).then_inc(self.weights_in[j % SLOTS], 16)
            self.issued += 1



PARAM_ROWS = [("hgrn_lb", 12), ("od_conv_w", 16), ("od_conv_b", 4), ("od_gate_a_b", 4), ("od_gate_x_b", 4),
              ("od_lru_lambda", 4), ("ffn1_norm_2", 16), ("mix_norm_2", 16), ("ffn2_norm_2", 16),
              ("mla_q_a_norm_2", 2), ("mla_kv_a_norm_2", 1), ("nsa_cmp_pos_2", 32)]
PARAM_AT = {}
_n = 0
for _name, _rows in PARAM_ROWS:
    PARAM_AT[_name] = _n
    _n += _rows
N_ROWS = _n
HEAD_GAINS = ["dil_q_norm_2", "dil_k_norm_2", "swa_q_norm_2", "swa_k_norm_2", "nsa_q_norm_2",
              "nsa_k0", "nsa_k1", "nsa_k2"]
GAIN_AT = {name: i for i, name in enumerate(HEAD_GAINS)}
LN_AT = {"ln_g": len(HEAD_GAINS), "ln_b": len(HEAD_GAINS) + 4 * KD}
N_ROWS2 = LN_AT["ln_b"] + 4 * KD


def flat_rows(ap):
    s = ap.shape
    if len(s) == 1:
        return ap.rearrange("(r c) -> r c", c=P)
    if len(s) == 2:
        return ap.rearrange("a (r c) -> (a r) c", c=P)
    if len(s) == 3:
        return ap.rearrange("a b (r c) -> (a b r) c", c=P)
    return ap.rearrange("a b (r l) c -> (a b r) (l c)", l=2)


def begin(k):
    nc, w, ps = k.nc, k.w, k.ps
    with nc.Block() as block:
        @block.sync
        def _(sp):
            for t in range(TT):
                sp.dma_start(k.x[:, t], w["x"][0, P * t:P * t + P, :]).then_inc(k.x_loaded.sem, 16)
            k.load_weights(sp, SLOTS)

        @block.scalar
        def _(act):
            for q in range(0, KD, 2):
                act.wait_ge(*k.flipped.after(q // 2 + 1))
                act.activation(k.act_hi[:, q:q + 2], ps[:, 4 + q // 2, :], ACT.Copy).then_inc(k.flip_copied.sem, 1)

        @block.gpsimd
        def _(pool):
            k.pool.done(pool, pool.memset(k.ident[:], 0.0))
            pool.affine_select(out=k.ident[:], in_=k.ident[:], compare_op=ALU.not_equal, fill=1.0, base=0,
                               pattern=[[-1, P]], channel_multiplier=1).then_inc(k.consts_ready.sem, 1)
            pool.memset(k.ones[:], 1.0)
            k.pool.done(pool, pool.memset(k.causal[:], 0.0))
            pool.affine_select(out=k.causal[:], in_=k.causal[:], compare_op=ALU.is_ge, fill=NEG, base=P,
                               pattern=[[-1, S]], channel_multiplier=1)

        @block.tensor
        def _(pe):
            pe.wait_ge(*k.consts_ready.after(1))
            pe.wait_ge(*k.x_loaded.after(16 * TT))
            for q in range(KD):
                for t in range(TT):
                    c = S * (q % 2) + P * t
                    ins = pe.transpose(ps[:, 4 + q // 2, c:c + P], k.x[:, t, P * q:P * q + P], k.ident[:])
                if q % 2:
                    ins.then_inc(k.flipped.sem, 1)

        @block.vector
        def _(dve):
            dve.memset(k.eps[:, 0:1], EPS_LN)
            dve.memset(k.eps[:, 1:2], EPS_RMS)
            for q in range(0, KD, 2):
                dve.wait_ge(*k.flip_copied.after(q // 2 + 1))
                dve.tensor_tensor(k.act_lo[:, q:q + 2], ps[:, 4 + q // 2, :].rearrange("p (q s) -> p q s", q=2),
                                  k.act_hi[:, q:q + 2].bitcast(F32), ALU.subtract)
    k.x_loaded.passed(16 * TT)
    k.consts_ready.passed(1)
    k.flipped.passed(KD // 2)
    k.flip_copied.passed(KD // 2)


def param_loads(k, rows, rows2, table, rel):
    w = k.w
    loads = [(rows[PARAM_AT[name]:PARAM_AT[name] + n, :], flat_rows(w[name])) for name, n in PARAM_ROWS]
    loads.append((k.small[:], w["const_small"]))
    for i, name in enumerate(HEAD_GAINS):
        src = w["nsa_k_norm_2"][0, int(name[-1]):int(name[-1]) + 1, :] if name.startswith("nsa_k") else w[name]
        loads += [(rows2[i:i + 1, half * HD:half * HD + HD], src) for half in range(2)]
    loads.append((k.fox_bias[:], w["ev_fox_bf"].rearrange("a h -> h a")))
    for name, row in LN_AT.items():
        loads.append((rows2[row:row + 4 * KD, :], flat_rows(w[name])))
    rb = w["rel_bias_2"]
    loads += [(table[:], w["const_bias_tables"]), (rel[0:32, 0:12], rb[:, 0:12]), (rel[0:32, 12:20], rb[:, 0:8]),
              (rel[0:32, 20:28], rb[:, 8:16]), (rel[32:32 + MASK_SETS, :], w["const_bias_sets"])]
    return loads


def parameters(k, rows, rows2, table, rel, bias, n_loads):
    with k.nc.Block() as block:
        @block.tensor
        def _(pe):
            pe.wait_ge(*k.params_loaded.after(16 * n_loads))
            pe.transpose(k.ps[:, 0, 0:N_ROWS], rows[0:N_ROWS, :], k.ident[0:N_ROWS, 0:N_ROWS])
            pe.transpose(k.ps[:, 1, 0:N_ROWS2], rows2[0:N_ROWS2, :], k.ident[0:N_ROWS2, 0:N_ROWS2])
            pe.matmul(k.ps[0:BIAS_HEADS, 2, 0:3 * P], rel[:], table[:], start=True, stop=True)\
              .then_inc(k.pe_a.sem, 1)

        @block.vector
        def _(dve):
            dve.wait_ge(*k.pe_a.after(1))
            dve.tensor_copy(bias[:], k.ps[0:BIAS_HEADS, 2, 0:3 * P]).then_inc(k.dve_a.sem, 1)
            dve.tensor_copy(k.cols[:, 0:N_ROWS], k.ps[:, 0, 0:N_ROWS])
            dve.tensor_copy(k.cols2[:, 0:N_ROWS2], k.ps[:, 1, 0:N_ROWS2])

        @block.sync
        def _(sp):
            sp.wait_ge(*k.dve_a.after(1))
            sp.dma_start(k.bias_dram, bias[:]).then_inc(k.bias_stored.sem, 16)
    k.params_loaded.passed(16 * n_loads)
    k.pe_a.passed(1)
    k.dve_a.passed(1)



def keep_warm(k, pe, n, bank):
    for _ in range(n):
        pe.matmul(k.ps[:, bank, 0:S], k.ones[:, 0:P], k.ones[:], start=True, stop=True)


def norm(k, block, residual, layer_norm=None, rms=None, meanwhile=None):
    ps, x, st = k.ps, k.x, k.st
    deferred = layer_norm is not None and rms is None
    BN, MV = slice(0, 12), slice(12, 14)
    SUM, NEG_MEAN, SHIFT = (slice(c, c + 1) for c in (14, 15, 16))
    VAR, STD, RSTD = (lambda t: slice(17 + t, 18 + t)), (lambda t: slice(19 + t, 20 + t)), (lambda t: slice(21 + t, 22 + t))
    SSQ, ROOT, RRMS = (lambda t: slice(23 + t, 24 + t)), (lambda t: slice(25 + t, 26 + t)), (lambda t: slice(27 + t, 28 + t))
    BY_DVE, LO_BY_POOL = (0, 1, 4, 5), (0, 3, 6)
    diag = k.diag
    a, b = residual

    def flat(t):
        return ps[:, 2 * t:2 * t + 2, :].rearrange("p b n -> p (b n)")

    def bank(q):
        return ps[:, 4 + q // 2, S * (q % 2):S * (q % 2) + S]

    @block.vector
    def _(dve):
        for t in (1, 0):
            if a == 1.0:
                ins = dve.scalar_tensor_tensor(out=x[:, t], in0=flat(t), scalar=b, in1=x[:, t],
                                               op0=ALU.mult, op1=ALU.add)
            else:
                ins = dve.scalar_tensor_tensor(out=x[:, t], in0=x[:, t], scalar=a, in1=flat(t),
                                               op0=ALU.mult, op1=ALU.add)
            k.dve.done(dve, ins)
            dve.sem_inc(k.summed.sem, 1)
        if layer_norm is not None:
            for h in range(2):
                ins = dve.bn_stats(st[:, 6 * h:6 * h + 6], x[:, 0, BANK * h:BANK * h + BANK])
            k.dve.done(dve, ins)
            dve.bn_aggr(st[:, MV], st[:, BN]).then_inc(k.stats_ready.sem, 1)
            dve.wait_ge(*k.root_ready.after(1))
            k.dve.done(dve, dve.reciprocal(st[:, RSTD(1)], st[:, STD(1)]))
            dve.sem_inc(k.stats_ready.sem, 1)
            dve.wait_ge(*k.root_ready.after(2))
            k.dve.done(dve, dve.reciprocal(st[:, RSTD(0)], st[:, STD(0)]))
            ins = dve.tensor_scalar(x[:, 0], x[:, 0], st[:, 12:13], st[:, RSTD(0)], ALU.subtract, ALU.mult)
            if deferred:
                ins.then_inc(k.normed_ready.sem, 1)
            else:
                k.dve.done(dve, ins)
                dve.wait_ge(*k.loaded.after(32))
                k.dve.done(dve, dve.tensor_tensor(x[:, 0], x[:, 0], k.gb[:, 0], ALU.mult))
                k.dve.done(dve, dve.tensor_tensor(x[:, 0], x[:, 0], k.gb[:, 1], ALU.add))
                dve.sem_inc(k.summed.sem, 1)
        if rms is not None:
            for t in (1, 0):
                dve.wait_ge(*k.root_ready.after((2 if layer_norm is not None else 0) + 2 - t))
                k.dve.done(dve, dve.reciprocal(st[:, RRMS(t)], st[:, ROOT(t)]))
                dve.tensor_scalar(diag[:, t], k.ident[:], st[:, RRMS(t)], None, ALU.mult)\
                   .then_inc(k.normed_ready.sem, 1)
        if deferred:
            for n, q in enumerate(BY_DVE):
                dve.wait_ge(*k.flipped.after(q // 2 + 1))
                g, h = (k.cols2[:, c:c + 1] for c in ln_columns(layer_norm, q))
                dve.tensor_scalar(k.whole[:, q], bank(q), g, h, ALU.mult, ALU.add).then_inc(k.whole_ready.sem, 1)
            for q in range(KD):
                if q not in LO_BY_POOL:
                    dve.wait_ge(*k.flip_copied.after(q + 1))
                    dve.tensor_tensor(k.act_lo[:, q], k.whole[:, q], k.act_hi[:, q].bitcast(F32), ALU.subtract)\
                       .then_inc(k.split_ready.sem, 1)
        else:
            for q in range(KD):
                dve.wait_ge(*k.flip_copied.after(2 * (q // 2) + 2))
                dve.scalar_tensor_tensor(out=k.act_lo[:, q], in0=bank(q), scalar=k.cols[:, rms + q:rms + q + 1],
                                         in1=k.act_hi[:, q].bitcast(F32), op0=ALU.mult, op1=ALU.subtract)\
                   .then_inc(k.split_ready.sem, 1)

    @block.scalar
    def _(act):
        if meanwhile:
            meanwhile[0](act, 0)
        if layer_norm is not None:
            act.wait_ge(*k.summed.after(1))
            k.act.done(act, act.activation(k.xn[:, 1], x[:, 1], ACT.Copy, accum_out=st[:, SUM]))
            k.act.done(act, act.activation(st[:, NEG_MEAN], st[:, SUM], ACT.Copy, scale=-1.0 / D))
            k.act.done(act, act.activation(k.xn[:, 1], x[:, 1], ACT.Square, bias=st[:, NEG_MEAN],
                                           accum_out=st[:, VAR(1)]))
            act.activation(st[:, STD(1)], st[:, VAR(1)], ACT.Sqrt, bias=k.eps[:, 0:1], scale=1.0 / D)\
               .then_inc(k.root_ready.sem, 1)
            act.wait_ge(*k.stats_ready.after(1))
            act.activation(st[:, STD(0)], st[:, 13:14], ACT.Sqrt, bias=k.eps[:, 0:1]).then_inc(k.root_ready.sem, 1)
            act.wait_ge(*k.stats_ready.after(2))
            k.act.done(act, act.activation(st[:, SHIFT], st[:, NEG_MEAN], ACT.Copy, scale=st[:, RSTD(1)]))
            ins = act.activation(x[:, 1], x[:, 1], ACT.Identity, bias=st[:, SHIFT], scale=st[:, RSTD(1)])
            if deferred:
                ins.then_inc(k.normed_ready.sem, 1)
            else:
                ins.then_inc(k.act_a.sem, 1)
        if rms is not None:
            for t in (1, 0):
                if layer_norm is None:
                    act.wait_ge(*k.summed.after(2 - t))
                elif t:
                    act.wait_ge(*k.pool_a.after(1))
                else:
                    act.wait_ge(*k.summed.after(3))
                k.act.done(act, act.activation(k.xn[:, t], x[:, t], ACT.Square, scale=D ** -0.5,
                                               accum_out=st[:, SSQ(t)]))
                act.activation(st[:, ROOT(t)], st[:, SSQ(t)], ACT.Sqrt, bias=k.eps[:, 1:2])\
                   .then_inc(k.root_ready.sem, 1)
        if meanwhile:
            meanwhile[0](act, 1)
        for q in range(KD):
            if deferred:
                if q in BY_DVE:
                    act.wait_ge(*k.whole_ready.after(BY_DVE.index(q) + 1))
                else:
                    act.wait_ge(*k.flipped.after(q // 2 + 1))
                    g, h = (k.cols2[:, c:c + 1] for c in ln_columns(layer_norm, q))
                    k.act.done(act, act.activation(k.whole[:, q], bank(q), ACT.Identity, bias=h, scale=g))
                act.activation(k.act_hi[:, q], k.whole[:, q], ACT.Copy).then_inc(k.flip_copied.sem, 1)
            else:
                act.wait_ge(*k.flipped.after(q // 2 + 1))
                act.activation(k.act_hi[:, q], bank(q), ACT.Copy, scale=k.cols[:, rms + q:rms + q + 1])\
                   .then_inc(k.flip_copied.sem, 1)

    @block.gpsimd
    def _(pool):
        if meanwhile:
            meanwhile[1](pool, 0)
        if layer_norm is not None and not deferred:
            pool.wait_ge(*k.act_a.after(1))
            pool.wait_ge(*k.loaded.after(32))
            k.pool.done(pool, pool.tensor_tensor(x[:, 1], x[:, 1], k.gb[:, 0], ALU.mult))
            pool.tensor_tensor(x[:, 1], x[:, 1], k.gb[:, 1], ALU.add).then_inc(k.pool_a.sem, 1)
        if meanwhile:
            meanwhile[1](pool, 1)
        if deferred:
            for q in LO_BY_POOL:
                pool.wait_ge(*k.flip_copied.after(q + 1))
                pool.tensor_tensor(k.act_lo[:, q], k.whole[:, q], k.act_hi[:, q].bitcast(F32), ALU.subtract)\
                    .then_inc(k.split_by_pool.sem, 1)

    @block.tensor
    def _(pe):
        keep_warm(k, pe, WARM[0] if rms is None else WARM[1] if layer_norm is None else WARM[2], 7)
        if rms is not None:
            for t in (1, 0):
                pe.wait_ge(*k.normed_ready.after(2 - t))
                for q in range(KD):
                    c = S * (q % 2) + P * t
                    ins = pe.matmul(ps[:, 4 + q // 2, c:c + P], x[:, t, P * q:P * q + P], diag[:, t],
                                    start=True, stop=True)
                    if q % 2 and t == 0:
                        ins.then_inc(k.flipped.sem, 1)
        else:
            pe.wait_ge(*k.normed_ready.after(2))
            for q in range(KD):
                for t in range(TT):
                    c = S * (q % 2) + P * t
                    ins = pe.transpose(ps[:, 4 + q // 2, c:c + P], x[:, t, P * q:P * q + P], k.ident[:])
                if q % 2:
                    ins.then_inc(k.flipped.sem, 1)
        keep_warm(k, pe, WARM[3], 0)

    @block.sync
    def _(sp):
        if layer_norm is not None:
            i, j = layer_norm
            for n, name in enumerate(("ln_g", "ln_b")):
                row = k.w[name][i, j:j + 1, :]
                sp.dma_start(k.gb[:, n], row.to_broadcast([P, D])).then_inc(k.loaded.sem, 16)
    n = (layer_norm is not None) + (rms is not None)
    k.summed.passed(TT + (layer_norm is not None and not deferred))
    k.stats_ready.passed(2 if layer_norm is not None else 0)
    k.root_ready.passed(2 * n)
    if layer_norm is not None and not deferred:
        k.act_a.passed(1)
        k.pool_a.passed(1)
    k.normed_ready.passed(TT)
    k.flipped.passed(KD // 2)
    k.flip_copied.passed(KD)
    if deferred:
        k.whole_ready.passed(len(BY_DVE))
        gain_loaded = k.loaded.after(32)

        def finish(pool):
            pool.wait_ge(*gain_loaded)
            for n, op in enumerate((ALU.mult, ALU.add)):
                for t in range(TT):
                    ins = pool.tensor_tensor(x[:, t], x[:, t], k.gb[:, n], op)
                k.pool.done(pool, ins)
        k.unfinished = finish
    k.loaded.passed(32 if layer_norm is not None else 0)
    by_dve = [q for q in range(KD) if not deferred or q not in LO_BY_POOL]
    by_pool = [q for q in range(KD) if q not in by_dve]
    ready = [k.split_ready.after(by_dve.index(q) + 1) if q in by_dve else k.split_by_pool.after(by_pool.index(q) + 1)
             for q in range(KD)]
    k.split_ready.passed(len(by_dve))
    k.split_by_pool.passed(len(by_pool))
    return ready


def ln_columns(layer_norm, q):
    i, j = layer_norm
    return [LN_AT[name] + KD * (2 * i + j) + q for name in ("ln_g", "ln_b")]


def store_result(k):
    with k.nc.Block() as block:
        @block.vector
        def _(dve):
            for t in range(TT):
                acc = k.ps[:, 2 * t:2 * t + 2, :].rearrange("p b n -> p (b n)")
                dve.scalar_tensor_tensor(out=k.x[:, t], in0=acc, scalar=0.5, in1=k.x[:, t],
                                         op0=ALU.mult, op1=ALU.add).then_inc(k.normed_ready.sem, 1)

        @block.sync
        def _(sp):
            for t in range(TT):
                sp.wait_ge(*k.normed_ready.after(t + 1))
                sp.dma_start(k.out[0, P * t:P * t + P, :], k.x[:, t]).then_inc(k.stored.sem, 16)
            sp.wait_ge(*k.stored.after(16 * TT))
    k.normed_ready.passed(TT)
    k.stored.passed(16 * TT)



def early_split(k, first, hi, lo, whole, hi_ready, split):
    def make_hi(eng, n):
        eng.wait_ge(k.weights_in[first % SLOTS], k.arrived[first])
        eng.activation(hi(n), whole(n), ACT.Copy).then_inc(hi_ready.sem, 1)

    def make_lo(eng, n):
        eng.wait_ge(*hi_ready.after(n + 1))
        eng.tensor_tensor(lo(n), whole(n), hi(n).bitcast(F32), ALU.subtract).then_inc(split.sem, 1)

    return make_hi, make_lo


def finish_norm(k, pool):
    if k.unfinished:
        k.unfinished(pool)
        k.unfinished = None


def split_products(pe, out, left, right, start, stop, **more):
    pe.matmul(out, left[0], right[0], start=start, stop=False, **more)
    pe.matmul(out, left[0], right[1], start=False, stop=False, **more)
    return pe.matmul(out, left[1], right[0], start=False, stop=stop, **more)


def product(k, name, kt, pieces, before=None, then="sqrt_and_others", loads=()):
    ps, nc = k.ps, k.nc
    first = k.first[name]
    early = 2 if before else 0
    per = kt // 2
    RING = 4
    done = [0]
    for kind, dst, width in pieces:
        done.append(done[-1] + {"token": TT, "feature": -(-width // P), "acc": 0}[kind])

    def results(i):
        kind, dst, width = pieces[i]
        if kind == "token":
            return [(4 * (i % 2) + t, ps[:, 4 * (i % 2) + t, 0:width], dst(t)) for t in range(TT)]
        if kind == "feature":
            return [(4 * (i % 2) + m, ps[0:min(P, width - P * m), 4 * (i % 2) + m, 0:S], dst(m))
                    for m in range(-(-width // P))]
        return []

    with ExitStack() as ctx:
        w_hi, w_lo = (ctx.enter_context(nc.sbuf_tensor(f"{name}_{n}", [P, RING, 2 * BANK], F32R)) for n in ("hi", "lo"))

        def part(buf, n, width):
            return buf[:, n % RING, 0:2 * width].rearrange("p (k n) -> p k n", k=2)

        def raw(i, g):
            return k.slot_view(first + i, kt, pieces[i][2])[:, 2 * g:2 * g + 2, :]

        block = ctx.enter_context(nc.Block())
        ready = None
        if before:
            ready = norm(k, block, **before, meanwhile=early_split(
                k, first, lambda n: part(w_hi, n, pieces[0][2]), lambda n: part(w_lo, n, pieces[0][2]),
                lambda n: raw(0, n), k.part_hi, k.early_split))

        @block.scalar
        def _(act):
            for i in range(len(pieces)):
                j = first + i
                act.wait_ge(k.weights_in[j % SLOTS], k.arrived[j])
                for g in range(per):
                    n = per * i + g
                    if n < early:
                        continue
                    if n >= RING:
                        act.wait_ge(*k.part_used.after(n - RING + 1))
                    act.activation(part(w_hi, n, pieces[i][2]), raw(i, g), ACT.Copy).then_inc(k.part_hi.sem, 1)
            act.preload_act_table_set(then)

        @block.vector
        def _(dve):
            def copy_results(i):
                for r, (bank, psum, dst) in enumerate(results(i)):
                    if r == 0:
                        dve.wait_ge(*k.part_used.after(per * (i + 1)))
                    dve.tensor_copy(dst, psum).then_inc(k.product_copied.sem, 1)

            for i, (kind, dst, width) in enumerate(pieces):
                for g in range(per):
                    n = per * i + g
                    if n < early:
                        continue
                    dve.wait_ge(*k.part_hi.after(n + 1))
                    dve.tensor_tensor(part(w_lo, n, width), raw(i, g), part(w_hi, n, width).bitcast(F32),
                                      ALU.subtract).then_inc(k.part_split.sem, 1)
                dve.wait_ge(*k.part_split.after(per * (i + 1) - early))
                if i == 0 and early:
                    dve.wait_ge(*k.early_split.after(early))
                dve.sem_inc(k.weights_used, 1)
                if i:
                    copy_results(i - 1)
            copy_results(len(pieces) - 1)

        @block.tensor
        def _(pe):
            for i, (kind, dst, width) in enumerate(pieces):
                if i >= 2 and done[i - 1]:
                    pe.wait_ge(*k.product_copied.after(done[i - 1]))
                for g in range(per):
                    n = per * i + g
                    pe.wait_ge(*(k.early_split.after(n + 1) if n < early else k.part_split.after(n + 1 - early)))
                    wh, wl = part(w_hi, n, width), part(w_lo, n, width)
                    for e in range(2):
                        q = 2 * g + e
                        start, stop = q == 0, q == kt - 1
                        if i == 0 and ready:
                            pe.wait_ge(*ready[q])
                        if kind == "feature":
                            for m, (bank, psum, _) in enumerate(results(i)):
                                c = slice(P * m, min(P * m + P, width))
                                ins = split_products(pe, psum, (wh[:, e, c], wl[:, e, c]),
                                                     (k.act_hi[:, q, :], k.act_lo[:, q, :]), start, stop)
                        else:
                            for t in range(TT):
                                bank = 2 * t + i if kind == "acc" else 4 * (i % 2) + t
                                c = slice(P * t, P * t + P)
                                ins = split_products(pe, ps[:, bank, 0:width], (k.act_hi[:, q, c], k.act_lo[:, q, c]),
                                                     (wh[:, e, :], wl[:, e, :]), start, stop)
                    ins.then_inc(k.part_used.sem, 1)

        @block.gpsimd
        def _(pool):
            finish_norm(k, pool)

        @block.sync
        def _(sp):
            for dst, src in loads:
                sp.dma_start(dst, src).then_inc(k.params_loaded.sem, 16)
            k.load_weights(sp, first + len(pieces) + SLOTS)
    n = per * len(pieces)
    k.part_hi.passed(n)
    k.part_split.passed(n - early)
    k.early_split.passed(early)
    k.part_used.passed(n)
    k.product_copied.passed(done[-1])


def out_product(k, name, kt):
    product(k, name, kt, [("acc", None, BANK)] * 2)


def feed_forward(k, name, before=None):
    ps, nc = k.ps, k.nc
    early = 2 if before else 0
    first = k.first[name]
    BODY = 4
    pairs = FT // 2

    def item(f, down):
        return first + 2 * (f // 2) + down

    with ExitStack() as ctx:
        def sb(part, shape, dt):
            return ctx.enter_context(nc.sbuf_tensor(f"{name}_{part}", shape, dt))

        silu, hid = sb("silu", [P, 2, S], F32), sb("hidden", [P, 2, S], F32)
        hid_hi, hid_lo = (sb(n, [P, 2, S], F32R) for n in ("hidden_hi", "hidden_lo"))
        gu_hi, gu_lo = (sb(n, [P, 2, 2, KD, P], F32R) for n in ("gate_up_hi", "gate_up_lo"))
        dn_hi, dn_lo = (sb(n, [P, 2, 2, BANK], F32R) for n in ("down_hi", "down_lo"))

        def raw_gate_up(f, u):
            w = k.slot[:, item(f, 0) % SLOTS, 2048 * u:2048 * u + 2048].rearrange("p (k n) -> p k n", k=KD)
            return w[:, :, P * (f % 2):P * (f % 2) + P]

        def raw_down(f):
            w = k.slot[:, item(f, 1) % SLOTS, 0:2048].rearrange("p (h k n) -> p h k n", h=2, k=2)
            return w[:, :, f % 2, :]

        def at(eng, mark, f, turn):
            eng.wait_ge(mark.sem, turn * BODY + (mark.at + f + 1))

        def arrived(eng, f, down, turn):
            j = item(f, down)
            eng.wait_ge(k.weights_in[j % SLOTS], turn * 32 + k.arrived[j])

        block = ctx.enter_context(nc.Block())
        ready = None
        if before:
            ready = norm(k, block, **before, meanwhile=early_split(
                k, first, lambda u: gu_hi[:, 0, u], lambda u: gu_lo[:, 0, u], lambda u: raw_gate_up(0, u),
                k.gate_up_hi, k.early_split))

        @block.tensor
        def _(pe):
            def gate_up(f, turn, first=False):
                for u in range(2):
                    if first and early:
                        pe.wait_ge(*k.early_split.after(u + 1))
                    else:
                        pe.wait_ge(k.gate_up_split.sem,
                                   turn * 2 * BODY + (k.gate_up_split.at + 2 * f + u + 1 - early))
                    if first and u == 0 and ready:
                        pe.wait_ge(*ready[1])
                    for q in range(KD):
                        if first and u == 0 and ready:
                            pe.wait_ge(*ready[q])
                        ins = split_products(pe, ps[:, 4 + f % 2, S * u:S * u + S],
                                             (gu_hi[:, f % 2, u, q, :], gu_lo[:, f % 2, u, q, :]),
                                             (k.act_hi[:, q, :], k.act_lo[:, q, :]), q == 0, q == KD - 1)
                ins.then_inc(k.gate_up_ready.sem, 1)

            def down(f, turn, start, stop):
                at(pe, k.down_split, f, turn)
                at(pe, k.hidden_split, f, turn)
                for t in range(TT):
                    c = slice(P * t, P * t + P)
                    for h in range(2):
                        ins = split_products(pe, ps[:, 2 * t + h, :], (hid_hi[:, f % 2, c], hid_lo[:, f % 2, c]),
                                             (dn_hi[:, f % 2, h, :], dn_lo[:, f % 2, h, :]), start, stop,
                                             skip_group_check=True)
                ins.then_inc(k.down_used.sem, 1)

            gate_up(0, 0, first=True)
            gate_up(1, 0)
            down(0, 0, True, False)
            turns = (FT - 2) // BODY
            assert 2 + BODY * turns == FT
            with pe.Fori(0, turns) as turn:
                for f in range(1, 1 + BODY):
                    gate_up(f + 1, turn)
                    down(f, turn, False, False)
            down(FT - 1, 0, False, True)

        FIRST = 2
        turns = (FT - FIRST - BODY) // BODY
        LAST = FIRST + BODY * turns

        def steps(eng, step):
            for f in range(FIRST):
                step(f, 0)
            with eng.Fori(0, turns) as turn:
                for f in range(FIRST, FIRST + BODY):
                    step(f, turn)
            for f in range(LAST, FT):
                step(f, 0)

        @block.scalar
        def _(act):
            def gate_up_hi(f, turn, skip=0):
                if f % 2 == 0:
                    arrived(act, f, 0, turn)
                for u in range(skip, 2):
                    act.activation(gu_hi[:, f % 2, u], raw_gate_up(f, u), ACT.Copy).then_inc(k.gate_up_hi.sem, 1)

            def down_hi(f, turn):
                if f % 2 == 0:
                    arrived(act, f, 1, turn)
                if f >= 2:
                    at(act, k.down_used, f - 2, turn)
                act.activation(dn_hi[:, f % 2], raw_down(f), ACT.Copy).then_inc(k.down_hi.sem, 1)

            def step(f, turn):
                at(act, k.gate_up_ready, f, turn)
                if f >= 2:
                    at(act, k.hidden_ready, f - 2, turn)
                act.activation(silu[:, f % 2, :], ps[:, 4 + f % 2, 0:S], ACT.Silu).then_inc(k.silu_ready.sem, 1)
                at(act, k.hidden_ready, f, turn)
                if f >= 2:
                    at(act, k.down_used, f - 2, turn)
                act.activation(hid_hi[:, f % 2, :], hid[:, f % 2, :], ACT.Copy).then_inc(k.hidden_hi.sem, 1)
                if f + 2 < FT:
                    gate_up_hi(f + 2, turn)
                if f + 1 < FT:
                    down_hi(f + 1, turn)

            gate_up_hi(0, 0, skip=early)
            gate_up_hi(1, 0)
            down_hi(0, 0)
            act.preload_act_table_set("silu_and_others")
            steps(act, step)
            act.preload_act_table_set("sqrt_and_others")

        @block.vector
        def _(dve):
            def gate_up_lo(f, turn, skip=0):
                for u in range(skip, 2):
                    dve.wait_ge(k.gate_up_hi.sem, turn * 2 * BODY + (k.gate_up_hi.at + 2 * f + u + 1))
                    dve.tensor_tensor(gu_lo[:, f % 2, u], raw_gate_up(f, u), gu_hi[:, f % 2, u].bitcast(F32),
                                      ALU.subtract).then_inc(k.gate_up_split.sem, 1)

            def down_lo(f, turn):
                at(dve, k.down_hi, f, turn)
                dve.tensor_tensor(dn_lo[:, f % 2], raw_down(f), dn_hi[:, f % 2].bitcast(F32),
                                  ALU.subtract).then_inc(k.down_split.sem, 1)
                if f % 2:
                    at(dve, k.down_split, f, turn)
                    dve.sem_inc(k.weights_used, 2)

            def step(f, turn):
                at(dve, k.silu_ready, f, turn)
                if f >= 2:
                    at(dve, k.hidden_split, f - 2, turn)
                dve.tensor_tensor(hid[:, f % 2, :], ps[:, 4 + f % 2, S:2 * S], silu[:, f % 2, :],
                                  ALU.mult).then_inc(k.hidden_ready.sem, 1)
                at(dve, k.hidden_hi, f, turn)
                dve.tensor_tensor(hid_lo[:, f % 2, :], hid[:, f % 2, :], hid_hi[:, f % 2, :].bitcast(F32),
                                  ALU.subtract).then_inc(k.hidden_split.sem, 1)
                if f + 2 < FT:
                    gate_up_lo(f + 2, turn)
                if f + 1 < FT:
                    down_lo(f + 1, turn)

            gate_up_lo(0, 0, skip=early)
            gate_up_lo(1, 0)
            down_lo(0, 0)
            if early:
                dve.wait_ge(*k.early_split.after(early))
            steps(dve, step)

        @block.gpsimd
        def _(pool):
            finish_norm(k, pool)

        @block.sync
        def _(sp):
            assert k.issued == first + SLOTS

            def pair(c, turn):
                for down in range(2):
                    j = first + 2 * c + down
                    sp.wait_ge(k.weights_used, turn * 4 + (j - SLOTS + 1))
                    for dst, src in k.items[j]:
                        step = turn * (512 * D if down else 512)
                        sp.dma_start(dst, bass.AP(src.tensor, src.offset + step, src.ap))\
                          .then_inc(k.weights_in[j % SLOTS], 16)

            turns = (pairs - 3) // 2
            with sp.Fori(0, turns) as turn:
                for c in (2, 3):
                    pair(c, turn)
            k.issued = first + 2 * (2 + 2 * turns)
            k.load_weights(sp, first + FT + SLOTS)
    k.gate_up_hi.passed(2 * FT)
    k.gate_up_split.passed(2 * FT - early)
    k.early_split.passed(early)
    for mark in (k.down_hi, k.down_split, k.hidden_hi, k.hidden_split, k.gate_up_ready, k.silu_ready,
                 k.hidden_ready, k.down_used):
        mark.passed(FT)



def softmax_attention(k, softmaxes, first_tile, base=None, fill=(0, 0, 0)):
    nc, ps = k.nc, k.ps
    M, G = len(softmaxes), len(softmaxes[0]["units"])
    RING, DIAGS = max(6, 3 * G), 3
    LAG = 2
    blocks = ((0, P), (P, P + S))
    heads = [x["head"] for x in softmaxes]
    base = base or (lambda p: None)

    def last_of_pair(m):
        if heads[m] % 2 and (m == M - 1 or heads[m + 1] != heads[m]):
            return heads[m] // 2
        return None

    with ExitStack() as ctx:
        def sb(name, shape):
            return ctx.enter_context(nc.sbuf_tensor(f"att{k.uid()}_{name}", shape, F32))

        logits, probs, probs_T = (sb(n, [P, RING, 3 * P]) for n in ("logits", "probs", "probs_T"))
        diag = sb("diag", [P, DIAGS, TT, P])
        nmax_u, rows = sb("nmax_u", [P, M, TT, G]), sb("rows", [P, M, TT, G])
        nmax, den, fac, esink = (sb(n, [P, M, TT]) for n in ("nmax", "den", "fac", "esink"))
        block = ctx.enter_context(nc.Block())

        @block.tensor
        def _(pe):
            def scores(m):
                for u, x in enumerate(softmaxes[m]["units"]):
                    n = m * G + u
                    bank = ps[:, n % 4, :]
                    if n >= 4:
                        pe.wait_ge(*k.logits_ready.after((n - 4) // G + 1))
                    for t in range(TT):
                        a, b = blocks[t]
                        keys = P * (t + 1)
                        ins = pe.matmul(bank[:, a:b], x["q"](t), x["kT"][:, 0:keys], start=True, stop="extra" not in x)
                        if "extra" in x:
                            lhsT, rhs = x["extra"]
                            ins = pe.matmul(bank[:, a:b], lhsT, rhs[:, 0:keys], start=False, stop=True)
                    ins.then_inc(k.scores_ready.sem, 1)

            def flips(m):
                pe.wait_ge(*k.pool_a.after(m + 1))
                for u in range(G):
                    n = m * G + u
                    if n >= 2:
                        pe.wait_ge(*k.probs_T_ready.after(n - 1))
                    for j in range(3):
                        ins = pe.matmul(ps[:, 4 + n % 2, P * j:P * j + P], probs[:, n % RING, P * j:P * j + P],
                                        diag[:, m % DIAGS, min(j, 1), :], start=True, stop=True)
                    ins.then_inc(k.probs_flipped.sem, 1)

            def values(m):
                h = heads[m]
                pair = h // 2
                new_head = m == 0 or heads[m - 1] != h
                whole = ps[:, 6 + pair % 2, :]
                if new_head and h % 2 == 0:
                    if pair >= 2:
                        pe.wait_ge(*k.heads_done.after(pair - 1))
                    if base(pair):
                        pe.matmul(whole[:, 0:S], *base(pair), start=True, stop=False, skip_group_check=True)
                pe.wait_ge(*k.probs_T_ready.after(m * G + G))
                o = whole[HD * (h % 2):HD * (h % 2) + HD, :]
                last_of_head = m == M - 1 or heads[m + 1] != h
                for u, x in enumerate(softmaxes[m]["units"]):
                    w = probs_T[:, (m * G + u) % RING, :]
                    pe.matmul(o[:, 0:S], x["v"](0), w[:, 0:S], start=new_head and u == 0 and not base(pair),
                              stop=False, skip_group_check=True)
                    ins = pe.matmul(o[:, P:S], x["v"](1), w[:, S:S + P], start=False,
                                    stop=last_of_head and u == G - 1, skip_group_check=True)
                ins.then_inc(k.heads_ready.sem, 1)

            for i in range(M + LAG + 1):
                if i < M:
                    scores(i)
                if i < len(fill):
                    keep_warm(k, pe, fill[i], 7)
                if LAG <= i < M + LAG:
                    flips(i - LAG)
                if i > LAG:
                    values(i - LAG - 1)

        @block.vector
        def _(dve):
            def add_bias(m):
                sink = softmaxes[m].get("sink")
                for u, x in enumerate(softmaxes[m]["units"]):
                    n = m * G + u
                    dve.wait_ge(*k.scores_ready.after(n + 1))
                    if n >= RING:
                        dve.wait_ge(*k.probs_ready.after(n - RING + 1))
                    for t in range(TT):
                        a, b = blocks[t]
                        ins = dve.tensor_tensor_reduce(out=logits[:, n % RING, a:b], in0=ps[:, n % 4, a:b],
                                                       in1=x["bias"][:, P * (1 - t):S], scale=-1.0, scalar=FLT_MAX,
                                                       op0=ALU.add, op1=ALU.min, accum_out=nmax_u[:, m, t, u:u + 1])
                if G > 1:
                    k.dve.done(dve, ins)
                    ins = dve.tensor_reduce(nmax[:, m, :], nmax_u[:, m], AX.X, ALU.min)
                elif sink:
                    k.dve.done(dve, ins)
                    ins = dve.tensor_scalar(nmax[:, m, :], nmax_u[:, m, :, 0], sink[1], None, ALU.min)
                ins.then_inc(k.logits_ready.sem, 1)

            def factors(m):
                sink, gate = softmaxes[m].get("sink"), softmaxes[m].get("gate")
                dve.wait_ge(*k.probs_ready.after(m * G + G))
                total = rows[:, m, :, 0]
                if G > 1:
                    k.dve.done(dve, dve.tensor_reduce(den[:, m, :], rows[:, m], AX.X, ALU.add))
                    total = den[:, m, :]
                elif sink:
                    k.dve.done(dve, dve.tensor_tensor(den[:, m, :], rows[:, m, :, 0], esink[:, m, :], ALU.add))
                    total = den[:, m, :]
                ins = dve.reciprocal(fac[:, m, :], total)
                if gate is not None:
                    k.dve.done(dve, ins)
                    ins = dve.tensor_tensor(fac[:, m, :], fac[:, m, :], gate, ALU.mult)
                ins.then_inc(k.dve_a.sem, 1)

            def copy_flips(m):
                for u in range(G):
                    n = m * G + u
                    dve.wait_ge(*k.probs_flipped.after(n + 1))
                    if n >= RING:
                        dve.wait_ge(*k.heads_ready.after((n - RING) // G + 1))
                    dve.tensor_copy(probs_T[:, n % RING, :], ps[:, 4 + n % 2, 0:3 * P]).then_inc(k.probs_T_ready.sem, 1)

            def lower_part(pair):
                dve.wait_ge(*k.act_b.after(pair + 1))
                tile = first_tile + pair
                dve.tensor_tensor(k.act_lo[:, tile], ps[:, 6 + pair % 2, 0:S], k.act_hi[:, tile].bitcast(F32),
                                  ALU.subtract).then_inc(k.heads_done.sem, 1)

            for i in range(M + LAG + 1):
                if i < M:
                    add_bias(i)
                if 1 <= i <= M:
                    factors(i - 1)
                if LAG <= i < M + LAG:
                    copy_flips(i - LAG)
                if i > LAG and last_of_pair(i - LAG - 1) is not None:
                    lower_part(last_of_pair(i - LAG - 1))

        @block.gpsimd
        def _(pool):
            for m in range(M):
                pool.wait_ge(*k.dve_a.after(m + 1))
                if m >= DIAGS:
                    pool.wait_ge(*k.probs_flipped.after(G * (m - DIAGS + 1)))
                pool.tensor_tensor(diag[:, m % DIAGS], bc(k.ident[:], 1, TT), bc(fac[:, m, :], 2, P), ALU.mult)\
                    .then_inc(k.pool_a.sem, 1)

        @block.scalar
        def _(act):
            def exponentials(m):
                sink = softmaxes[m].get("sink")
                act.wait_ge(*k.logits_ready.after(m + 1))
                top = nmax_u[:, m, :, 0] if G == 1 and not sink else nmax[:, m, :]
                if sink:
                    act.activation(esink[:, m, :], top, ACT.Exp, bias=sink[0])
                for u in range(G):
                    n = m * G + u
                    if n >= RING:
                        act.wait_ge(*k.probs_flipped.after(n - RING + 1))
                    for t in range(TT):
                        a, b = blocks[t]
                        ins = act.activation(probs[:, n % RING, a:b], logits[:, n % RING, a:b], ACT.Exp,
                                             bias=top[:, t:t + 1], scale=-1.0, accum_out=rows[:, m, t, u:u + 1])
                    ins.then_inc(k.probs_ready.sem, 1)

            for i in range(M + LAG + 1):
                if i < M:
                    exponentials(i)
                pair = last_of_pair(i - LAG - 1) if i > LAG else None
                if pair is not None:
                    act.wait_ge(*k.heads_ready.after(i - LAG))
                    act.activation(k.act_hi[:, first_tile + pair], ps[:, 6 + pair % 2, 0:S], ACT.Copy)\
                       .then_inc(k.act_b.sem, 1)
    for mark in (k.scores_ready, k.probs_ready, k.probs_flipped, k.probs_T_ready):
        mark.passed(M * G)
    for mark in (k.logits_ready, k.heads_ready, k.dve_a, k.pool_a):
        mark.passed(M)
    pairs = (heads[-1] + 1) // 2
    k.act_b.passed(pairs)
    k.heads_done.passed(pairs)


def transpose_mix(k, tiles):
    ps = k.ps
    with k.nc.Block() as block:
        @block.tensor
        def _(pe):
            for n, q in enumerate(tiles):
                for t in range(TT):
                    ins = pe.transpose(ps[:, n % 8, P * t:P * t + P], k.xn[:, t, P * q:P * q + P], k.ident[:])
                ins.then_inc(k.flipped.sem, 1)

        @block.scalar
        def _(act):
            for n, q in enumerate(tiles):
                act.wait_ge(*k.flipped.after(n + 1))
                act.activation(k.act_hi[:, q], ps[:, n % 8, 0:S], ACT.Copy).then_inc(k.act_a.sem, 1)

        @block.vector
        def _(dve):
            for n, q in enumerate(tiles):
                dve.wait_ge(*k.act_a.after(n + 1))
                dve.tensor_tensor(k.act_lo[:, q], ps[:, n % 8, 0:S], k.act_hi[:, q].bitcast(F32), ALU.subtract)
    k.flipped.passed(len(tiles))
    k.act_a.passed(len(tiles))



LEVELS = [S >> (i + 1) for i in range(8)]


def hgrn_masks():
    s, t = np.arange(P)[:, None], np.arange(P)[None, :]
    out = [((s // (2 * m) == t // (2 * m)) & (s % (2 * m) < m) & (t % (2 * m) >= m)) for m in LEVELS[1:]]
    return np.stack(out + [s == t], axis=1).astype(np.float32)


def hgrn(k, q, z, v, g):
    nc, ps, w = k.nc, k.ps, k.w
    H = HGRN_HEADS
    with ExitStack() as ctx:
        def sb(name, shape):
            return ctx.enter_context(nc.sbuf_tensor(f"hgrn_{name}", shape, F32))

        masks = sb("masks", [P, len(LEVELS), P])
        key, fgt, B = sb("key", [P, H, S]), sb("forget", [P, H, S]), sb("B", [P, H, S])
        dif, E, qe, ke = (sb(n, [P, 2, H * S]) for n in ("dif", "E", "qe", "ke"))
        sT = sb("scores_T", [P, H, 3, P])
        lbs, lb, oml, top, tot = (sb(n, [P, 12 if n == "lbs" else 4]) for n in ("lbs", "lb", "oml", "top", "tot"))
        ng = sb("norm_gain", [P, P])
        o2, sil = sb("o2", [P, TT, HALF]), sb("silu", [P, TT, HALF])
        ssq, rms = sb("ssq", [P, TT * H]), sb("rms", [P, TT * H])
        row = k.cols[:, PARAM_AT["hgrn_lb"]:PARAM_AT["hgrn_lb"] + 12]

        with nc.Block() as block:
            @block.sync
            def _(sp):
                sp.dma_start(masks[:], w["const_hgrn_masks"]).then_inc(k.loaded.sem, 16)
                sp.dma_start(ng[:], w["ev_hgrn_norm_g"].to_broadcast([P, P])).then_inc(k.loaded.sem, 16)

            @block.gpsimd
            def _(pool):
                pool.memset(sT[:], 0.0)
                pool.memset(qe[:], 0.0)
                pool.memset(ke[:], 0.0)

            @block.tensor
            def _(pe):
                keep_warm(k, pe, 26, 7)

            @block.scalar
            def _(act):
                act.activation(key[:], z[:], ACT.Sigmoid, scale=-1.0).then_inc(k.act_a.sem, 1)
                act.activation(fgt[:], z[:], ACT.Sigmoid).then_inc(k.act_a.sem, 1)
                act.wait_ge(*k.dve_a.after(1))
                act.activation(lbs[:], lbs[:], ACT.Exp).then_inc(k.act_a.sem, 1)
                act.wait_ge(*k.dve_a.after(2))
                act.activation(fgt[:], fgt[:], ACT.Ln).then_inc(k.act_a.sem, 1)

            @block.vector
            def _(dve):
                k.dve.done(dve, dve.tensor_tensor(top[:], row[:, 0:4], row[:, 4:8], ALU.max))
                k.dve.done(dve, dve.tensor_tensor(top[:], top[:], row[:, 8:12], ALU.max))
                dve.tensor_tensor(lbs[:].rearrange("p (r c) -> p r c", r=3), row.rearrange("p (r c) -> p r c", r=3),
                                  bc(top[:], 1, 3), ALU.subtract).then_inc(k.dve_a.sem, 1)
                dve.wait_ge(*k.act_a.after(3))
                k.dve.done(dve, dve.tensor_reduce(tot[:], lbs[:].rearrange("p (r c) -> p c r", r=3), AX.X, ALU.add))
                k.dve.done(dve, dve.reciprocal(tot[:], tot[:]))
                k.dve.done(dve, dve.tensor_tensor(lb[:], lbs[:, 0:4], tot[:], ALU.mult))
                k.dve.done(dve, dve.tensor_scalar(oml[:], lb[:], -1.0, 1.0, ALU.mult, ALU.add))
                for h in range(H):
                    ins = dve.tensor_scalar(fgt[:, h], fgt[:, h], oml[:, h:h + 1], lb[:, h:h + 1], ALU.mult, ALU.add)
                ins.then_inc(k.dve_a.sem, 1)
                for h in range(H):
                    ins = dve.tensor_scalar(key[:, h], key[:, h], oml[:, h:h + 1], None, ALU.mult)
                dve.wait_ge(*k.act_a.after(4))
                for h in range(H):
                    ins = dve.tensor_tensor_scan(B[:, h], k.ones[:], fgt[:, h], 0.0, ALU.mult, ALU.add)
                dve.wait_ge(*k.loaded.after(32))
        k.loaded.passed(32)
        k.act_a.passed(4)
        k.dve_a.passed(2)

        N = len(LEVELS)

        def half(buf, i, m, second):
            return buf[:, i % 2, :].rearrange("p (r c) -> p r c", c=2 * m)[:, :, m * second:m * second + m]

        with nc.Block() as block:
            @block.vector
            def _(dve):
                flat = B[:].rearrange("p h s -> p (h s)")

                def difference(i):
                    m = LEVELS[i]
                    pairs = flat.rearrange("p (r c) -> p r c", c=2 * m)
                    if i >= 2:
                        dve.wait_ge(*k.act_a.after(i - 1))
                    dve.tensor_tensor(dif[:, i % 2, :].rearrange("p (r c) -> p r c", c=2 * m), pairs,
                                      pairs[:, :, m - 1:m].to_broadcast([P, H * S // (2 * m), 2 * m]),
                                      ALU.subtract).then_inc(k.dve_a.sem, 1)

                def keep(i):
                    dve.wait_ge(*k.pe_a.after(i + 1))
                    b = 2 * (i % 2)
                    if i == 0:
                        dve.tensor_copy(sT[:, :, 1, :], ps[:, b, :].rearrange("p (h n) -> p h n", h=H))\
                           .then_inc(k.dve_b.sem, 1)
                        return
                    for t in range(TT):
                        mask = bc(masks[:, i - 1, :].bitcast(mybir.dt.int32), 1, H)
                        ins = dve.copy_predicated(sT[:, :, 2 * t, :], mask,
                                                  ps[:, b + t, :].rearrange("p (h n) -> p h n", h=H))
                    k.dve.done(dve, ins)
                    dve.sem_inc(k.dve_b.sem, 1)

                difference(0)
                difference(1)
                for i in range(N + 1):
                    if i + 2 < N:
                        difference(i + 2)
                    keep(i)

            @block.scalar
            def _(act):
                for i, m in enumerate(LEVELS):
                    act.wait_ge(*k.dve_a.after(i + 1))
                    if i >= 2:
                        act.wait_ge(*k.pool_a.after(i - 1))
                    act.activation(half(E, i, m, 0), half(dif, i, m, 0), ACT.Exp, scale=-1.0)
                    act.activation(half(E, i, m, 1), half(dif, i, m, 1), ACT.Exp).then_inc(k.act_a.sem, 1)

            @block.gpsimd
            def _(pool):
                for i, m in enumerate(LEVELS):
                    pool.wait_ge(*k.act_a.after(i + 1))
                    if i >= 2:
                        pool.wait_ge(*k.pe_a.after(i - 1))
                    pairs = dict(c=2 * m)
                    pool.tensor_tensor(half(qe, i, m, 1), q.rearrange("p h s -> p (h s)").rearrange(
                        "p (r c) -> p r c", **pairs)[:, :, m:2 * m], half(E, i, m, 1), ALU.mult)
                    pool.tensor_tensor(half(ke, i, m, 0), key[:].rearrange("p h s -> p (h s)").rearrange(
                        "p (r c) -> p r c", **pairs)[:, :, 0:m], half(E, i, m, 0), ALU.mult).then_inc(k.pool_a.sem, 1)

            @block.tensor
            def _(pe):
                for i in range(N + 1):
                    b = 2 * (i % 2)
                    if i < N:
                        pe.wait_ge(*k.pool_a.after(i + 1))
                    if i >= 2:
                        pe.wait_ge(*k.dve_b.after(i - 1))
                    for h in range(H):
                        for t in range(TT):
                            if i == 0:
                                if t:
                                    continue
                                left, right = ke[:, 0, S * h:S * h + P], qe[:, 0, S * h + P:S * h + S]
                            elif i < N:
                                c = S * h + P * t
                                left, right = ke[:, i % 2, c:c + P], qe[:, i % 2, c:c + P]
                            else:
                                left, right = key[:, h, P * t:P * t + P], q[:, h, P * t:P * t + P]
                            ins = pe.matmul(ps[:, b + t, P * h:P * h + P], left, right, start=True, stop=True)
                    ins.then_inc(k.pe_a.sem, 1)
                pe.wait_ge(*k.dve_b.after(N + 1))
                for t in range(TT):
                    for h in range(H):
                        for s in range(t + 1):
                            ins = pe.matmul(ps[:, 4 + t, P * h:P * h + P], sT[:, h, t + s, :],
                                            v[:, s, P * h:P * h + P], start=s == 0, stop=s == t)
                ins.then_inc(k.pe_b.sem, 1)
        k.dve_a.passed(N)
        k.act_a.passed(N)
        k.pool_a.passed(N)
        k.pe_a.passed(N + 1)
        k.dve_b.passed(N + 1)
        k.pe_b.passed(1)

        with nc.Block() as block:
            o = ps[:, 4:6, :]

            @block.tensor
            def _(pe):
                keep_warm(k, pe, 16, 7)

            @block.scalar
            def _(act):
                act.activation(o2[:], o, ACT.Square).then_inc(k.act_a.sem, 1)
                act.activation(sil[:], g, ACT.Silu).then_inc(k.act_a.sem, 1)
                act.wait_ge(*k.dve_a.after(1))
                act.activation(rms[:], ssq[:], ACT.Sqrt).then_inc(k.act_a.sem, 1)

            @block.gpsimd
            def _(pool):
                pool.wait_ge(*k.act_a.after(2))
                pool.tensor_tensor(sil[:].rearrange("p t (h n) -> p (t h) n", h=H),
                                   sil[:].rearrange("p t (h n) -> p (t h) n", h=H), bc(ng[:], 1, TT * H),
                                   ALU.mult).then_inc(k.pool_a.sem, 1)

            @block.vector
            def _(dve):
                dve.wait_ge(*k.act_a.after(1))
                k.dve.done(dve, dve.tensor_reduce(ssq[:], o2[:].rearrange("p t (h n) -> p (t h) n", h=H),
                                                  AX.X, ALU.add))
                dve.tensor_scalar(ssq[:], ssq[:], 1.0 / HGRN_DIM, EPS_LN, ALU.mult, ALU.add).then_inc(k.dve_a.sem, 1)
                dve.wait_ge(*k.act_a.after(3))
                k.dve.done(dve, dve.reciprocal(rms[:], rms[:]))
                k.dve.done(dve, dve.tensor_tensor(o2[:].rearrange("p t (h n) -> p (t h) n", h=H),
                                                  o.rearrange("p t (h n) -> p (t h) n", h=H),
                                                  bc(rms[:], 2, P), ALU.mult))
                dve.wait_ge(*k.pool_a.after(1))
                dve.tensor_tensor(k.xn[:, :, 0:HALF], o2[:], sil[:], ALU.mult)
        k.act_a.passed(3)
        k.dve_a.passed(1)
        k.pool_a.passed(1)


def log_sigmoid_parts(k, act, dve_mark, act_mark, x, a, n):
    k.act.done(act, act.activation(a, x, ACT.Abs))
    k.act.done(act, act.activation(a, a, ACT.Exp, scale=-1.0))
    return act.activation(a, a, ACT.Ln, bias=1.0)


def fox(k, q, key, v, f):
    nc = k.nc
    H = 8
    with ExitStack() as ctx:
        def sb(name, shape):
            return ctx.enter_context(nc.sbuf_tensor(f"fox_{name}", shape, F32))

        one, lf, c = sb("one_hot", [H, H, P]), sb("log_f", [H, S]), sb("minus_c", [H, S])
        with nc.Block() as block:
            @block.scalar
            def _(act):
                act.preload_act_table_set("natural_log_exp_and_others")
                act.activation(f, f, ACT.Identity, bias=k.fox_bias[:]).then_inc(k.act_a.sem, 1)
                act.wait_ge(*k.act_a.after(1))
                log_sigmoid_parts(k, act, None, None, f, lf[:], 1).then_inc(k.act_a.sem, 1)

            @block.gpsimd
            def _(pool):
                pool.tensor_copy(one[:], k.ident[0:H, 0:H].unsqueeze(2).to_broadcast([H, H, P]))

            @block.tensor
            def _(pe):
                keep_warm(k, pe, 10, 7)

            @block.vector
            def _(dve):
                dve.tensor_scalar(q, q, HD ** -0.5, None, ALU.mult)
                dve.wait_ge(*k.act_a.after(2))
                k.dve.done(dve, dve.scalar_tensor_tensor(out=f, in0=f, scalar=0.0, in1=lf[:], op0=ALU.min,
                                                         op1=ALU.subtract))
                k.dve.done(dve, dve.tensor_scalar(f, f, -1.0, None, ALU.mult))
                dve.tensor_tensor_scan(c[:], k.ones[0:H, :], f, 0.0, ALU.mult, ALU.add)
        k.act_a.passed(2)

        def unit(h):
            r = slice(HD * (h % 2), HD * (h % 2) + HD)
            return dict(q=lambda t: q[r, h // 2, P * t:P * t + P], kT=key[r, h // 2, :],
                        v=lambda s: v[:, s, HD * h:HD * h + HD], bias=k.causal, extra=(one[:, h, :], c))

        softmax_attention(k, [dict(head=h, units=[unit(h)]) for h in range(H)], NH, fill=(4, 2, 0))


def even_layer(k, loads, between):
    with ExitStack() as ctx:
        def sb(name, shape):
            return ctx.enter_context(k.nc.sbuf_tensor(f"ev_{name}", shape, F32))

        qa, fa, qb, kb = (sb(n, [P, NH, S]) for n in ("qa", "fa", "qb", "kb"))
        ia, ga, vb = (sb(n, [P, TT, HALF]) for n in ("ia", "ga", "vb"))
        fb = sb("fb", [8, S])

        def feature(dst):
            return "feature", lambda m: dst[:, m, :], HALF

        def token(dst):
            return "token", lambda t: dst[:, t, :], HALF

        product(k, "ev_in", KD, [feature(qa), feature(fa), token(ia), token(ga), feature(qb), feature(kb),
                                 token(vb), ("feature", lambda m: fb[:], 8)], loads=loads)
        between()
        hgrn(k, qa[:], fa[:], ia, ga[:])
        fox(k, qb[:], kb, vb, fb[:])
        transpose_mix(k, range(NH))



def rg_lru(k, xr, gr, meanwhile):
    nc, ps, w = k.nc, k.ps, k.w
    with ExitStack() as ctx:
        def sb(name, shape):
            return ctx.enter_context(nc.sbuf_tensor(f"lru_{name}", shape, F32))

        pad = sb("padded", [P, NH, S + 3])
        xc, a, u, r = (sb(n, [P, NH, S]) for n in ("xc", "a", "u", "r"))
        ig, th, g3 = (sb(n, [P, NH, S]) for n in ("ig", "th", "g3"))
        wa, wx = sb("wa", [P, NH, HD]), sb("wx", [P, NH, HD])
        sp8, sl = sb("sp8", [P, NH]), sb("sl", [P, NH])
        col = {n: k.cols[:, PARAM_AT[n]:PARAM_AT[n] + 4] for n in
               ("od_conv_b", "od_gate_a_b", "od_gate_x_b", "od_lru_lambda")}
        cw = k.cols[:, PARAM_AT["od_conv_w"]:PARAM_AT["od_conv_w"] + 16]
        lam = col["od_lru_lambda"]
        with nc.Block() as block:
            @block.sync
            def _(sp):
                sp.dma_start(wa[:], w["od_gate_a_w"][0].rearrange("(t n) i j -> (n i) t j", n=2)).then_inc(k.loaded.sem, 16)
                sp.dma_start(wx[:], w["od_gate_x_w"][0].rearrange("(t n) i j -> (n i) t j", n=2)).then_inc(k.loaded.sem, 16)

            @block.gpsimd
            def _(pool):
                pool.memset(pad[:, :, 0:3], 0.0)
                pool.tensor_copy(pad[:, :, 3:S + 3], xr).then_inc(k.pool_a.sem, 1)

            @block.scalar
            def _(act):
                act.preload_act_table_set("natural_log_exp_and_others")
                log_sigmoid_parts(k, act, None, None, lam, sl[:], 0).then_inc(k.act_a.sem, 1)
                for n in range(2 * NH):
                    t, which = n // 2, n % 2
                    act.wait_ge(*k.pe_a.after(n + 1))
                    act.activation((ig if which else r)[:, t, :], ps[:, n, 0:S], ACT.Sigmoid,
                                   bias=(col["od_gate_x_b"] if which else col["od_gate_a_b"])[:, t:t + 1])\
                       .then_inc(k.act_b.sem, 1)
                act.wait_ge(*k.dve_b.after(1))
                act.wait_ge(*k.act_b.after(2 * NH))
                for t in range(NH):
                    act.activation(a[:, t, :], r[:, t, :], ACT.Exp, scale=sp8[:, t:t + 1]).then_inc(k.act_b.sem, 1)
                act.wait_ge(*k.dve_b.after(2))
                for t in range(NH):
                    act.activation(th[:, t, :], u[:, t, :], ACT.Tanh).then_inc(k.act_b.sem, 1)
                act.wait_ge(*k.pool_b.after(1))
                act.activation(g3[:], g3[:], ACT.Tanh, scale=0.7978845608028654).then_inc(k.act_b.sem, 1)
                act.wait_ge(*k.dve_b.after(3))
                act.activation(u[:], u[:], ACT.Sqrt).then_inc(k.act_b.sem, 1)
                act.wait_ge(*k.dve_b.after(4))
                act.activation(k.act_hi[:, 0:NH, :], g3[:], ACT.Copy).then_inc(k.act_b.sem, 1)

            @block.tensor
            def _(pe):
                keep_warm(k, pe, 18, 7)
                pe.wait_ge(*k.loaded.after(32))
                pe.wait_ge(*k.dve_a.after(1))
                for n in range(2 * NH):
                    t, mat = n // 2, (wx if n % 2 else wa)
                    for b in range(2):
                        rows = slice(HD * b, HD * b + HD)
                        ins = pe.matmul(ps[rows, n, 0:S], mat[rows, t, :], xc[rows, t, :], start=True, stop=True)
                    ins.then_inc(k.pe_a.sem, 1)
                pe.wait_ge(*k.act_b.after(2 * NH))
                keep_warm(k, pe, 24, 7)

            @block.vector
            def _(dve):
                dve.wait_ge(*k.pool_a.after(1))
                for t in range(NH):
                    ins = dve.tensor_scalar(xc[:, t, :], pad[:, t, 0:S], cw[:, t:t + 1], col["od_conv_b"][:, t:t + 1],
                                            ALU.mult, ALU.add)
                k.dve.done(dve, ins)
                for j in range(1, 4):
                    for t in range(NH):
                        ins = dve.scalar_tensor_tensor(out=xc[:, t, :], in0=pad[:, t, j:j + S],
                                                       scalar=cw[:, 4 * j + t:4 * j + t + 1], in1=xc[:, t, :],
                                                       op0=ALU.mult, op1=ALU.add)
                    k.dve.done(dve, ins)
                dve.sem_inc(k.dve_a.sem, 1)
                dve.wait_ge(*k.act_a.after(1))
                k.dve.done(dve, dve.scalar_tensor_tensor(out=sp8[:], in0=lam, scalar=0.0, in1=sl[:], op0=ALU.min,
                                                         op1=ALU.subtract))
                k.dve.done(dve, dve.tensor_scalar(sp8[:], sp8[:], 8.0, None, ALU.mult))
                dve.sem_inc(k.dve_b.sem, 1)
                k.dve.done(dve, dve.tensor_scalar(sl[:], sp8[:], -1.0, None, ALU.mult))
                dve.wait_ge(*k.act_b.after(2 * NH))
                for t in range(NH):
                    ins = dve.tensor_scalar(u[:, t, :], r[:, t, :], sl[:, t:t + 1], None, ALU.mult)
                ins.then_inc(k.dve_b.sem, 1)
                dve.wait_ge(*k.act_b.after(4 * NH))
                k.dve.done(dve, dve.tensor_tensor(u[:], a[:], a[:], ALU.mult))
                k.dve.done(dve, dve.scalar_tensor_tensor(out=u[:], in0=u[:], scalar=1.0, in1=th[:], op0=ALU.add,
                                                         op1=ALU.mult))
                dve.sem_inc(k.dve_b.sem, 1)
                k.dve.done(dve, dve.tensor_tensor(ig[:], ig[:], xc[:], ALU.mult))
                dve.wait_ge(*k.act_b.after(4 * NH + 2))
                k.dve.done(dve, dve.tensor_tensor(u[:], u[:], ig[:], ALU.mult))
                for t in range(NH):
                    ins = dve.tensor_tensor_scan(xc[:, t, :], a[:, t, :], u[:, t, :], 0.0, ALU.mult, ALU.add)
                k.dve.done(dve, ins)
                k.dve.done(dve, dve.scalar_tensor_tensor(out=g3[:], in0=g3[:], scalar=1.0, in1=gr, op0=ALU.add,
                                                         op1=ALU.mult))
                dve.scalar_tensor_tensor(out=g3[:], in0=g3[:], scalar=0.5, in1=xc[:], op0=ALU.mult,
                                         op1=ALU.mult).then_inc(k.dve_b.sem, 1)
                dve.wait_ge(*k.act_b.after(4 * NH + 3))
                dve.tensor_tensor(k.act_lo[:, 0:NH, :], g3[:], k.act_hi[:, 0:NH, :].bitcast(F32), ALU.subtract)

            @block.gpsimd
            def _(pool):
                k.pool.done(pool, pool.tensor_tensor(g3[:], gr, gr, ALU.mult))
                k.pool.done(pool, pool.tensor_scalar(g3[:], g3[:], 0.044715, 1.0, ALU.mult, ALU.add))
                pool.tensor_tensor(g3[:], g3[:], gr, ALU.mult).then_inc(k.pool_b.sem, 1)
                meanwhile(pool)
        k.loaded.passed(32)
        k.pool_a.passed(1)
        k.pool_b.passed(1)
        k.pe_a.passed(2 * NH)
        k.act_a.passed(1)
        k.act_b.passed(4 * NH + 3)
        k.dve_a.passed(1)
        k.dve_b.passed(4)


def stick_masks(k, pool, q, minus, shut, tri):
    k.pool.done(pool, pool.tensor_scalar(q, q, HD ** -0.5, None, ALU.mult))
    pool.memset(minus[:], -1.0)
    pool.memset(shut[:], 0.0)
    k.pool.done(pool, pool.memset(tri[:], 1.0))
    for c in (0, 2 * P):
        for buf, fill in ((minus, 0.0), (shut, NEG)):
            pool.affine_select(out=buf[:, c:c + P], in_=buf[:, c:c + P], compare_op=ALU.is_gt, fill=fill,
                               base=0, pattern=[[1, P]], channel_multiplier=-1)
    pool.affine_select(out=tri[:], in_=tri[:], compare_op=ALU.is_ge, fill=0.0, base=0,
                       pattern=[[-1, P]], channel_multiplier=1)


def stick_breaking(k, q, key, v, minus, shut, tri):
    nc, ps = k.nc, k.ps
    H = 8
    W = 3 * P
    with ExitStack() as ctx:
        def sb(name, shape):
            return ctx.enter_context(nc.sbuf_tensor(f"stick_{name}", shape, F32))

        la, lom, lw, wt = (sb(n, [P, 2, W]) for n in ("la", "lom", "lw", "wt"))
        with nc.Block() as block:
            @block.tensor
            def _(pe):
                def rows(h):
                    return slice(HD * (h % 2), HD * (h % 2) + HD)

                def scores(h):
                    if h >= 4:
                        pe.wait_ge(*k.logits_ready.after(h - 3))
                    r, b = rows(h), ps[:, h % 4, :]
                    pe.matmul(b[:, 0:S], key[r, h // 2, 0:P], q[r, h // 2, :], start=True, stop=True)
                    pe.matmul(b[:, S:W], key[r, h // 2, P:S], q[r, h // 2, P:S], start=False, stop=True,
                              skip_group_check=True)\
                      .then_inc(k.scores_ready.sem, 1)

                def suffix(h):
                    pe.wait_ge(*k.dve_a.after(h + 1))
                    b, x = ps[:, h % 4, :], lom[:, h % 2, :]
                    pe.matmul(b[:, 0:S], tri[:], x[:, 0:S], start=False, stop=False, skip_group_check=True)
                    pe.matmul(b[:, P:S], k.ones[:, 0:P], x[:, S:W], start=False, stop=False, skip_group_check=True)
                    pe.matmul(b[:, S:W], tri[:], x[:, S:W], start=False, stop=True, skip_group_check=True)\
                      .then_inc(k.pe_a.sem, 1)

                def values(h):
                    pe.wait_ge(*k.probs_ready.after(h + 1))
                    if h >= 4:
                        pe.wait_ge(*k.heads_done.after(h // 2 - 1))
                    o = ps[rows(h), 6 + h // 2 % 2, :]
                    pe.matmul(o[:, 0:S], v[:, 0, HD * h:HD * h + HD], wt[:, h % 2, 0:S], start=True, stop=False)
                    pe.matmul(o[:, P:S], v[:, 1, HD * h:HD * h + HD], wt[:, h % 2, S:W], start=False, stop=True)\
                      .then_inc(k.heads_ready.sem, 1)

                for i in range(H + 2):
                    if i < H:
                        scores(i)
                    if i < 2:
                        keep_warm(k, pe, (4, 2)[i], 7)
                    if 1 <= i <= H:
                        suffix(i - 1)
                    if i >= 2:
                        values(i - 2)

            @block.scalar
            def _(act):
                act.preload_act_table_set("natural_log_exp_and_others")

                def softplus_part(h):
                    act.wait_ge(*k.scores_ready.after(h + 1))
                    if h >= 2:
                        act.wait_ge(*k.dve_a.after(h - 1))
                    log_sigmoid_parts(k, act, None, None, ps[:, h % 4, 0:W], la[:, h % 2, :], 0)\
                        .then_inc(k.act_a.sem, 1)

                def weights(h):
                    act.wait_ge(*k.logits_ready.after(h + 1))
                    if h >= 2:
                        act.wait_ge(*k.heads_ready.after(h - 1))
                    act.activation(wt[:, h % 2, :], lw[:, h % 2, :], ACT.Exp).then_inc(k.probs_ready.sem, 1)

                for i in range(H + 2):
                    if i < H:
                        softplus_part(i)
                    if 1 <= i <= H:
                        weights(i - 1)
                    if i >= 3 and i % 2:
                        pair = (i - 3) // 2
                        act.wait_ge(*k.heads_ready.after(2 * pair + 2))
                        act.activation(k.act_hi[:, NH + pair], ps[:, 6 + pair % 2, 0:S], ACT.Copy)\
                           .then_inc(k.act_b.sem, 1)

            @block.vector
            def _(dve):
                def break_part(h):
                    dve.wait_ge(*k.act_a.after(h + 1))
                    if h >= 2:
                        dve.wait_ge(*k.pe_a.after(h - 1))
                    x = lom[:, h % 2, :]
                    k.dve.done(dve, dve.scalar_tensor_tensor(out=x, in0=ps[:, h % 4, 0:W], scalar=0.0,
                                                             in1=la[:, h % 2, :], op0=ALU.max, op1=ALU.add))
                    dve.tensor_tensor(x, x, minus[:], ALU.mult).then_inc(k.dve_a.sem, 1)

                def close(h):
                    dve.wait_ge(*k.pe_a.after(h + 1))
                    if h >= 2:
                        dve.wait_ge(*k.probs_ready.after(h - 1))
                    dve.tensor_tensor(lw[:, h % 2, :], ps[:, h % 4, 0:W], shut[:], ALU.add)\
                       .then_inc(k.logits_ready.sem, 1)

                def finish(pair):
                    dve.wait_ge(*k.act_b.after(pair + 1))
                    dve.tensor_tensor(k.act_lo[:, NH + pair], ps[:, 6 + pair % 2, 0:S],
                                      k.act_hi[:, NH + pair].bitcast(F32), ALU.subtract).then_inc(k.heads_done.sem, 1)

                for i in range(H + 2):
                    if 1 <= i <= H:
                        close(i - 1)
                    if i < H:
                        break_part(i)
                    if i >= 3 and i % 2:
                        finish((i - 3) // 2)
        for mark in (k.scores_ready, k.dve_a, k.pe_a, k.act_a, k.probs_ready, k.heads_ready, k.logits_ready):
            mark.passed(H)
        k.act_b.passed(H // 2)
        k.heads_done.passed(H // 2)


def odd_layer(k, before):
    with ExitStack() as ctx:
        def sb(name, shape):
            return ctx.enter_context(k.nc.sbuf_tensor(f"od_{name}", shape, F32))

        xr, gr, qd, kd = (sb(n, [P, NH, S]) for n in ("xr", "gr", "qd", "kd"))
        vd = sb("vd", [P, TT, HALF])

        def feature(dst):
            return "feature", lambda m: dst[:, m, :], HALF

        product(k, "od_in", KD, [feature(xr), feature(gr), feature(qd), feature(kd),
                                       ("token", lambda t: vd[:, t, :], HALF)], before)
        minus, shut, tri = sb("minus", [P, 3 * P]), sb("shut", [P, 3 * P]), sb("tri", [P, P])
        rg_lru(k, xr[:], gr[:], lambda pool: stick_masks(k, pool, qd[:], minus, shut, tri))
        stick_breaking(k, qd[:], kd, vd, minus, shut, tri)


def first_block(k):
    sb = k.nc.sbuf_tensor
    with ExitStack() as ctx:
        rows, rows2 = (ctx.enter_context(sb(n, [P, P], F32)) for n in ("param_rows", "param_rows2"))
        table, rel, bias = (ctx.enter_context(sb(n, shape, F32)) for n, shape in (
            ("bias_table", [32 + MASK_SETS, 3 * P]), ("bias_rel", [32 + MASK_SETS, BIAS_HEADS]),
            ("bias_rows", [BIAS_HEADS, 3 * P])))
        loads = param_loads(k, rows, rows2, table, rel)
        begin(k)
        even_layer(k, loads, lambda: parameters(k, rows, rows2, table, rel, bias, len(loads)))
    out_product(k, "ev_out", KD)
    feed_forward(k, "ffn0", dict(residual=(ALPHA, 1.0), layer_norm=(0, 0)))
    odd_layer(k, dict(residual=(ALPHA, 1.0), layer_norm=(0, 1)))
    out_product(k, "od_out", KD)
    feed_forward(k, "ffn1", dict(residual=(ALPHA, 1.0), layer_norm=(1, 0)))



DELTA = np.arange(3 * P) - (P - 1)
MASK_SETS = 5
BIAS_HEADS = 12 + 8 + 8


def bias_tables():
    n = np.maximum(DELTA, 0)
    nf = np.maximum(n, 1).astype(np.float32)
    large = 16 + (np.log(nf / np.float32(16)) / np.float32(np.log(2048 / 16)) * np.float32(16)).astype(np.int32)
    bucket = np.where(n < 16, n, np.minimum(large, 31))
    one = ((np.arange(32)[:, None] == bucket) & (DELTA >= 0)).astype(np.float32)
    causal = DELTA >= 0
    valid = np.stack([causal & (DELTA <= 128), causal & (DELTA % 4 == 0), causal & (DELTA % 16 == 0),
                      causal & (DELTA < 128), causal])
    return np.concatenate([one, np.where(valid, 0.0, NEG).astype(np.float32)])


def bias_sets():
    of = [0] * 4 + [1] * 4 + [2] * 4 + [3] * 8 + [4] * 8
    return (np.arange(MASK_SETS)[:, None] == np.array(of)).astype(np.float32)


SEL, BLK, CNEG, COK, COS, SIN, SMALL = 0, 128, 136, 168, 200, 232, 264


def small_tables():
    out = np.zeros((P, SMALL), np.float32)
    p = np.arange(P)
    out[0:16, SEL:SEL + P] = np.arange(16)[:, None] == p % 16
    out[:, BLK:BLK + 8] = p[:, None] // 16 == np.arange(8)
    end = np.arange(16) * CMP_STRIDE + CMP_LEN - 1
    inv = np.power(np.float32(10000.0), -np.arange(16, dtype=np.float32) / np.float32(16))
    for t in range(TT):
        ok = end[None, :] <= (P * t + p)[:, None]
        out[:, CNEG + 16 * t:CNEG + 16 * t + 16] = np.where(ok, 0.0, NEG)
        out[:, COK + 16 * t:COK + 16 * t + 16] = ok
        angle = (P * t + p).astype(np.float32)[:, None] * inv[None, :]
        out[:, COS + 16 * t:COS + 16 * t + 16] = np.cos(angle)
        out[:, SIN + 16 * t:SIN + 16 * t + 16] = np.sin(angle)
    return out


def load_bias(k, eng, dst, first, n):
    eng.wait_ge(*k.bias_stored.after(16))
    src = bass.AP(k.bias_dram.tensor, first * 3 * P, [[1, P], [3 * P, n], [1, S]])
    eng.dma_start(dst, src).then_inc(k.bias_loaded.sem, 16)


def forwards(bias, head):
    x = bias[:, head, :]
    return bass.AP(x.tensor, x.offset + S - 1, [x.ap[0], [-1, S]])


def mla(k, z):
    nc, ps, w = k.nc, k.ps, k.w
    H, QK = MLA_H, MLA_QK
    with ExitStack() as ctx:
        def sb(name, shape):
            return ctx.enter_context(nc.sbuf_tensor(f"mla_{name}", shape, F32))

        qT, kT = sb("qT", [QK, H, S]), sb("kT", [QK, H, S])
        kv = sb("kv", [P, TT, H, P])
        with ExitStack() as inner:
            def sbi(name, shape):
                return inner.enter_context(nc.sbuf_tensor(f"mla_{name}", shape, F32))

            cn, cT = sbi("latent", [P, TT, 3 * P]), sbi("latent_T", [P, 3, S])
            qk, sq = sbi("qk", [P, 2, TT, H, QK]), sbi("sq", [P, 2, TT, H, QK])
            ss = sbi("ss", [P, 4])
            s2 = sbi("s2", [P, 2 * TT * H])
            gains = sbi("gains", [P, 2, QK])
            rot = sq[:].rearrange("p w t h d -> p (w t h d)")[:, 0:2 * 4 * TT * H * 16]\
                .rearrange("p (w i t h d) -> p w i t h d", w=2, i=4, t=TT, h=H)
            lat = ((0, 256), (256, 384))
            with nc.Block() as block:
                @block.sync
                def _(sp):
                    sp.dma_start(gains[:, 0], w["mla_q_norm_2"].to_broadcast([P, QK])).then_inc(k.loaded.sem, 16)
                    sp.dma_start(gains[:, 1], w["mla_k_norm_2"].to_broadcast([P, QK])).then_inc(k.loaded.sem, 16)

                @block.scalar
                def _(act):
                    for t in range(TT):
                        for i, (a, b) in enumerate(lat):
                            act.activation(cn[:, t, a:b], z[:, t, a:b], ACT.Square,
                                           scale=(b - a) ** -0.5, accum_out=ss[:, 2 * t + i:2 * t + i + 1])\
                               .then_inc(k.act_a.sem, 1)
                    act.wait_ge(*k.dve_a.after(1))
                    act.activation(ss[:], ss[:], ACT.Sqrt).then_inc(k.act_a.sem, 1)

                @block.vector
                def _(dve):
                    dve.wait_ge(*k.act_a.after(4))
                    dve.tensor_scalar(ss[:], ss[:], EPS_RMS, None, ALU.add).then_inc(k.dve_a.sem, 1)
                    dve.wait_ge(*k.act_a.after(5))
                    k.dve.done(dve, dve.reciprocal(ss[:], ss[:]))
                    for t in range(TT):
                        for i, (a, b) in enumerate(lat):
                            ins = dve.tensor_scalar(cn[:, t, a:b], z[:, t, a:b], ss[:, 2 * t + i:2 * t + i + 1], None,
                                                    ALU.mult)
                    ins.then_inc(k.dve_a.sem, 1)
                    for m in range(3):
                        dve.wait_ge(*k.pe_a.after(m + 1))
                        col = PARAM_AT["mla_q_a_norm_2"] + m
                        dve.tensor_scalar(cT[:, m, :], ps[:, m, 0:S], k.cols[:, col:col + 1], None, ALU.mult)\
                           .then_inc(k.dve_b.sem, 1)

                @block.tensor
                def _(pe):
                    keep_warm(k, pe, 10, 7)
                    pe.wait_ge(*k.dve_a.after(2))
                    for m in range(3):
                        for t in range(TT):
                            ins = pe.transpose(ps[:, m, P * t:P * t + P], cn[:, t, P * m:P * m + P], k.ident[:])
                        ins.then_inc(k.pe_a.sem, 1)
            k.act_a.passed(5)
            k.dve_a.passed(2)
            k.dve_b.passed(3)
            k.pe_a.passed(3)

            j = k.first["mla_b"]
            wq, wkv = k.slot_view(j, 2, 768), k.slot_view(j, 1, D, 1536)
            with nc.Block() as block:
                @block.tensor
                def _(pe):
                    pe.wait_ge(k.weights_in[j % SLOTS], k.arrived[j])
                    for t in range(TT):
                        for i, (a, b) in enumerate(((0, BANK), (BANK, 768))):
                            for m in range(2):
                                ins = pe.matmul(ps[:, 4 * t + i, 0:b - a], cT[:, m, P * t:P * t + P], wq[:, m, a:b],
                                                start=m == 0, stop=m == 1)
                        for i in range(2):
                            ins = pe.matmul(ps[:, 4 * t + 2 + i, :], cT[:, 2, P * t:P * t + P],
                                            wkv[:, 0, BANK * i:BANK * i + BANK], start=True, stop=True)
                        if t == 0:
                            ins.then_inc(k.pe_a.sem, 1)
                    ins.then_inc(k.weights_used, 1)

                @block.vector
                def _(dve):
                    for t in range(TT):
                        if t == 0:
                            dve.wait_ge(*k.pe_a.after(1))
                        else:
                            dve.wait_ge(k.weights_used, j + 1)
                        q = qk[:, 0, t].rearrange("p h d -> p (h d)")
                        dve.tensor_copy(q[:, 0:BANK], ps[:, 4 * t, :])
                        dve.tensor_copy(q[:, BANK:768], ps[:, 4 * t + 1, 0:256])

                @block.scalar
                def _(act):
                    for t in range(TT):
                        if t == 0:
                            act.wait_ge(*k.pe_a.after(1))
                        else:
                            act.wait_ge(k.weights_used, j + 1)
                        act.activation(kv[:, t], ps[:, 4 * t + 2:4 * t + 4, :].rearrange("p b (h d) -> p (b h) d", d=P),
                                       ACT.Copy)

                @block.gpsimd
                def _(pool):
                    for t in range(TT):
                        pool.tensor_copy(qk[:, 1, t, :, MLA_NOPE:QK], bc(z[:, t, 384:416], 1, H))

                @block.sync
                def _(sp):
                    k.load_weights(sp, j + 1 + SLOTS)
            k.pe_a.passed(1)

            def rotary(k, eng, steps, which):
                small = k.small
                x = qk[:, which, :, :, MLA_NOPE:QK]
                a, b = x[:, :, :, 0:16], x[:, :, :, 16:32]
                cos, sin = (bc(small[:, c:c + 32].rearrange("p (t d) -> p t d", t=TT), 2, H) for c in (COS, SIN))
                r = rot[:, which]
                for i, (u, v) in enumerate(((a, cos), (b, sin), (b, cos), (a, sin))):
                    ins = eng.tensor_tensor(r[:, i], u, v, ALU.mult)
                steps.done(eng, ins)
                eng.tensor_tensor(a, r[:, 0], r[:, 1], ALU.subtract)
                steps.done(eng, eng.tensor_tensor(b, r[:, 2], r[:, 3], ALU.add))

            with nc.Block() as block:
                @block.gpsimd
                def _(pool):
                    k.pool.done(pool, pool.tensor_copy(qk[:, 1, :, :, 0:MLA_NOPE], kv[:, :, :, 0:MLA_NOPE]))
                    pool.sem_inc(k.pool_a.sem, 1)
                    pool.wait_ge(*k.dve_a.after(2))
                    rotary(k, pool, k.pool, 1)
                    pool.sem_inc(k.pool_a.sem, 1)

                @block.scalar
                def _(act):
                    act.activation(sq[:, 0], qk[:, 0], ACT.Square, scale=QK ** -0.5).then_inc(k.act_a.sem, 1)
                    act.wait_ge(*k.pool_a.after(1))
                    act.activation(sq[:, 1], qk[:, 1], ACT.Square, scale=QK ** -0.5).then_inc(k.act_a.sem, 1)
                    act.wait_ge(*k.dve_a.after(1))
                    act.activation(s2[:], s2[:], ACT.Sqrt).then_inc(k.act_a.sem, 1)
                    for n in range(2 * H // 2):
                        which, m = n // (H // 2), n % (H // 2)
                        act.wait_ge(*k.pe_a.after(n + 1))
                        dst = (kT if which else qT)[:, 2 * m:2 * m + 2, :]
                        act.activation(dst, ps[0:QK, n, :].rearrange("p (h s) -> p h s", h=2), ACT.Copy,
                                       scale=1.0 if which else QK ** -0.5).then_inc(k.act_b.sem, 1)

                @block.vector
                def _(dve):
                    dve.wait_ge(*k.act_a.after(2))
                    k.dve.done(dve, dve.tensor_reduce(s2[:], sq[:].rearrange("p w t h d -> p (w t h) d"), AX.X, ALU.add))
                    dve.tensor_scalar(s2[:], s2[:], EPS_RMS, None, ALU.add).then_inc(k.dve_a.sem, 1)
                    dve.wait_ge(*k.act_a.after(3))
                    k.dve.done(dve, dve.reciprocal(s2[:], s2[:]))
                    dve.wait_ge(*k.loaded.after(32))
                    for which in (1, 0):
                        x = qk[:, which].rearrange("p t h d -> p (t h) d")
                        n = TT * H
                        k.dve.done(dve, dve.tensor_tensor(x, x, bc(s2[:, n * which:n * which + n], 2, QK), ALU.mult))
                        k.dve.done(dve, dve.tensor_tensor(x, x, bc(gains[:, which], 1, n), ALU.mult))
                        if which:
                            dve.sem_inc(k.dve_a.sem, 1)
                    rotary(k, dve, k.dve, 0)
                    dve.sem_inc(k.dve_b.sem, 1)

                @block.tensor
                def _(pe):
                    keep_warm(k, pe, 40, 7)
                    pe.wait_ge(*k.dve_b.after(1))
                    for n in range(2 * H // 2):
                        which, m = n // (H // 2), n % (H // 2)
                        if n == H // 2:
                            pe.wait_ge(*k.pool_a.after(2))
                        for h in (2 * m, 2 * m + 1):
                            for t in range(TT):
                                c = S * (h % 2) + P * t
                                ins = pe.transpose(ps[0:QK, n, c:c + P], qk[:, which, t, h, :], k.ident[:])
                        ins.then_inc(k.pe_a.sem, 1)
            k.loaded.passed(32)
            k.pool_a.passed(2)
            k.act_a.passed(3)
            k.act_b.passed(H)
            k.dve_a.passed(2)
            k.dve_b.passed(1)
            k.pe_a.passed(H)

        def unit(h):
            return dict(q=lambda t: qT[:, h, P * t:P * t + P], kT=kT[:, h, :],
                        v=lambda s: kv[:, s, h, MLA_NOPE:P], bias=k.causal)

        softmax_attention(k, [dict(head=h, units=[unit(h)]) for h in range(H)], 0)


def norm_and_flip(k, name, src, n_blocks, q_blocks, dst, tiles, gates=None):
    nc, ps = k.nc, k.ps
    B = n_blocks
    with ExitStack() as ctx:
        def sb(part, shape):
            return ctx.enter_context(nc.sbuf_tensor(f"{name}_{part}", shape, F32))

        sq = sb("sq", [P, TT, B, HD])
        nrm = sb("nrm", [P, TT, 2 * len(tiles), HD])
        rs = sb("rs", [P, TT, B])
        x = src.rearrange("p t (b d) -> p t b d", d=HD)
        runs = []
        for i, (a, b, gain) in enumerate(tiles):
            kind = (b - a, gain is None)
            if runs and runs[-1][2] == kind and a == runs[-1][1] + (2 if b > a else 1) * (i - runs[-1][0]):
                runs[-1][3] += 1
            else:
                runs.append([i, a, kind, 1])
        with nc.Block() as block:
            @block.scalar
            def _(act):
                for t in range(TT):
                    act.activation(sq[:, t], x[:, t], ACT.Square, scale=HD ** -0.5).then_inc(k.act_a.sem, 1)
                act.wait_ge(*k.dve_a.after(1))
                act.activation(rs[:], rs[:], ACT.Sqrt).then_inc(k.act_a.sem, 1)
                for i, (a, b, gain) in enumerate(tiles):
                    if gain is None:
                        continue
                    act.wait_ge(*k.pe_a.after(i + 1))
                    act.activation(dst[:, i, :], ps[:, i % 8, 0:S], ACT.Copy, scale=k.cols2[:, gain:gain + 1])\
                       .then_inc(k.act_b.sem, 1)
                if gates:
                    g = gates.rearrange("p t c -> p t c")
                    act.activation(g, g, ACT.Sigmoid)

            def spread(eng, t, run):
                i, a, (step, raw), n = run
                out = nrm[:, t, 2 * i:2 * i + 2 * n, :]
                wide = (2 if step else 1) * n
                src_x, r = x[:, t, a:a + wide, :], bc(rs[:, t, a:a + wide], 2, HD)
                if not step:
                    out = out.rearrange("p (b u) d -> p b u d", u=2)
                    src_x = bc(src_x, 2, 2)
                    r = bc(r, 2, 2)
                if raw:
                    return eng.tensor_copy(out, src_x)
                return eng.tensor_tensor(out, src_x, r, ALU.mult)

            @block.gpsimd
            def _(pool):
                ins = None
                for run in runs:
                    if run[2][1]:
                        for t in range(TT):
                            ins = spread(pool, t, run)
                if ins is not None:
                    ins.then_inc(k.pool_a.sem, 1)
                pool.wait_ge(*k.dve_a.after(2))
                for run in runs:
                    if not run[2][1]:
                        ins = spread(pool, 1, run)
                ins.then_inc(k.pool_b.sem, 1)

            @block.vector
            def _(dve):
                for t in range(TT):
                    dve.wait_ge(*k.act_a.after(t + 1))
                    ins = dve.tensor_reduce(rs[:, t], sq[:, t], AX.X, ALU.add)
                k.dve.done(dve, ins)
                dve.tensor_scalar(rs[:], rs[:], EPS_RMS, None, ALU.add).then_inc(k.dve_a.sem, 1)
                dve.wait_ge(*k.act_a.after(TT + 1))
                k.dve.done(dve, dve.reciprocal(rs[:], rs[:]))
                for a, b in q_blocks:
                    ins = dve.tensor_scalar(rs[:, :, a:b], rs[:, :, a:b], HD ** -0.5, None, ALU.mult)
                k.dve.done(dve, ins)
                dve.sem_inc(k.dve_a.sem, 1)
                for run in runs:
                    if not run[2][1]:
                        ins = spread(dve, 0, run)
                ins.then_inc(k.dve_a.sem, 1)
                for i, (a, b, gain) in enumerate(tiles):
                    if gain is None:
                        dve.wait_ge(*k.pe_a.after(i + 1))
                        dve.tensor_copy(dst[0:HD, i, :], ps[0:HD, i % 8, 0:S])
                        dve.tensor_copy(dst[HD:P, i, 0:S - 1], ps[HD:P, i % 8, 1:S]).then_inc(k.dve_b.sem, 1)

            @block.tensor
            def _(pe):
                keep_warm(k, pe, 16, 7)
                pe.wait_ge(*k.dve_a.after(3))
                pe.wait_ge(*k.pool_b.after(1))
                raw = [i for i, x in enumerate(tiles) if x[2] is None]
                for i in range(len(tiles)):
                    if raw and i == raw[0]:
                        pe.wait_ge(*k.pool_a.after(1))
                    if i >= 8:
                        if i - 8 in raw:
                            pe.wait_ge(*k.dve_b.after(raw.index(i - 8) + 1))
                        else:
                            pe.wait_ge(*k.act_b.after(i - 8 + 1 - sum(j < i - 8 for j in raw)))
                    for t in range(TT):
                        ins = pe.transpose(ps[:, i % 8, P * t:P * t + P],
                                           nrm[:, t, 2 * i:2 * i + 2, :].rearrange("p b d -> p (b d)"), k.ident[:])
                    ins.then_inc(k.pe_a.sem, 1)
        raw = sum(x[2] is None for x in tiles)
        k.act_a.passed(TT + 1)
        k.act_b.passed(len(tiles) - raw)
        k.dve_a.passed(3)
        k.dve_b.passed(raw)
        k.pe_a.passed(len(tiles))
        k.pool_a.passed(bool(raw))
        k.pool_b.passed(1)


def dilated(k, z, bias):
    with ExitStack() as ctx:
        qkT = ctx.enter_context(k.nc.sbuf_tensor("dil_qkT", [P, 12, S], F32))
        at = 416
        gq, gk = GAIN_AT["dil_q_norm_2"], GAIN_AT["dil_k_norm_2"]
        tiles = [(2 * i, 2 * i + 1, gq if i < 6 else gk) for i in range(12)]
        with k.nc.Block() as block:
            @block.vector
            def _(dve):
                dve.wait_ge(*k.bias_loaded.after(16))
        k.bias_loaded.passed(16)
        norm_and_flip(k, "dil", z[:, :, at:at + 24 * HD], 24, [(0, 12)], qkT, tiles)

        def unit(i):
            r = slice(HD * (i % 2), HD * (i % 2) + HD)
            v0 = at + HD * (24 + i)
            return dict(q=lambda t: qkT[r, i // 2, P * t:P * t + P], kT=qkT[r, 6 + i // 2, :],
                        v=lambda s: z[:, s, v0:v0 + HD], bias=forwards(bias, i))

        softmax_attention(k, [dict(head=h, units=[unit(4 * g + h) for g in range(3)]) for h in range(4)], NH,
                          fill=(6, 4, 3))


def latent_layer(k, before):
    with ExitStack() as ctx:
        z = ctx.enter_context(k.nc.sbuf_tensor("ab_z", [P, TT, 2720], F32))
        bias = ctx.enter_context(k.nc.sbuf_tensor("ab_bias", [P, 12, S], F32))
        with k.nc.Block() as block:
            @block.scalar
            def _(act):
                load_bias(k, act, bias[:], 0, 12)
        pieces = []
        for c in range(0, 2720, BANK):
            n = min(BANK, 2720 - c)
            pieces.append(("token", lambda t, c=c, n=n: z[:, t, c:c + n], n))
        product(k, "ab_in", KD, pieces, before)
        mla(k, z)
        dilated(k, z, bias)



def compressed(k, z, zT, q_tile, gate, vblk, prT):
    nc, ps, w = k.nc, k.ps, k.w
    G, H, C, GC = 2, 8, N_CMP, 2 * N_CMP
    small = k.small
    j = k.first["cmp_w1"]
    with ExitStack() as ctx:
        def sb(name, shape):
            return ctx.enter_context(nc.sbuf_tensor(f"cmp_{name}", shape, F32))

        w2 = sb("w2", [P, 2, HD])
        hb, hid = sb("hidden_bias", [P, 2]), sb("hidden", [P, 2, GC])
        kc, ksq, kss = sb("kc", [GC, 2, HD]), sb("ksq", [GC, HD]), sb("kss", [GC, 1])
        kcT, vc = sb("kcT", [P, G, 2, 16]), sb("vc", [C, G, HD])
        lg, pr = sb("lg", [P, TT, H, C]), sb("pr", [P, TT, H, 16])
        mx, sm = sb("mx", [P, TT, H]), sb("sm", [P, TT, H])
        w1 = [k.slot_view(j, 16, P, 2048 * i) for i in range(2)]
        blocks = sb("blocks", [P, 2, 16, GC + 1])
        with nc.Block() as block:
            @block.sync
            def _(sp):
                sp.dma_start(w2[:], w["nsa_cmp_w2_2"][0].rearrange("a p d -> p a d")).then_inc(k.loaded.sem, 16)
                k.load_weights(sp, j + 1 + SLOTS)

            @block.gpsimd
            def _(pool):
                at = PARAM_AT["nsa_cmp_pos_2"]
                pos = k.cols[:, at:at + 32].rearrange("p (i l) -> p i l", i=2)
                for i in range(2):
                    for g in range(G):
                        x = zT[:, 14 + 2 * i + g, 0:2 * CMP_STRIDE * (C // 2 + 1)]
                        src = bass.AP(x.tensor, x.offset, [x.ap[0], [2, 16], [CMP_STRIDE, C]])
                        pool.tensor_copy(blocks[:, i, :, C * g:C * g + C], src)
                pool.tensor_copy(blocks[:, :, :, GC], pos).then_inc(k.pool_b.sem, 1)
                pool.memset(pr[:], 0.0)
                pool.memset(kcT[:], 0.0).then_inc(k.pool_a.sem, 1)

            @block.tensor
            def _(pe):
                pe.wait_ge(k.weights_in[j % SLOTS], k.arrived[j])
                for i in range(2):
                    if i == 0:
                        keep_warm(k, pe, 8, 7)
                        pe.wait_ge(*k.pool_b.after(1))
                    for l in range(16):
                        ins = pe.matmul(ps[:, i, 0:4 * (GC + 1)].rearrange("p (r n) -> p r n", r=4), w1[i][:, l, :],
                                        bc(blocks[:, i, l, :], 1, 4), start=l == 0, stop=l == 15)
                    if i == 0:
                        ins.then_inc(k.pe_a.sem, 1)
                ins.then_inc(k.weights_used, 1)
                pe.wait_ge(*k.act_a.after(2))
                pe.wait_ge(*k.loaded.after(16))
                pe.matmul(ps[0:GC, 4, 0:HD], hid[:, 0, :], w2[:, 0, :], start=True, stop=True).then_inc(k.pe_a.sem, 1)
                for g in range(G):
                    ins = pe.matmul(ps[0:C, 5, HD * g:HD * g + HD], hid[:, 1, C * g:C * g + C], w2[:, 1, :],
                                    start=True, stop=True)
                ins.then_inc(k.pe_a.sem, 1)
                pe.wait_ge(*k.dve_b.after(1))
                pe.matmul(ps[:, 6, 0:P], small[0:C, SEL:SEL + P], vc[:].rearrange("c g d -> c (g d)"),
                          start=True, stop=True).then_inc(k.pe_a.sem, 1)
                pe.wait_ge(*k.dve_b.after(2))
                pe.transpose(ps[:, 7, 0:GC], kc[:].rearrange("c u d -> c (u d)"), k.ident[0:GC, 0:GC])\
                  .then_inc(k.pe_a.sem, 1)
                pe.wait_ge(*k.act_b.after(1))
                for t in range(TT):
                    for h in range(0, H, 2):
                        c = (t * H + h) * 16
                        ins = pe.matmul(ps[:, 0, c:c + 32], zT[:, q_tile + h // 2, P * t:P * t + P],
                                        kcT[:, h // (H // G)].rearrange("p u c -> p (u c)"), start=True, stop=True)
                ins.then_inc(k.pe_a.sem, 1)
                pe.wait_ge(*k.dve_b.after(3))
                for t in range(TT):
                    ins = pe.transpose(ps[:, 4, P * t:P * t + P], pr[:, t].rearrange("p h c -> p (h c)"), k.ident[:])
                ins.then_inc(k.pe_a.sem, 1)

            @block.scalar
            def _(act):
                for i in range(2):
                    act.wait_ge(*k.dve_a.after(i + 1))
                    act.activation(hid[:, i, :], ps[:, i, 0:GC], ACT.Gelu_apprx_tanh, bias=hb[:, i:i + 1])\
                       .then_inc(k.act_a.sem, 1)
                act.wait_ge(*k.dve_a.after(3))
                act.activation(kss[:], kss[:], ACT.Sqrt).then_inc(k.act_a.sem, 1)
                act.wait_ge(*k.pe_a.after(5))
                gain = GAIN_AT["nsa_k0"]
                act.wait_ge(*k.pool_a.after(1))
                for u in range(2):
                    r = slice(HD * u, HD * u + HD)
                    ins = act.activation(kcT[r, :, u, 0:C], ps[r, 7, 0:GC].rearrange("p (g c) -> p g c", g=G), ACT.Copy,
                                         scale=k.cols2[r, gain:gain + 1])
                ins.then_inc(k.act_b.sem, 1)
                act.wait_ge(*k.dve_a.after(4))
                act.activation(lg[:], lg[:], ACT.Exp).then_inc(k.act_a.sem, 1)

            @block.vector
            def _(dve):
                for i in range(2):
                    if i == 0:
                        dve.wait_ge(*k.pe_a.after(1))
                    else:
                        dve.wait_ge(k.weights_used, j + 1)
                    dve.tensor_copy(hb[:, i:i + 1], ps[:, i, GC:GC + 1]).then_inc(k.dve_a.sem, 1)
                dve.wait_ge(*k.pe_a.after(2))
                key = ps[0:GC, 4, 0:HD]
                k.dve.done(dve, dve.tensor_copy(kc[:, 0, :], key))
                k.dve.done(dve, dve.scalar_tensor_tensor(out=ksq[:], in0=kc[:, 0, :], scalar=1.0 / HD, in1=kc[:, 0, :],
                                                         op0=ALU.mult, op1=ALU.mult, accum_out=kss[:]))
                dve.tensor_scalar(kss[:], kss[:], EPS_RMS, None, ALU.add).then_inc(k.dve_a.sem, 1)
                dve.wait_ge(*k.pe_a.after(3))
                dve.tensor_copy(vc[:], ps[0:C, 5, 0:G * HD].rearrange("c (g d) -> c g d", g=G)).then_inc(k.dve_b.sem, 1)
                dve.wait_ge(*k.act_a.after(3))
                k.dve.done(dve, dve.reciprocal(kss[:], kss[:]))
                for u in range(2):
                    ins = dve.tensor_scalar(kc[:, u, :], key, kss[:, 0:1], None, ALU.mult)
                ins.then_inc(k.dve_b.sem, 1)
                dve.wait_ge(*k.pe_a.after(4))
                for g in range(G):
                    n = H // G
                    rep = bc(ps[:, 6, HD * g:HD * g + HD], 1, n)
                    dve.tensor_tensor(vblk[:, n * g:n * g + n, :], rep,
                                      bc(small[:, BLK + n * g:BLK + n * g + n], 2, HD), ALU.mult)
                dve.wait_ge(*k.pe_a.after(6))
                dve.wait_ge(*k.pool_a.after(1))
                neg, ok = (small[:, c:c + 32].rearrange("p (t c) -> p t c", t=TT)[:, :, 0:C] for c in (CNEG, COK))
                flat = lg[:].rearrange("p t h c -> p (t h) c")
                mxf, smf = mx[:].rearrange("p t h -> p (t h)"), sm[:].rearrange("p t h -> p (t h)")
                logits = ps[:, 0, 0:S].rearrange("p (t h c) -> p t h c", t=TT, h=H)[:, :, :, 0:C]
                ins = dve.tensor_tensor(lg[:], logits, bc(neg, 2, H), ALU.add)
                k.dve.done(dve, ins)
                k.dve.done(dve, dve.tensor_reduce(mxf, flat, AX.X, ALU.max))
                dve.tensor_tensor(flat, flat, bc(mxf, 2, C), ALU.subtract).then_inc(k.dve_a.sem, 1)
                dve.wait_ge(*k.act_a.after(4))
                k.dve.done(dve, dve.tensor_tensor(lg[:], lg[:], bc(ok, 2, H), ALU.mult))
                k.dve.done(dve, dve.tensor_reduce(smf, flat, AX.X, ALU.add))
                k.dve.done(dve, dve.tensor_scalar(smf, smf, 1e-30, None, ALU.max))
                k.dve.done(dve, dve.reciprocal(smf, smf))
                k.dve.done(dve, dve.tensor_tensor(sm[:], sm[:], gate, ALU.mult))
                dve.tensor_tensor(pr[:, :, :, 0:C].rearrange("p t h c -> p (t h) c"), flat, bc(smf, 2, C), ALU.mult)\
                   .then_inc(k.dve_b.sem, 1)
                dve.wait_ge(*k.pe_a.after(7))
                dve.tensor_copy(prT[:], ps[:, 4, 0:S])
    k.loaded.passed(16)
    k.pool_a.passed(1)
    k.pool_b.passed(1)
    k.pe_a.passed(7)
    k.act_a.passed(4)
    k.act_b.passed(1)
    k.dve_a.passed(4)
    k.dve_b.passed(3)


def sparse_layer(k, before):
    nc, w = k.nc, k.w
    assert S // 64 <= 16
    with ExitStack() as ctx:
        def sb(name, shape):
            return ctx.enter_context(nc.sbuf_tensor(f"cd_{name}", shape, F32))

        z = sb("z", [P, TT, 2072])
        bias = sb("bias", [P, 16, S])
        sink = sb("sink", [P, 2, 8])
        pieces = []
        for c in range(0, 2072, BANK):
            n = min(BANK, 2072 - c)
            pieces.append(("token", lambda t, c=c, n=n: z[:, t, c:c + n], n))
        with nc.Block() as block:
            @block.scalar
            def _(act):
                load_bias(k, act, bias[:], 12, 16)
                act.dma_start(sink[:, 0, :], w["swa_sinks_2"].to_broadcast([P, 8])).then_inc(k.bias_loaded.sem, 16)
        product(k, "cd_in", KD, pieces, before)
        with nc.Block() as block:
            @block.vector
            def _(dve):
                dve.wait_ge(*k.bias_loaded.after(32))
                dve.tensor_scalar(sink[:, 1, :], sink[:, 0, :], -1.0, None, ALU.mult)
        k.bias_loaded.passed(32)
        zT = sb("zT", [P, 18, S])
        g = GAIN_AT
        tiles = ([(2 * i, 2 * i + 1, g["swa_q_norm_2"]) for i in range(4)]
                 + [(8 + i, 8 + i, g["swa_k_norm_2"]) for i in range(2)]
                 + [(12 + 2 * i, 13 + 2 * i, g["nsa_q_norm_2"]) for i in range(4)]
                 + [(24 + i, 24 + i, g["nsa_k1"]) for i in range(2)]
                 + [(28 + i, 28 + i, g["nsa_k2"]) for i in range(2)]
                 + [(20 + i, 20 + i, None) for i in range(4)])
        gates = z[:, :, 2048:2072]
        norm_and_flip(k, "cd", z[:, :, 0:2048], 32, [(0, 8), (12, 20)], zT, tiles, gates=gates)
        G4 = 4

        def unit(h, q_tile, k_tile, v_block, bias_at):
            r = slice(HD * (h % 2), HD * (h % 2) + HD)
            v0 = HD * (v_block + h // G4)
            return dict(q=lambda t: zT[r, q_tile + h // 2, P * t:P * t + P], kT=zT[r, k_tile + h // G4, :],
                        v=lambda s: z[:, s, v0:v0 + HD], bias=forwards(bias, bias_at + h))

        def gate(branch):
            return gates.rearrange("p t (h b) -> p t h b", b=3)[:, :, :, branch]

        H = 8
        softmaxes = [dict(head=h, units=[unit(h, 0, 4, 10, 0)], sink=(sink[:, 0, h:h + 1], sink[:, 1, h:h + 1]))
                     for h in range(H)]
        for h in range(H):
            for branch, k_tile, v_block in ((1, 10, 26), (2, 12, 30)):
                softmaxes.append(dict(head=H + h, units=[unit(h, 6, k_tile, v_block, 8)],
                                      gate=gate(branch)[:, :, h]))
        vblk, prT = sb("cmp_values", [P, H, HD]), sb("cmp_probs_T", [P, TT * P])
        compressed(k, z, zT, 6, gate(0), vblk, prT)
        softmax_attention(k, softmaxes, 0, fill=(4, 2, 0),
                          base=lambda p: (vblk[:, 2 * p - H:2 * p - H + 2, :].rearrange("p h d -> p (h d)"), prT[:])
                          if 2 * p >= H else None)


def second_block(k):
    for layer in range(2):
        if layer == 0:
            first = dict(residual=(ALPHA, 1.0), layer_norm=(1, 1), rms=PARAM_AT["ffn1_norm_2"])
        else:
            first = dict(residual=(1.0, 0.5), rms=PARAM_AT["ffn1_norm_2"] + KD)
        feed_forward(k, f"ffn{2 + 2 * layer}", first)
        mix = dict(residual=(1.0, 0.5), rms=PARAM_AT["mix_norm_2"] + KD * layer)
        if layer == 0:
            latent_layer(k, mix)
            out_product(k, "ab_out", 6)
        else:
            sparse_layer(k, mix)
            out_product(k, "cd_out", KD)
        feed_forward(k, f"ffn{3 + 2 * layer}", dict(residual=(1.0, 1.0), rms=PARAM_AT["ffn2_norm_2"] + KD * layer))
    store_result(k)


def program(nc, w, out):
    k = Core(nc, w, out)
    first_block(k)
    second_block(k)



def kernel(**inputs):
    from concourse import bacc
    from concourse.bass_utils import run_bass_kernel_spmd

    nc = bacc.Bacc("TRN2", target_bir_lowering=False, num_devices=1)
    tables = {"const_hgrn_masks": hgrn_masks(), "const_bias_tables": bias_tables(),
              "const_bias_sets": bias_sets(), "const_small": small_tables()}
    arrays, w = {}, {}
    for name, a in {**inputs, **tables}.items():
        a = np.ascontiguousarray(a)
        arrays[f"in_{name}"] = a
        w[name] = nc.dram_tensor(f"in_{name}", a.shape, mybir.dt.from_np(a.dtype), kind="ExternalInput").ap()
    out = nc.dram_tensor("out_0", (1, S, D), F32, kind="ExternalOutput").ap()
    program(nc, w, out)
    result = run_bass_kernel_spmd(nc, [arrays], core_ids=[0])
    return result.results[0]["out_0"]
```
